# Optimizing a Trainium2 kernel written in Bass

```python
import functools
import jax, jax.numpy as jnp
from jax import lax
import numpy as np

D_MODEL = 1024
BATCH = 1
SEQ = 512
DEPTH = 2
DEC_BATCH = 1
DEC_SEQ = 64
PAST_LEN = 128

CHUNK = 64
N_META = 16
HEAD_DIM = 64
N_Q_HEADS = 16
N_KV_HEADS = 2
GROUP = N_Q_HEADS // N_KV_HEADS
ROT_DIM = HEAD_DIM // 4
ROPE_THETA = 500000.0
WINDOW = 128
WIN_CHUNKS = WINDOW // CHUNK
ATTN_SCALE = HEAD_DIM ** -0.5
SC_WIDTH = D_MODEL
SC_K = 3
CF_WIDTH = D_MODEL
CF_K = 31
D_FF = 2816
FFN_K = 3
NORM_EPS = 1e-5
NEG_BIG = -1e30
Q_W = N_Q_HEADS * HEAD_DIM
KV_W = N_KV_HEADS * HEAD_DIM
IN_SIZES = (Q_W, KV_W, KV_W, SC_WIDTH, SC_WIDTH, SC_WIDTH, CF_WIDTH, CF_WIDTH, 3 * D_MODEL)
N_IN = sum(IN_SIZES)
IN_SPLITS = tuple(int(c) for c in np.cumsum(IN_SIZES)[:-1])

kernel_name = 'hybrid_streaming_swa_shortconv_conformer_step'

def rmsnorm(x, g):
    xf = x.astype(jnp.float32)
    y = xf * lax.rsqrt(jnp.mean(xf * xf, axis=-1, keepdims=True) + NORM_EPS)
    return (y * g.astype(jnp.float32)).astype(x.dtype)

def layernorm(x, g, b):
    xf = x.astype(jnp.float32)
    mu = jnp.mean(xf, axis=-1, keepdims=True)
    xc = xf - mu
    y = xc * lax.rsqrt(jnp.mean(xc * xc, axis=-1, keepdims=True) + NORM_EPS)
    return (y * g.astype(jnp.float32) + b.astype(jnp.float32)).astype(x.dtype)

def partial_rotary(x, pos):
    half = ROT_DIM // 2
    inv_freq = jnp.power(ROPE_THETA, -jnp.arange(0, ROT_DIM, 2, dtype=jnp.float32) / ROT_DIM)
    ang = pos.astype(jnp.float32)[:, None] * inv_freq[None, :]
    cos = jnp.cos(ang)[None, :, None, :].astype(x.dtype)
    sin = jnp.sin(ang)[None, :, None, :].astype(x.dtype)
    x1, x2 = x[..., :half], x[..., half:ROT_DIM]
    return jnp.concatenate([x1 * cos - x2 * sin, x2 * cos + x1 * sin, x[..., ROT_DIM:]], axis=-1)

def sink_softmax(s, sink):
    m = jnp.maximum(jnp.max(s, axis=-1, keepdims=True), sink)
    e = jnp.exp(s - m)
    return e / (jnp.sum(e, axis=-1, keepdims=True) + jnp.exp(sink - m))

def causal_dwconv(x, hist, w):
    xh = jnp.concatenate([hist.astype(x.dtype), x], axis=1)
    y = lax.conv_general_dilated(xh, w[:, None, :].astype(x.dtype), window_strides=(1,), padding='VALID',
                                 dimension_numbers=('NWC', 'WIO', 'NWC'), feature_group_count=x.shape[-1])
    return y, xh[:, xh.shape[1] - (w.shape[0] - 1):]

def swa_prompt(q, k, v, sinks):
    n, l = q.shape[:2]
    lead = CHUNK - N_META
    nb = (l + lead) // CHUNK
    front = lead + WIN_CHUNKS * CHUNK
    qb = jnp.pad(q, ((0, 0), (lead, 0), (0, 0), (0, 0))).reshape(n, nb, CHUNK, N_KV_HEADS, GROUP, HEAD_DIM)

    def band(a):
        ab = jnp.pad(a, ((0, 0), (front, 0), (0, 0), (0, 0))).reshape(n, nb + WIN_CHUNKS, CHUNK, N_KV_HEADS, HEAD_DIM)
        return jnp.concatenate([ab[:, i:i + nb] for i in range(WIN_CHUNKS + 1)], axis=2)

    kb, vb = band(k), band(v)
    valid = (jnp.arange((nb + WIN_CHUNKS) * CHUNK) >= front).reshape(nb + WIN_CHUNKS, CHUNK)
    valid = jnp.concatenate([valid[i:i + nb] for i in range(WIN_CHUNKS + 1)], axis=1)
    s = jnp.einsum('nbqhgd,nbkhd->nbhgqk', qb, kb).astype(jnp.float32) * ATTN_SCALE
    s = jnp.where(valid[None, :, None, None, None, :], s, NEG_BIG)
    sink = sinks.astype(jnp.float32).reshape(N_KV_HEADS, GROUP)[None, None, :, :, None, None]
    p = sink_softmax(s, sink)
    o = jnp.einsum('nbhgqk,nbkhd->nbqhgd', p.astype(v.dtype), vb)
    o = o.reshape(n, nb * CHUNK, Q_W)[:, lead:]
    return o, k[:, l - WINDOW:], v[:, l - WINDOW:]

def swa_sample(q, k, v, sinks, ck, cv):
    n, s_len = q.shape[:2]
    kc = jnp.concatenate([ck.astype(k.dtype), k], axis=1)
    vc = jnp.concatenate([cv.astype(v.dtype), v], axis=1)
    qg = q.reshape(n, s_len, N_KV_HEADS, GROUP, HEAD_DIM)
    s = jnp.einsum('nqhgd,nkhd->nhgqk', qg, kc).astype(jnp.float32) * ATTN_SCALE
    sink = sinks.astype(jnp.float32).reshape(N_KV_HEADS, GROUP)[None, :, :, None, None]
    p = sink_softmax(s, sink)
    o = jnp.einsum('nhgqk,nkhd->nqhgd', p.astype(vc.dtype), vc).reshape(n, s_len, Q_W)
    w = ck.shape[1]
    return o, kc[:, kc.shape[1] - w:], vc[:, vc.shape[1] - w:]

def trunk_layer(x, pos, attend, sc_hist, cf_hist, ffn_hist, p):
    n, l = x.shape[:2]
    xn = rmsnorm(x, p['norm1_g'])
    proj = xn @ p['w_in']
    q, k, v, sc_b, sc_c, sc_h, cf_a, cf_gate, gate_pre = jnp.split(proj, IN_SPLITS, axis=-1)
    q = partial_rotary(q.reshape(n, l, N_Q_HEADS, HEAD_DIM), pos)
    k = partial_rotary(k.reshape(n, l, N_KV_HEADS, HEAD_DIM), pos)
    v = v.reshape(n, l, N_KV_HEADS, HEAD_DIM)
    y_attn, new_k, new_v = attend(q, k, v, p['attn_sinks'])
    y_attn = y_attn @ p['w_attn_out']
    sc_conv, new_sc = causal_dwconv(sc_c * sc_h, sc_hist, p['sc_conv_w'])
    y_sc = (sc_b * sc_conv) @ p['w_sc_out']
    glu = cf_a * jax.nn.sigmoid(cf_gate)
    cf_conv, new_cf = causal_dwconv(glu, cf_hist, p['cf_conv_w'])
    y_cf = jax.nn.silu(layernorm(cf_conv, p['cf_ln_g'], p['cf_ln_b'])) @ p['w_cf_out']
    g_attn, g_sc, g_cf = jnp.split(jax.nn.sigmoid(gate_pre + p['b_gate']), 3, axis=-1)
    x = x + (g_attn * y_attn + g_sc * y_sc + g_cf * y_cf) @ p['w_o']
    h = rmsnorm(x, p['norm2_g']) @ p['w_up']
    h, new_ffn = causal_dwconv(h, ffn_hist, p['ffn_conv_w'])
    hg, hu = jnp.split(h, 2, axis=-1)
    x = x + (jax.nn.silu(hg) * hu) @ p['w_down']
    return x, (new_k, new_v, new_sc, new_cf, new_ffn)

def setup_inputs(seed: int = 0) -> dict:
    key = jax.random.key(seed)
    ks = jax.random.split(key, 32)
    f32 = jnp.float32
    nrm = lambda k, shape, s: jax.random.normal(k, shape, f32) * s
    swa_cache = min(WINDOW, PAST_LEN)
    return {
        'x_prompt': nrm(ks[0], (BATCH, SEQ, D_MODEL), 1.0),
        'x_sample': nrm(ks[1], (DEC_BATCH, DEC_SEQ, D_MODEL), 1.0),
        'cache_k': nrm(ks[2], (DEPTH, DEC_BATCH, swa_cache, N_KV_HEADS, HEAD_DIM), 1.0),
        'cache_v': nrm(ks[3], (DEPTH, DEC_BATCH, swa_cache, N_KV_HEADS, HEAD_DIM), 1.0),
        'state_sc': nrm(ks[4], (DEPTH, DEC_BATCH, SC_K - 1, SC_WIDTH), 0.5),
        'state_cf': nrm(ks[5], (DEPTH, DEC_BATCH, CF_K - 1, CF_WIDTH), 0.5),
        'state_ffn': nrm(ks[6], (DEPTH, DEC_BATCH, FFN_K - 1, 2 * D_FF), 1.0),
        'meta_tokens': nrm(ks[7], (N_META, D_MODEL), 1.0),
        'norm1_g': 1.0 + nrm(ks[8], (DEPTH, D_MODEL), 0.02),
        'w_in': nrm(ks[9], (DEPTH, D_MODEL, N_IN), D_MODEL ** -0.5),
        'b_gate': nrm(ks[10], (DEPTH, 3 * D_MODEL), 0.02),
        'attn_sinks': nrm(ks[11], (DEPTH, N_Q_HEADS), 0.5),
        'w_attn_out': nrm(ks[12], (DEPTH, Q_W, D_MODEL), Q_W ** -0.5),
        'sc_conv_w': nrm(ks[13], (DEPTH, SC_K, SC_WIDTH), SC_K ** -0.5),
        'w_sc_out': nrm(ks[14], (DEPTH, SC_WIDTH, D_MODEL), SC_WIDTH ** -0.5),
        'cf_conv_w': nrm(ks[15], (DEPTH, CF_K, CF_WIDTH), CF_K ** -0.5),
        'cf_ln_g': 1.0 + nrm(ks[16], (DEPTH, CF_WIDTH), 0.02),
        'cf_ln_b': nrm(ks[17], (DEPTH, CF_WIDTH), 0.02),
        'w_cf_out': nrm(ks[18], (DEPTH, CF_WIDTH, D_MODEL), CF_WIDTH ** -0.5),
        'w_o': nrm(ks[19], (DEPTH, D_MODEL, D_MODEL), D_MODEL ** -0.5),
        'norm2_g': 1.0 + nrm(ks[20], (DEPTH, D_MODEL), 0.02),
        'w_up': nrm(ks[21], (DEPTH, D_MODEL, 2 * D_FF), D_MODEL ** -0.5),
        'ffn_conv_w': nrm(ks[22], (DEPTH, FFN_K, 2 * D_FF), FFN_K ** -0.5),
        'w_down': nrm(ks[23], (DEPTH, D_FF, D_MODEL), D_FF ** -0.5),
        'final_g': 1.0 + nrm(ks[24], (D_MODEL,), 0.02),
    }

def reference(x_prompt, x_sample, cache_k, cache_v, state_sc, state_cf, state_ffn, meta_tokens, norm1_g, w_in,
              b_gate, attn_sinks, w_attn_out, sc_conv_w, w_sc_out, cf_conv_w, cf_ln_g, cf_ln_b, w_cf_out, w_o,
              norm2_g, w_up, ffn_conv_w, w_down, final_g):
    b = x_prompt.shape[0]
    ds = x_sample.shape[1]
    dt = x_prompt.dtype
    xp = jnp.concatenate([jnp.broadcast_to(meta_tokens.astype(dt)[None], (b, N_META, D_MODEL)), x_prompt], axis=1)
    pos_p = jnp.arange(xp.shape[1], dtype=jnp.int32)
    xs = x_sample
    pos_s = PAST_LEN + jnp.arange(ds, dtype=jnp.int32)
    zero_sc = jnp.zeros((b, SC_K - 1, SC_WIDTH), dt)
    zero_cf = jnp.zeros((b, CF_K - 1, CF_WIDTH), dt)
    zero_ffn = jnp.zeros((b, FFN_K - 1, 2 * D_FF), dt)
    st_p, st_s = [], []
    for i in range(DEPTH):
        p = dict(norm1_g=norm1_g[i], w_in=w_in[i], b_gate=b_gate[i], attn_sinks=attn_sinks[i],
                 w_attn_out=w_attn_out[i], sc_conv_w=sc_conv_w[i], w_sc_out=w_sc_out[i], cf_conv_w=cf_conv_w[i],
                 cf_ln_g=cf_ln_g[i], cf_ln_b=cf_ln_b[i], w_cf_out=w_cf_out[i], w_o=w_o[i], norm2_g=norm2_g[i],
                 w_up=w_up[i], ffn_conv_w=ffn_conv_w[i], w_down=w_down[i])
        xp, sp = trunk_layer(xp, pos_p, swa_prompt, zero_sc, zero_cf, zero_ffn, p)
        attend_s = functools.partial(swa_sample, ck=cache_k[i], cv=cache_v[i])
        xs, ss = trunk_layer(xs, pos_s, attend_s, state_sc[i], state_cf[i], state_ffn[i], p)
        st_p.append(sp)
        st_s.append(ss)
    y_prompt = rmsnorm(xp, final_g)[:, N_META:]
    y_sample = rmsnorm(xs, final_g)
    k_prompt = jnp.stack([s[0] for s in st_p])
    v_prompt = jnp.stack([s[1] for s in st_p])
    sc_prompt = jnp.stack([s[2] for s in st_p])
    cf_prompt = jnp.stack([s[3] for s in st_p])
    ffn_prompt = jnp.stack([s[4] for s in st_p])
    k_sample = jnp.stack([s[0] for s in st_s])
    v_sample = jnp.stack([s[1] for s in st_s])
    sc_sample = jnp.stack([s[2] for s in st_s])
    cf_sample = jnp.stack([s[3] for s in st_s])
    ffn_sample = jnp.stack([s[4] for s in st_s])
    return (y_prompt, y_sample, k_prompt, v_prompt, sc_prompt, cf_prompt, ffn_prompt,
            k_sample, v_sample, sc_sample, cf_sample, ffn_sample)


_drawn_inputs = setup_inputs


def setup_inputs(seed=0):
    import zlib

    import numpy as np

    out = dict(_drawn_inputs(seed))
    spreads = {}
    factors = {'b_gate': 8.0,
     'attn_sinks': 24.42,
     'cf_ln_g': 5.374,
     'cf_ln_b': 6.213,
     'final_g': 23.278,
     'state_sc': 2.985,
     'norm2_g': 2.751}
    for name, (base, spread) in spreads.items():
        noise = np.random.default_rng([zlib.crc32(name.encode()), seed]).standard_normal(out[name].shape)
        drawn = base * np.exp(spread * noise) if base else spread * noise
        out[name] = __import__('jax').numpy.asarray(drawn.astype(out[name].dtype))
    for name, factor in factors.items():
        out[name] = (out[name] * factor).astype(out[name].dtype)
    return out
```

```python
import numpy as np
import concourse.bass as bass
from concourse import mybir
from contextlib import ExitStack

F32 = mybir.dt.float32
F32R = mybir.dt.float32r
ALU = mybir.AluOpType
ACT = mybir.ActivationFunctionType
AX = mybir.AxisListType

DEPTH, D_MODEL, SEQ, N_META, DEC_SEQ, CHUNK, WINDOW, PAST = 2, 1024, 512, 16, 64, 64, 128, 128
HEAD_DIM, N_HEADS, N_KV, ROT, THETA = 64, 16, 2, 16, 500000.0
D_FF, SC_K, CF_K, FFN_K, EPS = 2816, 3, 31, 3, 1e-5
TP = N_META + SEQ
TOK = TP + DEC_SEQ
HALF = TOK // 2
KT = D_MODEL // 128
FT = D_FF // 128
THIRDS = (8, 8, 6)
SCALE = HEAD_DIM ** -0.5
N_CHUNK = 1 + SEQ // CHUNK
CF_H, S_H = CF_K - 1, SC_K - 1
CF_IN, CF_OUT = 2 * CF_H + TOK, CF_H + TOK
S_IN, S_OUT = 2 * S_H + TOK, S_H + TOK
VEC = {}
VEC_N = 0
for _name, _n in (("g1", KT), ("g2", KT), ("bg", 3 * KT), ("lng", KT), ("lnb", KT), ("scw", SC_K * KT),
                  ("cfw", CF_K * KT), ("ffw", FFN_K * 2 * FT), ("sch", S_H * KT), ("ffh", S_H * 2 * FT), ("sink", 8)):
    VEC[_name] = VEC_N
    VEC_N += _n
CON = {}
CON_N = 0
for _name, _n in (("cos", TOK), ("sin", TOK), ("ident", 128), ("ones", 128), ("rot", 128), ("ka", 128), ("kar", 128),
                  ("kb", 128), ("kbr", 128), ("eps", 1)):
    CON[_name] = CON_N
    CON_N += _n

P_CF, P_Q, P_K, P_V, P_OA, P_SC, P_OS, P_OC, P_WO, P_FF = 0, 16, 24, 25, 26, 42, 66, 82, 98, 106
PANELS = 174
A_N1, A_CF, A_Q, A_K, A_V, A_OA, A_SC, A_OS, A_MEAN, A_VAR, A_OC, A_N2, A_FF, NA = \
    0, 1, 9, 17, 18, 19, 27, 35, 37, 40, 45, 53, 54, 76
D_CF, D_Q, D_K, D_V, D_OA, D_SC, D_OS, D_OC, D_WO, D_FF, ND = 0, 8, 16, 20, 22, 30, 46, 54, 62, 70, 116
CHUNKS = N_CHUNK + 1

O_KD, O_VV, O_QS, O_P, O_PT1, O_PT2, O_ON = 0, 1440, 3488, 4512, 6048, 7072, 8096
O_QR, O_TQ, O_SG = 4512, 6048, 7232
O_SQ, O_RT, O_MU, O_NT = 0, 1244, 1866, 2488
O_CT, O_CH, O_CV, O_BT = 0, 1184, 2376, 3564
O_HG, O_HU, O_GC, O_UC, O_PB = 0, 1192, 2384, 3572, 4760
N_SCRATCH = 8608

PIECES = ((0, 0, HALF, 0), (1, 0, TP - HALF, HALF), (1, TP - HALF, DEC_SEQ, TP))


def halves(ap):
    return ap.rearrange("p (h n) -> p h n", h=2)


def after(t0, hist):
    return t0 + hist + (hist if t0 >= TP else 0)


def a_free(l, a):
    return l * NA + a + 1


def a_ready(l, a):
    return l * NA + a + 3


def d_free(l, d):
    return l * ND + d + 1


def d_ready(l, d):
    return l * ND + d + 3


def chunk_span(c):
    if isinstance(c, int):
        if c == CHUNKS - 1:
            return TP, TP, WINDOW + DEC_SEQ
        if c == 0:
            return 0, 0, N_META
        if c < 3:
            return N_META + CHUNK * (c - 1), 0, N_META + CHUNK * c
    return c * CHUNK + (N_META - CHUNK), c * CHUNK + (N_META - 3 * CHUNK), 3 * CHUNK


def it2(l, n, v):
    return l * 16 + n * 2 + (v - 4)


def v_blocks(j):
    if j == 0:
        return [(0, 128)] + [(chunk_span(c)[1], 128) for c in range(3, N_CHUNK)]
    return [(chunk_span(c)[1] + 128, CHUNK) for c in range(3, N_CHUNK)] + [(TP, DEC_SEQ), (128, N_META)]


def has(c):
    return not isinstance(c, int) or 0 <= c < CHUNKS


def v_tile(c):
    if isinstance(c, int):
        return 7 if c == CHUNKS - 1 else max(c - 2, 0)
    return c - 2


def encoder(nc, weights, xt, vecs, consts, final_g, kcache, vcache, cfhist, spill, y, kp, vp, scp, cfp, ffp, ks, vs):
    ctx = ExitStack()

    def sb(name, shape, dt=F32):
        return ctx.enter_context(nc.sbuf_tensor(name, shape, dt))

    def sem(name):
        return ctx.enter_context(nc.semaphore(name))

    xh, xl = sb("xn_hi", [128, KT, TOK], F32R), sb("xn_lo", [128, KT, TOK], F32R)
    bh, bl = sb("branch_hi", [128, KT, TOK], F32R), sb("branch_lo", [128, KT, TOK], F32R)
    X = sb("x_q_merged", [128, KT, TOK])
    raw = sb("raw", [128, 2, KT * 128])
    wh, wl = sb("w_hi", [128, 2, KT * 128], F32R), sb("w_lo", [128, 2, KT * 128], F32R)
    scr = sb("scratch", [128, N_SCRATCH])
    vec = sb("vec", [128, DEPTH * VEC_N])
    con = sb("con", [128, CON_N])
    fg = sb("fg", [128, KT])
    sct = sb("sc_tail", [128, KT, 2 * S_H])
    fft = sb("ffn_tail", [128, 2 * FT, 2 * S_H])
    mx, nm, ds_, es = (sb(n, [128, N_KV, 4]) for n in ("score_max", "neg_max", "sink_diff", "sink_exp"))
    sums, rinv = sb("exp_sums", [128, N_KV, 4]), sb("inv_den", [128, N_KV, 4])
    nsink = sb("neg_sink", [128, DEPTH * 8])
    with nc.sbuf_tensor("glu", [128, KT, CF_IN], F32) as G, nc.sbuf_tensor("cf_acc", [128, KT, CF_OUT], F32) as acc:
        pass
    with nc.sbuf_tensor("merged_hi", [128, KT, TOK], F32R) as mh, nc.sbuf_tensor("merged_lo", [128, KT, TOK], F32R) as ml:
        pass
    PS = ctx.enter_context(nc.psum_tensor("ps", [128, 8, 512], F32))

    def view(off, n):
        return scr[:, off:off + n]

    def slot(off, n, s):
        return scr[:, off + n * s:off + n * (s + 1)]

    KD = view(O_KD, 2 * 720).rearrange("p (v n) -> p v n", v=2)
    VV = view(O_VV, 2048).rearrange("p (c j n) -> p c j n", c=8, j=2)
    ident, ones = con[:, CON["ident"]:CON["ident"] + 128], con[:, CON["ones"]:CON["ones"] + 128]
    cos, sin = con[:, CON["cos"]:CON["cos"] + TOK], con[:, CON["sin"]:CON["sin"] + TOK]
    eps = con[:, CON["eps"]:CON["eps"] + 1]

    def f(ap):
        return ap.bitcast(F32)

    def col(l, name, i, n=1):
        if isinstance(l, int) and isinstance(i, int):
            at = l * VEC_N + VEC[name] + i
            return vec[:, at:at + n]
        return vec[:, bass.ds(l * VEC_N + VEC[name] + i, n)]

    def tile(t, m, a=0, n=None):
        n = t.shape[2] if n is None else n
        if isinstance(m, int) and isinstance(a, int):
            return t[:, m, a:a + n]
        return t[:, :, :].rearrange("p t n -> p (t n)")[:, bass.ds(m * t.shape[2] + a, n)]

    def a_tile(a, n=HALF):
        b = 2 * (a % 2)
        return PS[:, b:b + 2, 0:n]

    def d_tile(d, n=HALF):
        b = 4 + 2 * (d % 2)
        return PS[:, b:b + 2, 0:n]

    def d_piece(d, piece):
        return PS[:, 4 + 2 * (d % 2) + piece[0], piece[1]:piece[1] + piece[2]]

    def a_piece(a, piece):
        return PS[:, 2 * (a % 2) + piece[0], piece[1]:piece[1] + piece[2]]

    raw_in = [sem("raw_in0"), sem("raw_in1")]
    hi_done, lo_done = sem("hi_done"), sem("lo_done")
    panel_done = sem("panel_done")
    a_out, d_out = sem("a_out"), sem("d_out")
    inputs_in = sem("inputs_in")
    x_spilled = sem("x_spilled")
    x_back = sem("x_back")
    cache_in = sem("cache_in")
    hist_in = sem("hist_in")
    kv_out = sem("kv_out")
    tails_out = sem("tails_out")
    small_out = sem("small_out")
    vs_out = sem("vs_out")
    y_out = sem("y_out")
    sq_done, sq_used = sem("sq_done"), sem("sq_used")
    rs_done = sem("rs_done")
    nx_mul, nx_hi, nx_lo = sem("nx_mul"), sem("nx_hi"), sem("nx_lo")
    qrot = sem("qrot")
    qtmp = sem("qtmp")
    krot = sem("krot")
    qrot_ps, krot_ps = sem("qrot_ps"), sem("krot_ps")
    vt_ps = sem("vt_ps")
    mean_ps = sem("mean_ps")
    zero_qs = sem("zero_qs")
    qs_done = sem("qs_done")
    s_done = sem("s_done")
    nm_done = sem("nm_done")
    mx_done = sem("mx_done")
    es_done, p_done = sem("es_done"), sem("p_done")
    t_done = sem("t_done")
    pt1_done, pt2_done = sem("pt1_done"), sem("pt2_done")
    den_done, rinv_done = sem("den_done"), sem("rinv_done")
    o_done, on_done, ot_done = sem("o_done"), sem("on_done"), sem("ot_done")
    oh_done, ol_done = sem("oh_done"), sem("ol_done")
    tap_done = sem("tap_done")
    mg_done = sem("mg_done")
    mg_hi, mg_lo = sem("mg_hi"), sem("mg_lo")
    sc_hist = sem("sc_hist")
    sc_tap = sem("sc_tap")
    sc_hi, sc_lo = sem("sc_hi"), sem("sc_lo")
    sc_tail_done = sem("sc_tail_done")
    ln_sub, ln_mul, ln_silu = sem("ln_sub"), sem("ln_mul"), sem("ln_silu")
    cf_hi, cf_lo = sem("cf_hi"), sem("cf_lo")
    g_zero = sem("g_zero")
    ff_hist = sem("ff_hist")
    ff_tap = sem("ff_tap")
    ff_gate, ff_silu, ff_prod = sem("ff_gate"), sem("ff_silu"), sem("ff_prod")
    ff_hi, ff_lo = sem("ff_hi"), sem("ff_lo")
    ff_tail_done = sem("ff_tail_done")
    yn_done = sem("yn_done")
    nsink_done = sem("nsink_done")
    carrier = sem("carrier")

    thirds, at = [], (0, P_FF, A_FF, D_FF)
    for n in THIRDS:
        thirds.append((at[0], n, at[1], at[2], at[3]))
        at = (at[0] + n, at[1] + 2 * n + KT, at[2] + n, at[3] + n + KT)

    block = ctx.enter_context(nc.Block())

    @block.sync
    def _(sp):
        sp.dma_start(X[:, :, :], xt).then_inc(inputs_in, 16)
        sp.dma_start(vec[:, :], vecs).then_inc(inputs_in, 16)
        sp.dma_start(con[:, :], consts).then_inc(inputs_in, 16)
        sp.dma_start(fg[:, :], final_g).then_inc(inputs_in, 16)
        for s in range(2):
            sp.dma_start(raw[:, s, :], weights[s, :, :]).then_inc(raw_in[s], 16)
        with sp.Fori(0, DEPTH * PANELS // 2) as i:
            for s in range(2):
                sp.wait_ge(lo_done, 2 * i + s + 1)
                sp.dma_start(raw[:, s, :], weights.rearrange("w p n -> p w n")[:, bass.ds(2 * i + (s + 2), 1), :]) \
                    .then_inc(raw_in[s], 16)

    @block.gpsimd
    def _(pool):
        def plain():
            nc.gpsimd.sem_inc(carrier, 1)

        pool.wait_ge(inputs_in, 64)
        pool.dma_start(vs[:, 0:WINDOW - DEC_SEQ, :], vcache[:, DEC_SEQ:WINDOW, :]).then_inc(vs_out, 16)
        with pool.Fori(0, DEPTH) as l:
            pool.wait_ge(inputs_in, 64)
            pool.wait_ge(d_out, l * ND + 2)
            plain()
            pool.dma_start(spill, X[:, :, :]).then_inc(x_spilled, 16)
            pool.dma_start(G[:, :, TP + CF_H:TP + 2 * CF_H], cfhist[bass.ds(l, 1), :, :, :]
                           .rearrange("l p t n -> (l p) t n")).then_inc(hist_in, 16)
            pool.wait_ge(nx_lo, l * 16 + 8)
            plain()
            pool.dma_start(KD[:, :, TP:TP + WINDOW], kcache[bass.ds(l, 1), :, :, :]
                           .rearrange("l p v n -> (l p) v n")).then_inc(cache_in, 16)
            pool.dma_start(VV[:, 7, 0, :], vcache[bass.ds(l, 1), :, :].rearrange("l p n -> (l p) n")).then_inc(cache_in, 16)
            nc.gpsimd.memset(view(O_QS, 1024), 0.0).then_inc(zero_qs, 1)
            pool.wait_ge(krot, l * 2 + 2)
            pool.wait_ge(cache_in, l * 32 + 32)
            plain()
            for v in range(N_KV):
                r = slice(64 * v, 64 * v + 64)
                pool.dma_start(kp[bass.ds(l, 1), r, :].rearrange("l p n -> (l p) n"),
                               KD[r, v, TP - WINDOW:TP]).then_inc(kv_out, 16)
                pool.dma_start(ks[bass.ds(l, 1), r, :].rearrange("l p n -> (l p) n"),
                               KD[r, v, TP + DEC_SEQ:TP + DEC_SEQ + WINDOW]).then_inc(kv_out, 16)
            pool.wait_ge(d_out, d_ready(l, D_V + 1))
            plain()
            pool.dma_start(vp[bass.ds(l, 1), 0:64, :].rearrange("l p n -> (l p) n"), VV[64:128, 6, 0, :]).then_inc(kv_out, 16)
            pool.dma_start(vp[bass.ds(l, 1), 64:128, :].rearrange("l p n -> (l p) n"), VV[0:64, 6, 1, :]).then_inc(kv_out, 16)
            pool.dma_start(vs[bass.ds(l, 1), WINDOW - DEC_SEQ:WINDOW, :].rearrange("l p n -> (l p) n"),
                           VV[0:64, 7, 1, :]).then_inc(kv_out, 16)
            pool.wait_ge(d_out, d_ready(l, D_CF + 7))
            plain()
            pool.dma_start(cfp[bass.ds(l, 1), :, :, 0, :].rearrange("l p t n -> (l p) t n"),
                           G[:, :, TP:TP + CF_H]).then_inc(tails_out, 16)
            pool.dma_start(cfp[bass.ds(l, 1), :, :, 1, :].rearrange("l p t n -> (l p) t n"),
                           G[:, :, CF_IN - CF_H:CF_IN]).then_inc(tails_out, 16)
            pool.wait_ge(zero_qs, l + 1)
            plain()

            def stage(c, n):
                q0 = chunk_span(c)[0]
                for v in range(N_KV):
                    pool.wait_ge(s_done, l * 20 + n * 2 + v + 1)
                    plain()
                    dst = view(O_QS + 512 * v, 512).rearrange("p (i n) -> p i n", i=4)
                    if isinstance(q0, int):
                        src = X[:, 4 * v:4 * v + 4, q0:q0 + 64]
                    else:
                        src = X[:, 4 * v:4 * v + 4, bass.ds(q0, 64)]
                    nc.gpsimd.tensor_copy(dst[0:64, :, 0:64], src[0:64, :, :])
                    nc.gpsimd.tensor_copy(dst[64:128, :, 64:128], src[64:128, :, :]).then_inc(qs_done, 1)

            pool.wait_ge(qrot, l * KT + KT)
            plain()
            for c in range(3):
                stage(c, c)
            with pool.Fori(3, N_CHUNK) as c:
                stage(c, c)
            stage(CHUNKS - 1, CHUNKS - 1)
            pool.wait_ge(sc_tail_done, l * KT + KT)
            plain()
            pool.dma_start(scp[bass.ds(l, 1), :, :].rearrange("l p n -> (l p) n"),
                           sct[:, :, :].rearrange("p t n -> p (t n)")).then_inc(small_out, 16)
            with pool.Fori(0, KT) as m:
                pool.wait_ge(mg_lo, l * KT + m + 1)
                pool.wait_ge(x_spilled, l * 16 + 16)
                plain()
                pool.dma_start(tile(X, m), spill[:, bass.ds(m, 1), :].rearrange("p t n -> p (t n)")).then_inc(x_back, 16)
                pool.wait_ge(x_back, l * (KT * 16) + m * 16 + 16)
            pool.wait_ge(ff_tail_done, l * (2 * FT) + (2 * FT + 2))
            plain()
            pool.dma_start(ffp[bass.ds(l, 1), :, :].rearrange("l p n -> (l p) n"),
                           fft[:, :, :].rearrange("p t n -> p (t n)")).then_inc(small_out, 16)
            pool.wait_ge(small_out, l * 32 + 32)
            plain()
        for m in range(KT):
            pool.wait_ge(yn_done, m + 1)
            pool.dma_start(y[:, m, :], X[:, m, :]).then_inc(y_out, 16)
        pool.wait_ge(y_out, 16 * KT)
        pool.wait_ge(vs_out, 16)
        pool.wait_ge(kv_out, DEPTH * 7 * 16)
        pool.wait_ge(tails_out, DEPTH * 32)

    @block.tensor
    def _(pe):
        def panel(w, s, out, nk, rh, rl, kwait=None):
            pe.wait_ge(lo_done, w + 1)
            for k in range(nk):
                if kwait:
                    pe.wait_ge(kwait[0], kwait[1] + k + 1)
                wk = slice(k * 128, k * 128 + 128)
                for j, (a, b) in enumerate(((wh, rh), (wh, rl), (wl, rh))):
                    for h in range(2):
                        last = nc.tensor.matmul(out[:, h, :], a[:, s, wk], b[:, k, h * HALF:(h + 1) * HALF],
                                                start=(k == 0 and j == 0), stop=(k == nk - 1 and j == 2))
            last.then_inc(panel_done, 1)

        def sum_squares(l, a, base, n, m, s):
            first, final = isinstance(m, int) and m == 0, isinstance(m, int) and m == KT - 1
            if first:
                pe.wait_ge(a_out, a_free(l, a))
            pe.wait_ge(sq_done, base + m + 1)
            for h in range(2):
                last = nc.tensor.matmul(a_tile(a, n)[:, h, :], ones, slot(O_SQ, 622, s)[:, h * n:(h + 1) * n],
                                        start=first, stop=final)
            last.then_inc(sq_used, 1)

        def residual(l, w, d, nk, rh, rl, kwait, norm):
            def body(i):
                for j in range(2):
                    pe.wait_ge(d_out, l * ND + i * 2 + (d + j + 1))
                    panel(l * PANELS + i * 2 + (w + j), j, d_tile(d + j), nk, rh, rl, kwait=kwait if j == 0 else None)
                    if norm is not None and (j or not isinstance(i, int)):
                        sum_squares(*norm, HALF, i * 2 + (j - 1), 1 - j)
            body(0)
            with pe.Fori(1, 4) as i:
                body(i)
            if norm is not None:
                sum_squares(*norm, HALF, KT - 1, 1)

        def pair(l, w, a, d, rg, ro, kwait=None):
            pe.wait_ge(a_out, a_free(l, a[0]))
            panel(w, 0, a_tile(a[1]), KT, *rg, kwait=kwait)
            pe.wait_ge(d_out, d_free(l, d[0]))
            panel(w + 1, 1, d_tile(d[1]), KT, *ro)

        def scores(l, c, n, v):
            k0, nk = chunk_span(c)[1:]
            it = l * 20 + n * 2 + v
            pe.wait_ge(qs_done, it + 1)
            pe.wait_ge(p_done, it + 1)
            for i in range(4):
                keys = KD[:, v, k0:k0 + nk] if isinstance(k0, int) else \
                    view(O_KD, 1440)[:, bass.ds(k0 + 720 * v, nk)]
                last = nc.tensor.matmul(PS[:, 2 * v + i // 2, 256 * (i % 2):256 * (i % 2) + nk],
                                        view(O_QS + 512 * v + 128 * i, 128), keys, start=True, stop=True)
            last.then_inc(s_done, 1)

        def turn(l, c, n, v):
            nk = chunk_span(c)[2]
            n1, n2 = min(nk, 128), max(nk - 128, 0)
            it = l * 20 + n * 2 + v
            pe.wait_ge(p_done, it + 3)
            pe.wait_ge(pt1_done, it + 1)
            if n2:
                pe.wait_ge(pt2_done, it2(l, n, v) + 1)
            for i in range(4):
                P = view(O_P + 768 * v + 192 * i, 192)
                last = nc.tensor.transpose(PS[0:n1, 4, 128 * i:128 * i + 128], P[:, 0:n1], ident)
                if n2:
                    last = nc.tensor.transpose(PS[0:n2, 5, 128 * i:128 * i + 128], P[:, 128:nk], ident)
            last.then_inc(t_done, 1)

        def values(l, c, n, v):
            nk = chunk_span(c)[2]
            n1, n2 = min(nk, 128), max(nk - 128, 0)
            vt = v_tile(c)
            it = l * 20 + n * 2 + v
            pe.wait_ge(pt1_done, it + 2)
            if n2:
                pe.wait_ge(pt2_done, it2(l, n, v) + 2)
            pe.wait_ge(on_done, it + 1)
            for i in range(4):
                for j, (nn, o) in enumerate(((n1, O_PT1), (n2, O_PT2))):
                    if nn:
                        if isinstance(vt, int):
                            vals = VV[0:nn, vt, j, 64 * v:64 * v + 64]
                        else:
                            vals = scr[0:nn, bass.ds(vt * 256 + (O_VV + 128 * j + 64 * v), 64)]
                        last = nc.tensor.matmul(PS[:, 6, 64 * i:64 * i + 64],
                                                scr[0:nn, o + 512 * v + 128 * i:o + 512 * v + 128 * i + 128], vals,
                                                start=(i == 0 and j == 0), stop=(j == (1 if n2 else 0)),
                                                skip_group_check=True)
            last.then_inc(o_done, 1)

        def turn_back(l, n, v):
            it = l * 20 + n * 2 + v
            pe.wait_ge(on_done, it + 2)
            pe.wait_ge(ol_done, it + 1)
            for j in range(2):
                last = nc.tensor.transpose(PS[:, 7, 128 * j:128 * j + 128], view(O_ON + 256 * v + 128 * j, 128), ident)
            last.then_inc(ot_done, 1)

        def attention(l, n):
            if has(n):
                scores(l, n, n, 0)
            if has(n - 2):
                values(l, n - 2, n - 2, 1)
            if has(n - 1):
                turn(l, n - 1, n - 1, 0)
            if has(n - 2):
                turn_back(l, n - 2, 0)
            if has(n):
                scores(l, n, n, 1)
            if has(n - 1):
                values(l, n - 1, n - 1, 0)
                turn(l, n - 1, n - 1, 1)
            if has(n - 2):
                turn_back(l, n - 2, 1)

        nc.tensor.sem_inc(sq_used, 2)
        nc.tensor.sem_inc(s_done, 2)
        nc.tensor.sem_inc(t_done, 2)
        nc.tensor.sem_inc(o_done, 2)
        pe.wait_ge(inputs_in, 64)
        for m in range(KT):
            sum_squares(0, A_N1, 0, HALF, m, m % 2)
        with pe.Fori(0, DEPTH) as l:
            W = l * PANELS
            with pe.Fori(0, 4) as i:
                for j in range(2):
                    pair(l, W + i * 4 + (P_CF + 2 * j), (i * 2 + (A_CF + j), A_CF + j), (i * 2 + (D_CF + j), D_CF + j),
                         (xh, xl), (xh, xl), kwait=(nx_lo, l * 16) if j == 0 else None)
            with pe.Fori(0, 4) as i:
                for j in range(2):
                    pe.wait_ge(a_out, l * NA + i * 2 + (A_Q + j + 1))
                    panel(W + i * 2 + (P_Q + j), j, a_tile(A_Q + j), KT, xh, xl)
                for j in range(2):
                    pe.wait_ge(a_out, l * NA + i * 2 + (A_Q + j + 3))
                    pe.wait_ge(d_out, l * ND + i * 2 + (D_Q + j + 1))
                    for h in range(2):
                        last = nc.tensor.matmul(d_tile(D_Q + j)[:, h, :], con[:, CON["rot"]:CON["rot"] + 128],
                                                slot(O_QR, TOK, j)[:, h * HALF:(h + 1) * HALF], start=True, stop=True)
                    last.then_inc(qrot_ps, 1)
            pe.wait_ge(a_out, a_free(l, A_K))
            panel(W + P_K, 0, a_tile(A_K), KT, xh, xl)
            pe.wait_ge(a_out, a_free(l, A_V))
            panel(W + P_V, 1, a_tile(A_V), KT, xh, xl)
            pe.wait_ge(a_out, a_ready(l, A_K))
            for j, name in enumerate(("ka", "kar", "kb", "kbr")):
                pe.wait_ge(d_out, d_free(l, D_K + j))
                for h in range(2):
                    last = nc.tensor.matmul(d_tile(D_K + j)[:, h, :], con[:, CON[name]:CON[name] + 128],
                                            slot(O_QR, TOK, 0)[:, h * HALF:(h + 1) * HALF], start=True, stop=True)
                last.then_inc(krot_ps, 1)
            pe.wait_ge(a_out, a_ready(l, A_V))
            for j in range(2):
                pe.wait_ge(d_out, d_free(l, D_V + j))
                nc.tensor.sem_inc(carrier, 1)
                for b, (t0, n) in enumerate(v_blocks(j)):
                    last = nc.tensor.transpose(PS[0:n, 4 + 2 * ((D_V + j) % 2) + b // 4, 128 * (b % 4):128 * (b % 4) + 128],
                                               slot(O_QR, TOK, 1)[:, t0:t0 + n], ident)
                last.then_inc(vt_ps, 1)
            pe.wait_ge(a_out, a_ready(l, A_V))
            pe.wait_ge(d_out, d_ready(l, D_V + 1))
            pe.wait_ge(cache_in, l * 32 + 32)
            pe.wait_ge(krot, l * 2 + 2)
            for n in range(5):
                attention(l, n)
            with pe.Fori(5, N_CHUNK) as n:
                attention(l, n)
            for n in range(N_CHUNK, CHUNKS + 2):
                attention(l, n)
            pe.wait_ge(ol_done, l * 20 + 21)
            nc.tensor.sem_inc(carrier, 1)
            with pe.Fori(0, 4) as i:
                for j in range(2):
                    pair(l, W + i * 4 + (P_OA + 2 * j), (i * 2 + (A_OA + j), A_OA + j), (i * 2 + (D_OA + j), D_OA + j),
                         (xh, xl), (bh, bl))
            with pe.Fori(0, 4) as i:
                for j in range(2):
                    w = W + i * 6 + (P_SC + 3 * j)
                    pe.wait_ge(a_out, l * NA + i * 2 + (A_SC + j + 1))
                    panel(w, j % 2, a_tile(A_SC + j), KT, xh, xl)
                    for e in range(2):
                        pe.wait_ge(d_out, l * ND + i * 4 + (D_SC + 2 * j + e + 1))
                        panel(w + (1 + e), (j + 1 + e) % 2, d_tile(D_SC + 2 * j + e), KT, xh, xl)

            def out_sc(i0, n, a0):
                def body(i):
                    for j in range(2):
                        pair(l, W + i * 4 + (P_OS + 4 * i0 + 2 * j), (i * 2 + (a0 + j), a0 + j),
                             (i * 2 + (D_OS + 2 * i0 + j), D_OS + j), (xh, xl), (bh, bl),
                             kwait=None)
                if n == 1:
                    body(0)
                else:
                    with pe.Fori(0, n) as i:
                        body(i)
            pe.wait_ge(sc_lo, l * KT + KT)
            out_sc(0, 1, A_OS)
            pe.wait_ge(a_out, a_free(l, A_MEAN))
            pe.wait_ge(tap_done, l * 248 + 248)
            for m in range(KT):
                for h in range(2):
                    last = nc.tensor.matmul(a_tile(A_MEAN, 311)[:, h, :], ones, acc[:, m, h * 311:(h + 1) * 311],
                                            start=(m == 0), stop=(m == KT - 1))
            last.then_inc(mean_ps, 1)
            out_sc(1, 1, A_MEAN + 1)
            for m in range(KT):
                sum_squares(l, A_VAR, l * 24 + 8, 311, m, m % 2)
            out_sc(2, 2, A_VAR + 1)
            with pe.Fori(0, 4) as i:
                for j in range(2):
                    pe.wait_ge(a_out, l * NA + i * 2 + (A_OC + j + 1))
                    panel(W + i * 4 + (P_OC + 2 * j), 0, a_tile(A_OC + j), KT, xh, xl)
                    pe.wait_ge(d_out, l * ND + i * 2 + (D_OC + j + 1))
                    panel(W + i * 4 + (P_OC + 2 * j + 1), 1, d_tile(D_OC + j), KT, bh, bl,
                          kwait=(cf_lo, l * KT) if j == 0 else None)
            residual(l, P_WO, D_WO, KT, mh, ml, (mg_lo, l * KT), (l, A_N2, l * 24 + 16))
            for t0, n, p0, a0, d0 in thirds:
                with pe.Fori(0, n // 2) as i:
                    for j in range(2):
                        pair(l, W + i * 4 + (p0 + 2 * j), (i * 2 + (a0 + j), a0 + j), (i * 2 + (d0 + j), d0 + j),
                             (xh, xl), (xh, xl), kwait=(nx_lo, l * 16 + 8) if j == 0 else None)
                residual(l, p0 + 2 * n, d0 + n, n, bh, bl, (ff_lo, l * FT + t0),
                         (l + 1, A_N1, (l + 1) * 24) if t0 + n == FT else None)

    @block.scalar
    def _(act):
        def step(wbase, off, s):
            act.wait_ge(panel_done, wbase + (off + 1))
            act.wait_ge(raw_in[s], wbase * 8 + ((off - s) // 2 + 2) * 16)
            nc.scalar.activation(wh[:, s, :], raw[:, s, :], ACT.Copy).then_inc(hi_done, 1)

        def square(base, m, s, src, n):
            act.wait_ge(sq_used, base + m + 1)
            nc.scalar.activation(slot(O_SQ, 622, s)[:, 0:n], src, ACT.Square).then_inc(sq_done, 1)

        def residual(l, w, d, norm):
            def body(i):
                for j in range(2):
                    step(l * PANELS + i * 2, w + j, j)
                    if norm is not None:
                        act.wait_ge(d_out, l * ND + i * 2 + (d + j + 3))
                        square(norm, i * 2 + j, j, tile(X, i * 2 + j), TOK)
            with act.Fori(0, 4) as i:
                body(i)

        def root(l, a, base, n):
            act.wait_ge(sq_used, base + KT + 2)
            nc.scalar.activation(halves(view(O_RT, 2 * n)), a_tile(a, n), ACT.Sqrt, bias=eps, scale=1.0 / D_MODEL) \
                .then_inc(a_out, 1)

        def norm(l, a, sqb, nxb, g):
            root(l, a, sqb, HALF)
            for m in range(KT):
                act.wait_ge(nx_mul, nxb + m + 1)
                nc.scalar.activation(xh[:, m, :], slot(O_NT, TOK, m % 3), ACT.Identity, bias=0.0, scale=col(l, g, m)) \
                    .then_inc(nx_hi, 1)

        def gate(a, j, b, used):
            act.wait_ge(d_out, used)
            nc.scalar.activation(halves(slot(O_SG, TOK, j)), a_tile(a), ACT.Sigmoid, bias=b).then_inc(a_out, 1)

        nc.scalar.sem_inc(a_out, 2)
        nc.scalar.sem_inc(p_done, 2)
        nc.scalar.sem_inc(pt1_done, 1)
        act.wait_ge(raw_in[0], 16)
        nc.scalar.activation(wh[:, 0, :], raw[:, 0, :], ACT.Copy).then_inc(hi_done, 1)
        act.wait_ge(raw_in[1], 16)
        nc.scalar.activation(wh[:, 1, :], raw[:, 1, :], ACT.Copy).then_inc(hi_done, 1)
        act.wait_ge(inputs_in, 64)
        for m in range(KT):
            square(0, m, m % 2, X[:, m, :], TOK)
        with act.Fori(0, DEPTH) as l:
            W = l * PANELS
            norm(l, A_N1, l * 24, l * 16, "g1")
            with act.Fori(0, 4) as i:
                for j in range(2):
                    step(W + i * 4, P_CF + 2 * j, 0)
                    gate(A_CF + j, j, 0.0, l * ND + i * 2 + (D_CF + j + 1))
                    step(W + i * 4, P_CF + 2 * j + 1, 1)
            with act.Fori(0, 4) as i:
                for j in range(2):
                    step(W + i * 2, P_Q + j, j)
                    act.wait_ge(d_out, l * ND + i * 2 + (D_Q + j + 1))
                    nc.scalar.activation(halves(slot(O_QR, TOK, j)), a_tile(A_Q + j), ACT.Copy).then_inc(a_out, 1)
            step(W, P_K, 0)
            act.wait_ge(qrot, l * KT + KT)
            nc.scalar.activation(halves(slot(O_QR, TOK, 0)), a_tile(A_K), ACT.Copy).then_inc(a_out, 1)
            step(W, P_V, 1)
            nc.scalar.activation(halves(slot(O_QR, TOK, 1)), a_tile(A_V), ACT.Copy).then_inc(a_out, 1)

            def exps(n, v):
                nk = chunk_span(n)[2]
                it = l * 20 + n * 2 + v
                act.wait_ge(nm_done, 2 * it + 2)
                act.wait_ge(rinv_done, it + 1)
                nc.scalar.activation(es[:, v, :], ds_[:, v, :], ACT.Exp).then_inc(es_done, 1)
                act.wait_ge(t_done, it + 1)
                for i in range(4):
                    last = nc.scalar.activation(view(O_P + 768 * v + 192 * i, nk),
                                                PS[:, 2 * v + i // 2, 256 * (i % 2):256 * (i % 2) + nk], ACT.Exp,
                                                bias=nm[:, v, i:i + 1], scale=SCALE, accum_out=sums[:, v, i:i + 1])
                last.then_inc(p_done, 1)

            def copy_first(n, v):
                n1 = min(chunk_span(n)[2], 128)
                it = l * 20 + n * 2 + v
                act.wait_ge(t_done, it + 3)
                act.wait_ge(o_done, it + 1)
                nc.scalar.activation(scr[0:n1, O_PT1 + 512 * v:O_PT1 + 512 * v + 512], PS[0:n1, 4, :], ACT.Copy) \
                    .then_inc(pt1_done, 1)

            def outputs_hi(n, v):
                q0 = chunk_span(n)[0]
                act.wait_ge(ot_done, l * 20 + n * 2 + v + 1)
                src = PS[:, 7, 0:256].rearrange("p (t n) -> p t n", n=64)
                dst = bh[:, 4 * v:4 * v + 4, q0:q0 + 64] if isinstance(q0, int) else bh[:, 4 * v:4 * v + 4, bass.ds(q0, 64)]
                nc.scalar.activation(dst, src, ACT.Copy).then_inc(oh_done, 1)

            def attention(n):
                for v in range(N_KV):
                    if has(n - 1):
                        copy_first(n - 1, v)
                    if has(n - 2) and v == 0:
                        outputs_hi(n - 2, v)
                    if has(n):
                        exps(n, v)
                    if has(n - 2) and v == 1:
                        outputs_hi(n - 2, v)

            for n in range(5):
                attention(n)
            with act.Fori(5, N_CHUNK) as n:
                attention(n)
            for n in range(N_CHUNK, CHUNKS + 2):
                attention(n)
            with act.Fori(0, 4) as i:
                for j in range(2):
                    step(W + i * 4, P_OA + 2 * j, 0)
                    gate(A_OA + j, j, col(l, "bg", i * 2 + j), l * ND + i * 2 + (D_OA + j + 1))
                    step(W + i * 4, P_OA + 2 * j + 1, 1)
            act.wait_ge(kv_out, l * 112 + 112)
            with act.Fori(0, 4) as i:
                for j in range(2):
                    step(W + i * 6, P_SC + 3 * j, j)
                    act.wait_ge(d_out, l * ND + i * 4 + (D_SC + 2 * j))
                    nc.scalar.activation(halves(slot(O_CT, TOK, j)), a_tile(A_SC + j), ACT.Copy).then_inc(a_out, 1)
                    step(W + i * 6, P_SC + 3 * j + 1, 1 - j)
                    step(W + i * 6, P_SC + 3 * j + 2, j)
                    act.wait_ge(d_out, l * ND + i * 4 + (D_SC + 2 * j + 1 + 3))
                    nc.scalar.activation(tile(bh, i * 2 + j), slot(O_BT, TOK, j), ACT.Copy).then_inc(sc_hi, 1)

            def out_sc(i0, n, a0):
                def body(i):
                    for j in range(2):
                        step(W + i * 4, P_OS + 4 * i0 + 2 * j, 0)
                        gate(a0 + j, j, col(l, "bg", i * 2 + (KT + 2 * i0 + j)), l * ND + i * 2 + (D_OS + 2 * i0 + j + 1))
                        step(W + i * 4, P_OS + 4 * i0 + 2 * j + 1, 1)
                if n == 1:
                    body(0)
                else:
                    with act.Fori(0, n) as i:
                        body(i)
            out_sc(0, 1, A_OS)
            act.wait_ge(mean_ps, l + 1)
            nc.scalar.activation(halves(view(O_MU, 622)), a_tile(A_MEAN, 311), ACT.Copy, scale=1.0 / D_MODEL) \
                .then_inc(a_out, 1)
            out_sc(1, 1, A_MEAN + 1)
            for m in range(KT):
                act.wait_ge(ln_sub, l * KT + m + 1)
                square(l * 24 + 8, m, m % 2, acc[:, m, :], CF_OUT)
            root(l, A_VAR, l * 24 + 8, 311)
            out_sc(2, 2, A_VAR + 1)
            for m in range(KT):
                act.wait_ge(ln_mul, l * KT + m + 1)
                nc.scalar.activation(acc[:, m, :], acc[:, m, :], ACT.Silu, bias=col(l, "lnb", m), scale=col(l, "lng", m)) \
                    .then_inc(ln_silu, 1)
            for m in range(KT):
                act.wait_ge(ln_silu, l * KT + m + 1)
                nc.scalar.activation(bh[:, m, 0:TP], acc[:, m, 0:TP], ACT.Copy)
                nc.scalar.activation(bh[:, m, TP:TOK], acc[:, m, TP + CF_H:CF_OUT], ACT.Copy).then_inc(cf_hi, 1)
            with act.Fori(0, 4) as i:
                for j in range(2):
                    step(W + i * 4, P_OC + 2 * j, 0)
                    gate(A_OC + j, j, col(l, "bg", i * 2 + (2 * KT + j)), l * ND + i * 2 + (D_OC + j + 1))
                    step(W + i * 4, P_OC + 2 * j + 1, 1)
                    act.wait_ge(mg_done, l * 16 + i * 2 + (8 + j + 1))
                    act.wait_ge(tails_out, l * 32 + 32)
                    nc.scalar.activation(tile(mh, i * 2 + j), tile(X, i * 2 + j), ACT.Copy).then_inc(mg_hi, 1)
            residual(l, P_WO, D_WO, l * 24 + 16)
            norm(l, A_N2, l * 24 + 16, l * 16 + 8, "g2")
            for t0, n, p0, a0, d0 in thirds:
                with act.Fori(0, n // 2) as i:
                    for j in range(2):
                        m = i * 2 + (t0 + j)
                        step(W + i * 4, p0 + 2 * j, 0)
                        act.wait_ge(ff_tap, l * (FT * 6) + i * 12 + (t0 * 6 + 6 * j + 6))
                        act.wait_ge(ff_tail_done, l * (2 * FT) + i * 4 + (2 * t0 + 2 * j))
                        for piece in PIECES:
                            o = after(piece[3], S_H)
                            last = nc.scalar.activation(slot(O_HG, S_IN, j)[:, o:o + piece[2]], a_piece(a0 + j, piece), ACT.Copy)
                        last.then_inc(a_out, 1)
                        step(W + i * 4, p0 + 2 * j + 1, 1)
                        act.wait_ge(ff_tap, l * (FT * 6) + i * 12 + (t0 * 6 + 6 * j + 3 + 12))
                        nc.scalar.activation(slot(O_GC, S_OUT, j), slot(O_GC, S_OUT, j), ACT.Silu).then_inc(ff_silu, 1)
                        act.wait_ge(ff_prod, l * FT + i * 2 + (t0 + j + 1))
                        src = slot(O_PB, S_OUT, j)
                        nc.scalar.activation(tile(bh, i * 2 + j, 0, TP), src[:, 0:TP], ACT.Copy)
                        nc.scalar.activation(tile(bh, i * 2 + j, TP, DEC_SEQ), src[:, TP + S_H:S_OUT], ACT.Copy) \
                            .then_inc(ff_hi, 1)
                residual(l, p0 + 2 * n, d0 + n, (l + 1) * 24 if t0 + n == FT else None)
        root(DEPTH, A_N1, DEPTH * 24, HALF)

    @block.vector
    def _(dve):
        V = nc.vector

        def low(s):
            return V.tensor_tensor(wl[:, s, :], raw[:, s, :], f(wh[:, s, :]), ALU.subtract).then_inc(lo_done, 1)

        def step(wbase, off, s):
            dve.wait_ge(panel_done, wbase + (off + 1))
            dve.wait_ge(hi_done, wbase + (off + 3))
            low(s)

        def rsqrt(a_at, n, count):
            dve.wait_ge(a_out, a_at)
            V.reciprocal(view(O_RT, 2 * n), view(O_RT, 2 * n)).then_inc(rs_done, 1)
            dve.wait_ge(rs_done, count)

        def norm(l, a, nxb, g, count):
            rsqrt(a_ready(l, a), HALF, count)

            def lo(m):
                dve.wait_ge(nx_hi, nxb + m + 1)
                V.scalar_tensor_tensor(xl[:, m, :], slot(O_NT, TOK, m % 3), col(l, g, m), f(xh[:, m, :]), ALU.mult,
                                       ALU.subtract).then_inc(nx_lo, 1)
            for m in range(KT):
                if m >= 3:
                    dve.wait_ge(nx_lo, nxb + m - 2)
                V.tensor_tensor(slot(O_NT, TOK, m % 3), X[:, m, :], view(O_RT, TOK), ALU.mult).then_inc(nx_mul, 1)
                if m:
                    lo(m - 1)
            lo(KT - 1)

        def taps(l, k, t0, t1):
            for t in range(t0, t1):
                src = tile(G, t, k, CF_OUT)
                if isinstance(k, int) and k == 0:
                    V.tensor_scalar(acc[:, t, :], src, col(l, "cfw", t * CF_K), None, ALU.mult).then_inc(tap_done, 1)
                else:
                    dve.wait_ge(tap_done, l * 248 + k * 8 + (t - 7))
                    V.scalar_tensor_tensor(acc[:, t, :], src, col(l, "cfw", k + t * CF_K), acc[:, t, :], ALU.mult, ALU.add) \
                        .then_inc(tap_done, 1)

        def conv3(l, src, dst, name, t, sem_, base):
            V.tensor_scalar(dst, src[:, 0:S_OUT], col(l, name, t * 3), None, ALU.mult).then_inc(sem_, 1)
            for k in (1, 2):
                dve.wait_ge(sem_, base + k)
                V.scalar_tensor_tensor(dst, src[:, k:k + S_OUT], col(l, name, t * 3 + k), dst, ALU.mult, ALU.add) \
                    .then_inc(sem_, 1)

        def keep_tail(t, m, src, sem_):
            V.tensor_copy(tile(t, m, 0, S_H), src[:, TP:TP + S_H])
            V.tensor_copy(tile(t, m, S_H, S_H), src[:, S_IN - S_H:S_IN]).then_inc(sem_, 1)

        V.sem_inc(d_out, 2)
        V.sem_inc(pt2_done, 1)
        V.sem_inc(on_done, 1)
        V.sem_inc(ol_done, 1)
        V.sem_inc(rinv_done, 2)
        V.sem_inc(ff_tap, 12)
        V.sem_inc(ff_tail_done, 2)
        for s in range(2):
            dve.wait_ge(hi_done, s + 1)
            low(s)
        dve.wait_ge(inputs_in, 64)
        for l_ in range(DEPTH):
            V.tensor_scalar(nsink[:, 8 * l_:8 * l_ + 8], col(l_, "sink", 0, 8), -1.0, None, ALU.mult).then_inc(nsink_done, 1)
        dve.wait_ge(nsink_done, DEPTH)
        with dve.Fori(0, DEPTH) as l:
            W = l * PANELS
            V.memset(G[:, :, 0:CF_H], 0.0).then_inc(g_zero, 1)
            norm(l, A_N1, l * 16, "g1", l * 3 + 1)
            with dve.Fori(0, 4) as i:
                for j in range(2):
                    step(W + i * 4, P_CF + 2 * j, 0)
                    step(W + i * 4, P_CF + 2 * j + 1, 1)
                    dve.wait_ge(a_out, l * NA + i * 2 + (A_CF + j + 3))
                    for piece in PIECES:
                        last = V.tensor_tensor(tile(G, i * 2 + j, after(piece[3], CF_H), piece[2]),
                                               slot(O_SG, TOK, j)[:, piece[3]:piece[3] + piece[2]],
                                               d_piece(D_CF + j, piece), ALU.mult)
                    last.then_inc(d_out, 1)
            dve.wait_ge(d_out, d_ready(l, D_CF + 7))
            dve.wait_ge(g_zero, l + 1)
            dve.wait_ge(hist_in, l * 16 + 16)
            taps(l, 0, 0, KT)
            dve.wait_ge(x_spilled, l * 16 + 16)
            V.sem_inc(carrier, 1)
            with dve.Fori(0, 4) as i:
                for j in range(2):
                    step(W + i * 2, P_Q + j, j)
                    taps(l, i + 1, 4 * j, 4 * j + 4)
                for j in range(2):
                    dve.wait_ge(a_out, l * NA + i * 2 + (A_Q + j + 3))
                    V.tensor_tensor(tile(X, i * 2 + j), slot(O_QR, TOK, j), cos, ALU.mult).then_inc(qtmp, 1)
                    dve.wait_ge(qrot_ps, l * KT + i * 2 + (j + 1))
                    V.tensor_tensor(halves(slot(O_TQ, TOK, j)), halves(sin), d_tile(D_Q + j), ALU.mult).then_inc(d_out, 1)
                    dve.wait_ge(d_out, l * ND + i * 2 + (D_Q + j + 3))
                    V.tensor_tensor(tile(X, i * 2 + j), tile(X, i * 2 + j), slot(O_TQ, TOK, j), ALU.add).then_inc(qrot, 1)
            step(W, P_K, 0)
            step(W, P_V, 1)
            for v in range(N_KV):
                for j in range(2):
                    dve.wait_ge(krot_ps, l * 4 + 2 * v + j + 1)
                    V.tensor_tensor(halves(slot(O_TQ, TOK, j)), halves((cos, sin)[j]), d_tile(D_K + 2 * v + j), ALU.mult) \
                        .then_inc(d_out, 1)
                dve.wait_ge(d_out, d_ready(l, D_K + 2 * v + 1))
                V.tensor_tensor(KD[:, v, 0:TP], slot(O_TQ, TOK, 0)[:, 0:TP], slot(O_TQ, TOK, 1)[:, 0:TP], ALU.add)
                V.tensor_tensor(KD[:, v, TP + WINDOW:720], slot(O_TQ, TOK, 0)[:, TP:TOK], slot(O_TQ, TOK, 1)[:, TP:TOK],
                                ALU.add).then_inc(krot, 1)
                dve.wait_ge(krot, l * 2 + v + 1)
            for j in range(2):
                dve.wait_ge(vt_ps, l * 2 + j + 1)
                b0 = 4 + 2 * ((D_V + j) % 2)
                groups = (((0, 0, 4, 128, 0), (1, 0, 3, 128, 4)), ((0, 0, 4, 64, 1), (1, 0, 3, 64, 5), (1, 3, 1, 16, 0)))[j]
                for b, c0, n, rows, v0 in groups:
                    last = V.tensor_copy(VV[0:rows, v0:v0 + n, j, :],
                                         PS[0:rows, b0 + b, 128 * c0:128 * (c0 + n)].rearrange("p (t n) -> p t n", n=128))
                last.then_inc(d_out, 1)
            dve.wait_ge(d_out, d_ready(l, D_V + 1))

            def maxima(n, v):
                nk = chunk_span(n)[2]
                it = l * 20 + n * 2 + v
                dve.wait_ge(s_done, it + 3)
                sc = PS[:, 2 * v:2 * v + 2, :].rearrange("p b (i n) -> p (b i) n", i=2)[:, :, 0:nk]
                V.tensor_reduce(mx[:, v, :], sc, AX.X, ALU.max).then_inc(mx_done, 1)
                dve.wait_ge(mx_done, it + 1)
                dve.wait_ge(p_done, it + 1)
                ns = nsink[:, bass.ds(l * 8 + 4 * v, 4)]
                V.scalar_tensor_tensor(nm[:, v, :], mx[:, v, :], -SCALE, ns, ALU.mult, ALU.min).then_inc(nm_done, 1)
                dve.wait_ge(nm_done, 2 * it + 1)
                V.tensor_tensor(ds_[:, v, :], nm[:, v, :], ns, ALU.subtract).then_inc(nm_done, 1)

            def copy_rest(n, v):
                n2 = max(chunk_span(n)[2] - 128, 0)
                it = l * 20 + n * 2 + v
                if n2:
                    dve.wait_ge(t_done, it + 3)
                    dve.wait_ge(o_done, it + 1)
                    V.tensor_copy(scr[0:n2, O_PT2 + 512 * v:O_PT2 + 512 * v + 512], PS[0:n2, 5, :]).then_inc(pt2_done, 1)

            def denominators(n, v):
                it = l * 20 + n * 2 + v
                dve.wait_ge(p_done, it + 3)
                V.tensor_tensor(sums[:, v, :], sums[:, v, :], es[:, v, :], ALU.add).then_inc(den_done, 1)
                dve.wait_ge(den_done, it + 1)
                V.reciprocal(rinv[:, v, :], sums[:, v, :]).then_inc(rinv_done, 1)

            def norm_outputs(n, v):
                it = l * 20 + n * 2 + v
                dve.wait_ge(rinv_done, it + 3)
                dve.wait_ge(o_done, it + 3)
                V.tensor_tensor(view(O_ON + 256 * v, 256).rearrange("p (i n) -> p i n", i=4),
                                PS[:, 6, 0:256].rearrange("p (i n) -> p i n", i=4),
                                rinv[:, v, :].rearrange("p (i o) -> p i o", o=1).to_broadcast([128, 4, 64]),
                                ALU.mult).then_inc(on_done, 1)

            def outputs_lo(n, v):
                q0 = chunk_span(n)[0]
                dve.wait_ge(oh_done, l * 20 + n * 2 + v + 1)
                src = PS[:, 7, 0:256].rearrange("p (t n) -> p t n", n=64)
                at = slice(q0, q0 + 64) if isinstance(q0, int) else bass.ds(q0, 64)
                V.tensor_tensor(bl[:, 4 * v:4 * v + 4, at], src, f(bh[:, 4 * v:4 * v + 4, at]), ALU.subtract) \
                    .then_inc(ol_done, 1)

            def attention(n):
                if has(n - 1):
                    denominators(n - 1, 0)
                if has(n):
                    maxima(n, 0)
                if has(n - 2):
                    norm_outputs(n - 2, 1)
                if has(n - 1):
                    copy_rest(n - 1, 0)
                if has(n):
                    taps(l, n + 5, 0, 4)
                if has(n - 2):
                    outputs_lo(n - 2, 0)
                if has(n - 1):
                    denominators(n - 1, 1)
                if has(n):
                    maxima(n, 1)
                if has(n - 1):
                    norm_outputs(n - 1, 0)
                    copy_rest(n - 1, 1)
                if has(n):
                    taps(l, n + 5, 4, 8)
                if has(n - 2):
                    outputs_lo(n - 2, 1)

            for n in range(5):
                attention(n)
            with dve.Fori(5, N_CHUNK) as n:
                attention(n)
            for n in range(N_CHUNK, CHUNKS + 2):
                attention(n)
            with dve.Fori(0, 4) as i:
                for j in range(2):
                    step(W + i * 4, P_OA + 2 * j, 0)
                    taps(l, i * 2 + (15 + j), 0, 4)
                    step(W + i * 4, P_OA + 2 * j + 1, 1)
                    dve.wait_ge(a_out, l * NA + i * 2 + (A_OA + j + 3))
                    V.tensor_tensor(halves(tile(X, i * 2 + j)), halves(slot(O_SG, TOK, j)), d_tile(D_OA + j),
                                    ALU.mult).then_inc(d_out, 1)
                    taps(l, i * 2 + (15 + j), 4, 8)
            dve.wait_ge(kv_out, l * 112 + 112)
            for j in range(2):
                V.memset(slot(O_CH, S_IN, j)[:, 0:S_H], 0.0).then_inc(sc_hist, 1)
            with dve.Fori(0, 4) as i:
                for j in range(2):
                    m = i * 2 + j
                    step(W + i * 6, P_SC + 3 * j, j)
                    ch, cv = slot(O_CH, S_IN, j), slot(O_CV, S_OUT, j)
                    V.tensor_copy(ch[:, TP + S_H:TP + 2 * S_H], col(l, "sch", m * 2, 2)).then_inc(sc_hist, 1)
                    taps(l, i * 2 + (23 + j), 0, 4)
                    step(W + i * 6, P_SC + 3 * j + 1, 1 - j)
                    dve.wait_ge(a_out, l * NA + i * 2 + (A_SC + j + 3))
                    for piece in PIECES:
                        o = after(piece[3], S_H)
                        last = V.tensor_tensor(ch[:, o:o + piece[2]], slot(O_CT, TOK, j)[:, piece[3]:piece[3] + piece[2]],
                                               d_piece(D_SC + 2 * j, piece), ALU.mult)
                    last.then_inc(d_out, 1)
                    dve.wait_ge(d_out, l * ND + i * 4 + (D_SC + 2 * j + 3))
                    keep_tail(sct, m, ch, sc_tail_done)
                    conv3(l, ch, cv, "scw", m, sc_tap, l * 24 + i * 6 + 3 * j)
                    step(W + i * 6, P_SC + 3 * j + 2, j)
                    dve.wait_ge(sc_tap, l * 24 + i * 6 + (3 * j + 3))
                    bt = slot(O_BT, TOK, j)
                    for piece in PIECES:
                        o = piece[3] + (S_H if piece[3] >= TP else 0)
                        last = V.tensor_tensor(bt[:, piece[3]:piece[3] + piece[2]], cv[:, o:o + piece[2]],
                                               d_piece(D_SC + 2 * j + 1, piece), ALU.mult)
                    last.then_inc(d_out, 1)
                    taps(l, i * 2 + (23 + j), 4, 8)
                    dve.wait_ge(sc_hi, l * KT + i * 2 + (j + 1))
                    V.tensor_tensor(tile(bl, m), bt, f(tile(bh, m)), ALU.subtract).then_inc(sc_lo, 1)

            def merge(m, j, d, ready):
                V.tensor_tensor(halves(slot(O_TQ, TOK, j)), halves(slot(O_SG, TOK, j)), d_tile(d), ALU.mult) \
                    .then_inc(d_out, 1)
                dve.wait_ge(d_out, ready)
                V.tensor_tensor(tile(X, m), tile(X, m), slot(O_TQ, TOK, j), ALU.add).then_inc(mg_done, 1)

            def out_sc(i0, n, a0):
                def body(i):
                    for j in range(2):
                        step(W + i * 4, P_OS + 4 * i0 + 2 * j, 0)
                        step(W + i * 4, P_OS + 4 * i0 + 2 * j + 1, 1)
                        dve.wait_ge(a_out, l * NA + i * 2 + (a0 + j + 3))
                        merge(i * 2 + (2 * i0 + j), j, D_OS + j, l * ND + i * 2 + (D_OS + 2 * i0 + j + 3))
                if n == 1:
                    body(0)
                else:
                    with dve.Fori(0, n) as i:
                        body(i)
            out_sc(0, 1, A_OS)
            dve.wait_ge(a_out, a_ready(l, A_MEAN))
            for m in range(KT):
                V.tensor_tensor(acc[:, m, :], acc[:, m, :], view(O_MU, 622), ALU.subtract).then_inc(ln_sub, 1)
            out_sc(1, 1, A_MEAN + 1)
            out_sc(2, 1, A_VAR + 1)
            rsqrt(a_ready(l, A_VAR), 311, l * 3 + 2)
            for m in range(KT):
                V.tensor_tensor(acc[:, m, :], acc[:, m, :], view(O_RT, 622), ALU.mult).then_inc(ln_mul, 1)
            out_sc(3, 1, A_VAR + 3)
            for m in range(KT):
                dve.wait_ge(cf_hi, l * KT + m + 1)
                V.tensor_tensor(bl[:, m, 0:TP], acc[:, m, 0:TP], f(bh[:, m, 0:TP]), ALU.subtract)
                V.tensor_tensor(bl[:, m, TP:TOK], acc[:, m, TP + CF_H:CF_OUT], f(bh[:, m, TP:TOK]), ALU.subtract) \
                    .then_inc(cf_lo, 1)
            with dve.Fori(0, 4) as i:
                for j in range(2):
                    m = i * 2 + j
                    step(W + i * 4, P_OC + 2 * j, 0)
                    step(W + i * 4, P_OC + 2 * j + 1, 1)
                    dve.wait_ge(a_out, l * NA + i * 2 + (A_OC + j + 3))
                    merge(m, j, D_OC + j, l * ND + i * 2 + (D_OC + j + 3))
                    dve.wait_ge(mg_hi, l * KT + i * 2 + (j + 1))
                    V.tensor_tensor(tile(ml, m), tile(X, m), f(tile(mh, m)), ALU.subtract).then_inc(mg_lo, 1)
            with dve.Fori(0, 4) as i:
                for j in range(2):
                    step(W + i * 2, P_WO + j, j)
                    dve.wait_ge(x_back, l * (KT * 16) + i * 32 + (16 * j + 16))
                    V.tensor_tensor(halves(tile(X, i * 2 + j)), halves(tile(X, i * 2 + j)), d_tile(D_WO + j), ALU.add) \
                        .then_inc(d_out, 1)
            norm(l, A_N2, l * 16 + 8, "g2", l * 3 + 3)
            dve.wait_ge(nx_lo, l * 16 + 16)
            for j in range(2):
                V.memset(slot(O_HG, S_IN, j)[:, 0:S_H], 0.0).then_inc(ff_hist, 1)
                V.memset(slot(O_HU, S_IN, j)[:, 0:S_H], 0.0).then_inc(ff_hist, 1)
            for t0, n, p0, a0, d0 in thirds:
                with dve.Fori(0, n // 2) as i:
                    for j in range(2):
                        m = i * 2 + (t0 + j)
                        hg, hu = slot(O_HG, S_IN, j), slot(O_HU, S_IN, j)
                        gc, uc = slot(O_GC, S_OUT, j), slot(O_UC, S_OUT, j)
                        tb = l * (FT * 6) + i * 12 + (t0 * 6 + 6 * j + 12)
                        step(W + i * 4, p0 + 2 * j, 0)
                        V.tensor_copy(hg[:, TP + S_H:TP + 2 * S_H], col(l, "ffh", m * 2, 2)).then_inc(ff_hist, 1)
                        V.tensor_copy(hu[:, TP + S_H:TP + 2 * S_H], col(l, "ffh", m * 2 + 2 * FT, 2)).then_inc(ff_hist, 1)
                        dve.wait_ge(a_out, l * NA + i * 2 + (a0 + j + 3))
                        dve.wait_ge(ff_hist, l * (4 + 2 * FT) + i * 4 + (4 + 2 * t0 + 2 * j + 2))
                        keep_tail(fft, m, hg, ff_tail_done)
                        conv3(l, hg, gc, "ffw", m, ff_tap, tb)
                        step(W + i * 4, p0 + 2 * j + 1, 1)
                        for piece in PIECES:
                            o = after(piece[3], S_H)
                            last = V.tensor_copy(hu[:, o:o + piece[2]], d_piece(d0 + j, piece))
                        last.then_inc(d_out, 1)
                        dve.wait_ge(d_out, l * ND + i * 2 + (d0 + j + 3))
                        keep_tail(fft, m + FT, hu, ff_tail_done)
                        conv3(l, hu, uc, "ffw", m + FT, ff_tap, tb + 3)
                        dve.wait_ge(ff_silu, l * FT + i * 2 + (t0 + j + 1))
                        dve.wait_ge(ff_tap, tb + 6)
                        pb_ = slot(O_PB, S_OUT, j)
                        V.tensor_tensor(pb_, gc, uc, ALU.mult).then_inc(ff_prod, 1)
                        dve.wait_ge(ff_hi, l * FT + i * 2 + (t0 + j + 1))
                        V.tensor_tensor(tile(bl, i * 2 + j, 0, TP), pb_[:, 0:TP], f(tile(bh, i * 2 + j, 0, TP)), ALU.subtract)
                        V.tensor_tensor(tile(bl, i * 2 + j, TP, DEC_SEQ), pb_[:, TP + S_H:S_OUT],
                                        f(tile(bh, i * 2 + j, TP, DEC_SEQ)), ALU.subtract).then_inc(ff_lo, 1)
                with dve.Fori(0, 4) as i:
                    for j in range(2):
                        step(W + i * 2, p0 + 2 * n + j, j)
                        V.tensor_tensor(halves(tile(X, i * 2 + j)), halves(tile(X, i * 2 + j)), d_tile(d0 + n + j), ALU.add) \
                            .then_inc(d_out, 1)
            dve.wait_ge(d_out, (l + 1) * ND + 2)
        rsqrt(a_ready(DEPTH, A_N1), HALF, DEPTH * 3 + 1)
        for m in range(KT):
            V.scalar_tensor_tensor(X[:, m, :], X[:, m, :], fg[:, m:m + 1], view(O_RT, TOK), ALU.mult, ALU.mult) \
                .then_inc(yn_done, 1)


def weight_panels(w_in, w_attn_out, w_sc_out, w_cf_out, w_o, w_up, w_down):
    q, kv = N_HEADS * HEAD_DIM, N_KV * HEAD_DIM
    at = np.cumsum([0, q, kv, kv] + [D_MODEL] * 8)
    panels = []
    wa = w_attn_out.reshape(DEPTH, N_KV, 2, 2, 2, HEAD_DIM, D_MODEL).transpose(0, 1, 2, 4, 3, 5, 6)
    wa = wa.reshape(DEPTH, q, D_MODEL)

    def cols(w, l, c, rows=slice(None)):
        p = w[l, rows, c * 128:(c + 1) * 128]
        p = p.reshape(-1, 128, 128).transpose(1, 0, 2)
        if p.shape[1] < KT:
            p = np.concatenate([p, np.zeros((128, KT - p.shape[1], 128), p.dtype)], axis=1)
        return p.reshape(128, KT * 128)

    for l in range(DEPTH):
        part = [w_in[:, :, at[i]:at[i + 1]] for i in range(10)] + [w_in[:, :, at[10]:]]
        wq, wk, wv, sb_, sc_, sh_, ca, cg, ga, gs, gc = part
        for m in range(KT):
            panels += [cols(cg, l, m), cols(ca, l, m)]
        panels += [cols(wq, l, m) for m in range(KT)]
        panels += [cols(wk, l, 0), cols(wv, l, 0)]
        for m in range(KT):
            panels += [cols(ga, l, m), cols(wa, l, m)]
        for m in range(KT):
            panels += [cols(sc_, l, m), cols(sh_, l, m), cols(sb_, l, m)]
        for m in range(KT):
            panels += [cols(gs, l, m), cols(w_sc_out, l, m)]
        for m in range(KT):
            panels += [cols(gc, l, m), cols(w_cf_out, l, m)]
        panels += [cols(w_o, l, m) for m in range(KT)]
        t0 = 0
        for n in THIRDS:
            for m in range(t0, t0 + n):
                panels += [cols(w_up, l, m), cols(w_up, l, m + FT)]
            panels += [cols(w_down, l, m, slice(t0 * 128, (t0 + n) * 128)) for m in range(KT)]
            t0 += n
    return np.ascontiguousarray(np.stack(panels + panels[:2]))


def channel_major(a):
    lead = a.shape[:-1]
    a = a.reshape(*lead, a.shape[-1] // 128, 128)
    n = a.ndim
    return a.transpose(n - 1, n - 2, *range(n - 2))


def constants():
    half = ROT // 2
    pos = np.concatenate([np.arange(TP), PAST + np.arange(DEC_SEQ)]).astype(np.float32)
    inv = np.power(np.float32(THETA), -np.arange(0, ROT, 2, dtype=np.float32) / np.float32(ROT)).astype(np.float32)
    ang = inv[:, None] * pos[None, :]
    c = np.ones((HEAD_DIM, TOK), np.float32)
    s = np.zeros((HEAD_DIM, TOK), np.float32)
    for d in range(ROT):
        c[d], s[d] = np.cos(ang[d % half]), np.sin(ang[d % half])
    rot = np.zeros((128, 128), np.float32)
    for h in (0, HEAD_DIM):
        for d in range(half):
            rot[h + d + half, h + d] = -1.0
            rot[h + d, h + d + half] = 1.0
    eye = np.eye(128, dtype=np.float32)
    dup = [np.concatenate([m[:, v:v + 64]] * 2, axis=1) for v in (0, 64) for m in (eye, rot)]
    parts = [np.concatenate([c, c]), np.concatenate([s, s]), eye, np.ones((128, 128), np.float32), rot, dup[0], dup[1],
             dup[2], dup[3], np.full((128, 1), EPS, np.float32)]
    return np.ascontiguousarray(np.concatenate(parts, axis=1))


def kernel(x_prompt, x_sample, cache_k, cache_v, state_sc, state_cf, state_ffn, meta_tokens, norm1_g, w_in,
           b_gate, attn_sinks, w_attn_out, sc_conv_w, w_sc_out, cf_conv_w, cf_ln_g, cf_ln_b, w_cf_out, w_o,
           norm2_g, w_up, ffn_conv_w, w_down, final_g):
    import concourse.bacc as bacc
    from concourse.bass_utils import run_bass_kernel_spmd

    (x_prompt, x_sample, cache_k, cache_v, state_sc, state_cf, state_ffn, meta_tokens, norm1_g, w_in, b_gate, attn_sinks,
     w_attn_out, sc_conv_w, w_sc_out, cf_conv_w, cf_ln_g, cf_ln_b, w_cf_out, w_o, norm2_g, w_up, ffn_conv_w, w_down,
     final_g) = (np.asarray(a) for a in (
         x_prompt, x_sample, cache_k, cache_v, state_sc, state_cf, state_ffn, meta_tokens, norm1_g, w_in, b_gate,
         attn_sinks, w_attn_out, sc_conv_w, w_sc_out, cf_conv_w, cf_ln_g, cf_ln_b, w_cf_out, w_o, norm2_g, w_up,
         ffn_conv_w, w_down, final_g))
    vecs = []
    for l in range(DEPTH):
        sinks = np.repeat(attn_sinks[l].reshape(8, 2).transpose(1, 0), 64, axis=0)
        vecs += [channel_major(norm1_g[l]), channel_major(norm2_g[l]), channel_major(b_gate[l]), channel_major(cf_ln_g[l]),
                 channel_major(cf_ln_b[l]), channel_major(sc_conv_w[l]), channel_major(cf_conv_w[l]),
                 channel_major(ffn_conv_w[l]), channel_major(state_sc[l, 0]), channel_major(state_ffn[l, 0]), sinks]
    kc = cache_k[:, 0].transpose(0, 3, 2, 1)
    arrays = {
        "weights": weight_panels(w_in, w_attn_out, w_sc_out, w_cf_out, w_o, w_up, w_down),
        "xt": channel_major(np.concatenate([meta_tokens, x_prompt[0], x_sample[0]])),
        "vecs": np.concatenate([v.reshape(128, -1) for v in vecs], axis=1),
        "consts": constants(),
        "final_g": channel_major(final_g),
        "kcache": np.concatenate([kc, kc], axis=1),
        "vcache": cache_v.reshape(DEPTH, WINDOW, N_KV * HEAD_DIM),
        "cfhist": np.stack([channel_major(state_cf[l, 0]) for l in range(DEPTH)]),
    }
    arrays = {k: np.ascontiguousarray(v) for k, v in arrays.items()}
    outs = {
        "y": (128, KT, TOK), "kp": (DEPTH, 128, WINDOW), "vp": (DEPTH, WINDOW, 128), "scp": (DEPTH, 128, KT * 2 * S_H),
        "cfp": (DEPTH, 128, KT, 2, CF_H), "ffp": (DEPTH, 128, 2 * FT * 2 * S_H), "ks": (DEPTH, 128, WINDOW),
        "vs": (DEPTH, WINDOW, 128),
    }
    nc = bacc.Bacc("TRN2", target_bir_lowering=False, num_devices=1)
    aps = {k: nc.dram_tensor(f"in_{k}", v.shape, F32, kind="ExternalInput").ap() for k, v in arrays.items()}
    aps["spill"] = nc.dram_tensor("spill", (128, KT, TOK), F32, kind="Internal").ap()
    for k, shape in outs.items():
        aps[k] = nc.dram_tensor(f"out_{k}", shape, F32, kind="ExternalOutput").ap()
    encoder(nc, **aps)
    r = run_bass_kernel_spmd(nc, [{f"in_{k}": v for k, v in arrays.items()}], core_ids=[0]).results[0]
    got = {k: np.asarray(r[f"out_{k}"]) for k in outs}

    def rows(a):
        return np.ascontiguousarray(a.transpose(2, 1, 0).reshape(a.shape[2], -1))

    y = rows(got["y"])

    def heads(a, frames_last):
        a = a.transpose(0, 2, 1) if frames_last else a
        return np.ascontiguousarray(a).reshape(DEPTH, 1, WINDOW, N_KV, HEAD_DIM)

    def tails(a, tiles, n, g):
        a = a.reshape(DEPTH, 128, tiles, 2, n)[:, :, :, g]
        return np.ascontiguousarray(np.stack([rows(a[l]) for l in range(DEPTH)])[:, None])

    return (y[N_META:TP][None], y[TP:][None],
            heads(got["kp"], True), heads(got["vp"], False), tails(got["scp"], KT, S_H, 0), tails(got["cfp"], KT, CF_H, 0),
            tails(got["ffp"], 2 * FT, S_H, 0),
            heads(got["ks"], True), heads(got["vs"], False), tails(got["scp"], KT, S_H, 1), tails(got["cfp"], KT, CF_H, 1),
            tails(got["ffp"], 2 * FT, S_H, 1))
```

```python
import numpy as np
import concourse.bass as bass
from concourse import mybir
from contextlib import ExitStack

F32 = mybir.dt.float32
F32R = mybir.dt.float32r
ALU = mybir.AluOpType
ACT = mybir.ActivationFunctionType
AX = mybir.AxisListType

DEPTH, D_MODEL, SEQ, N_META, DEC_SEQ, CHUNK, WINDOW, PAST = 2, 1024, 512, 16, 64, 64, 128, 128
HEAD_DIM, N_HEADS, N_KV, ROT, THETA = 64, 16, 2, 16, 500000.0
D_FF, SC_K, CF_K, FFN_K, EPS = 2816, 3, 31, 3, 1e-5
TP = N_META + SEQ
TOK = TP + DEC_SEQ
HALF = TOK // 2
KT = D_MODEL // 128
FT = D_FF // 128
THIRDS = (8, 8, 6)
SCALE = HEAD_DIM ** -0.5
N_CHUNK = 1 + SEQ // CHUNK
CF_H, S_H = CF_K - 1, SC_K - 1
CF_IN, CF_OUT = 2 * CF_H + TOK, CF_H + TOK
S_IN, S_OUT = 2 * S_H + TOK, S_H + TOK
VEC = {}
VEC_N = 0
for _name, _n in (("g1", KT), ("g2", KT), ("bg", 3 * KT), ("lng", KT), ("lnb", KT), ("scw", SC_K * KT),
                  ("cfw", CF_K * KT), ("ffw", FFN_K * 2 * FT), ("sch", S_H * KT), ("ffh", S_H * 2 * FT), ("sink", 8)):
    VEC[_name] = VEC_N
    VEC_N += _n
CON = {}
CON_N = 0
for _name, _n in (("ident", 128), ("ones", 128), ("rot", 128), ("ka", 128), ("kar", 128), ("kb", 128), ("kbr", 128),
                  ("eps", 1), ("cos", TOK), ("sin", TOK)):
    CON[_name] = CON_N
    CON_N += _n

P_CF, P_Q, P_K, P_V, P_OA, P_SC, P_OS, P_OC, P_WO, P_FF = 0, 16, 24, 25, 26, 42, 66, 82, 98, 106
PANELS = 174
A_N1, A_CF, A_Q, A_K, A_V, A_OA, A_SC, A_OS, A_MEAN, A_VAR, A_OC, A_N2, A_FF, NA = \
    0, 1, 9, 17, 18, 19, 27, 35, 37, 41, 45, 53, 54, 76
D_CF, D_Q, D_K, D_V, D_OA, D_SC, D_OS, D_OC, D_WO, D_FF, ND = 0, 8, 16, 20, 22, 30, 46, 54, 62, 70, 116
S_N1, S_MEAN, S_VAR, S_N2, NS = 0, 1, 2, 3, 4
Q_N1, Q_VAR, Q_N2, NQ = 0, 1, 2, 3
TAPS_GLU = 8
CHUNKS = N_CHUNK + 1

O_KD, O_VV, O_QS, O_P, O_PT1, O_PT2, O_ON = 0, 1440, 3488, 4512, 6048, 7072, 8096
O_QR, O_TQ, O_SG = 4512, 6048, 7232
O_SQ, O_SS, O_RT, O_MU, O_NT = 0, 1244, 1866, 2488, 2488
O_CT, O_CH, O_CV, O_BT = 0, 1184, 2376, 3564
O_HG, O_HU, O_GC, O_UC, O_PB, O_RF = 0, 1192, 2384, 3572, 4760, 5960
N_SCRATCH = 8608

PIECES = ((0, 0, HALF, 0), (1, 0, TP - HALF, HALF), (1, TP - HALF, DEC_SEQ, TP))


def halves(ap):
    return ap.rearrange("p (h n) -> p h n", h=2)


def after(t0, hist):
    return t0 + hist + (hist if t0 >= TP else 0)


def a_free(l, a):
    return l * NA + a + 1


def a_ready(l, a):
    return l * NA + a + 3


def d_free(l, d):
    return l * ND + d + 1


def d_ready(l, d):
    return l * ND + d + 3


def a_gate_sc(m):
    return A_OS + m + (m >= 2) + (m >= 5)


def chunk_span(c):
    if isinstance(c, int):
        if c == CHUNKS - 1:
            return TP, TP, WINDOW + DEC_SEQ
        if c == 0:
            return 0, 0, N_META
        if c < 3:
            return N_META + CHUNK * (c - 1), 0, N_META + CHUNK * c
    return c * CHUNK + (N_META - CHUNK), c * CHUNK + (N_META - 3 * CHUNK), 3 * CHUNK


def it2(l, n, v):
    return l * 16 + n * 2 + (v - 4)


def v_blocks(j):
    if j == 0:
        return [(0, 128)] + [(chunk_span(c)[1], 128) for c in range(3, N_CHUNK)]
    return [(chunk_span(c)[1] + 128, CHUNK) for c in range(3, N_CHUNK)] + [(TP, DEC_SEQ), (128, N_META)]


def has(c):
    return not isinstance(c, int) or 0 <= c < CHUNKS


def v_tile(c):
    if isinstance(c, int):
        return 7 if c == CHUNKS - 1 else max(c - 2, 0)
    return c - 2


def encoder(nc, weights, xt, vecs, consts, final_g, kcache, vcache, cfhist, spill, y, kp, vp, scp, cfp, ffp, ks, vs):
    ctx = ExitStack()

    def sb(name, shape, dt=F32):
        return ctx.enter_context(nc.sbuf_tensor(name, shape, dt))

    def sem(name):
        return ctx.enter_context(nc.semaphore(name))

    xh, xl = sb("xn_hi", [128, KT, TOK], F32R), sb("xn_lo", [128, KT, TOK], F32R)
    bh, bl = sb("branch_hi", [128, KT, TOK], F32R), sb("branch_lo", [128, KT, TOK], F32R)
    X = sb("x_q_merged", [128, KT, TOK])
    raw = sb("raw", [128, 2, KT * 128])
    wh, wl = sb("w_hi", [128, 2, KT * 128], F32R), sb("w_lo", [128, 2, KT * 128], F32R)
    scr = sb("scratch", [128, N_SCRATCH])
    vec = sb("vec", [128, DEPTH * VEC_N])
    con = sb("con", [128, CON_N])
    fg = sb("fg", [128, KT])
    sct = sb("sc_tail", [128, KT, 2 * S_H])
    fft = sb("ffn_tail", [128, 2 * FT, 2 * S_H])
    mx, nm, ds_, es = (sb(n, [128, N_KV, 4]) for n in ("score_max", "neg_max", "sink_diff", "sink_exp"))
    sums, rinv = sb("exp_sums", [128, N_KV, 4]), sb("inv_den", [128, N_KV, 4])
    nsink = sb("neg_sink", [128, DEPTH * 8])
    with nc.sbuf_tensor("glu", [128, KT, CF_IN], F32) as G, nc.sbuf_tensor("cf_acc", [128, KT, CF_OUT], F32) as acc:
        pass
    with nc.sbuf_tensor("merged_hi", [128, KT, TOK], F32R) as mh, nc.sbuf_tensor("merged_lo", [128, KT, TOK], F32R) as ml:
        pass
    PS = ctx.enter_context(nc.psum_tensor("ps", [128, 8, 512], F32))

    def view(off, n):
        return scr[:, off:off + n]

    def slot(off, n, s):
        return scr[:, off + n * s:off + n * (s + 1)]

    KD = view(O_KD, 2 * 720).rearrange("p (v n) -> p v n", v=2)
    VV = view(O_VV, 2048).rearrange("p (c j n) -> p c j n", c=8, j=2)
    ident, ones = con[:, CON["ident"]:CON["ident"] + 128], con[:, CON["ones"]:CON["ones"] + 128]
    cos, sin = con[:, CON["cos"]:CON["cos"] + TOK], con[:, CON["sin"]:CON["sin"] + TOK]
    eps = con[:, CON["eps"]:CON["eps"] + 1]

    def f(ap):
        return ap.bitcast(F32)

    def col(l, name, i, n=1):
        if isinstance(l, int) and isinstance(i, int):
            at = l * VEC_N + VEC[name] + i
            return vec[:, at:at + n]
        return vec[:, bass.ds(l * VEC_N + VEC[name] + i, n)]

    def tile(t, m, a=0, n=None):
        n = t.shape[2] if n is None else n
        if isinstance(m, int) and isinstance(a, int):
            return t[:, m, a:a + n]
        return t[:, :, :].rearrange("p t n -> p (t n)")[:, bass.ds(m * t.shape[2] + a, n)]

    def a_tile(a, n=HALF):
        b = 2 * (a % 2)
        return PS[:, b:b + 2, 0:n]

    def d_tile(d, n=HALF):
        b = 4 + 2 * (d % 2)
        return PS[:, b:b + 2, 0:n]

    def d_piece(d, piece):
        return PS[:, 4 + 2 * (d % 2) + piece[0], piece[1]:piece[1] + piece[2]]

    def a_piece(a, piece):
        return PS[:, 2 * (a % 2) + piece[0], piece[1]:piece[1] + piece[2]]

    raw_in = [sem("raw_in0"), sem("raw_in1")]
    hi_done, lo_done = sem("hi_done"), sem("lo_done")
    panel_done = sem("panel_done")
    a_out, d_out = sem("a_out"), sem("d_out")
    x_in = [sem(f"x_in{i}") for i in range(4)]
    inputs_in = sem("inputs_in")
    late_in = sem("late_in")
    x_spilled = sem("x_spilled")
    x_back = sem("x_back")
    cache_in = sem("cache_in")
    hist_in = sem("hist_in")
    kv_out = sem("kv_out")
    tails_out = sem("tails_out")
    small_out = sem("small_out")
    vs_out = sem("vs_out")
    y_out = sem("y_out")
    sq_done, sq_sum = sem("sq_done"), sem("sq_sum")
    mean_sum = sem("mean_sum")
    sum_ps = sem("sum_ps")
    rs_done = sem("rs_done")
    nx_mul, nx_hi, nx_lo = sem("nx_mul"), sem("nx_hi"), sem("nx_lo")
    qrot = sem("qrot")
    qtmp = sem("qtmp")
    krot = sem("krot")
    qrot_ps, krot_ps = sem("qrot_ps"), sem("krot_ps")
    vt_ps = sem("vt_ps")
    zero_qs = sem("zero_qs")
    qs_done = sem("qs_done")
    s_done = sem("s_done")
    nm_done = sem("nm_done")
    mx_done = sem("mx_done")
    es_done, p_done = sem("es_done"), sem("p_done")
    t_done = sem("t_done")
    pt1_done, pt2_done = sem("pt1_done"), sem("pt2_done")
    den_done, rinv_done = sem("den_done"), sem("rinv_done")
    o_done, on_done, ot_done = sem("o_done"), sem("on_done"), sem("ot_done")
    oh_done, ol_done = sem("oh_done"), sem("ol_done")
    tap_glu, tap_rest = sem("tap_glu"), [sem(f"tap_rest{g}") for g in range(4)]
    mg_done = sem("mg_done")
    mg_hi, mg_lo = sem("mg_hi"), sem("mg_lo")
    sc_hist = sem("sc_hist")
    sc_tap = sem("sc_tap")
    sc_hi, sc_lo = sem("sc_hi"), sem("sc_lo")
    sc_tail_done = sem("sc_tail_done")
    ln_sub, ln_mul, ln_silu = sem("ln_sub"), sem("ln_mul"), sem("ln_silu")
    cf_hi, cf_lo = sem("cf_hi"), sem("cf_lo")
    g_zero = sem("g_zero")
    ff_zero, ff_hist = sem("ff_zero"), sem("ff_hist")
    ff_first, ff_tap = sem("ff_first"), sem("ff_tap")
    ff_gate, ff_silu, ff_prod = sem("ff_gate"), sem("ff_silu"), sem("ff_prod")
    ff_hi, ff_lo = sem("ff_hi"), sem("ff_lo")
    ff_tail_done = sem("ff_tail_done")
    yn_done = sem("yn_done")
    nsink_done = sem("nsink_done")
    carrier = sem("carrier")

    thirds, at = [], (0, P_FF, A_FF, D_FF)
    for n in THIRDS:
        thirds.append((at[0], n, at[1], at[2], at[3]))
        at = (at[0] + n, at[1] + 2 * n + KT, at[2] + n, at[3] + n + KT)

    block = ctx.enter_context(nc.Block())

    @block.sync
    def _(sp):
        for i in range(4):
            sp.dma_start(X[:, 2 * i:2 * i + 2, :], xt[:, 2 * i:2 * i + 2, :]).then_inc(x_in[i], 16)
        sp.dma_start(con[:, 0:CON["cos"]], consts[:, 0:CON["cos"]]).then_inc(inputs_in, 16)
        sp.dma_start(vec[:, :], vecs).then_inc(inputs_in, 16)
        for s in range(2):
            sp.dma_start(raw[:, s, :], weights[s, :, :]).then_inc(raw_in[s], 16)
        sp.dma_start(con[:, CON["cos"]:], consts[:, CON["cos"]:]).then_inc(late_in, 16)
        sp.dma_start(fg[:, :], final_g).then_inc(late_in, 16)
        with sp.Fori(0, DEPTH * PANELS // 2) as i:
            for s in range(2):
                sp.wait_ge(lo_done, 2 * i + s + 1)
                sp.dma_start(raw[:, s, :], weights.rearrange("w p n -> p w n")[:, bass.ds(2 * i + (s + 2), 1), :]) \
                    .then_inc(raw_in[s], 16)

    @block.gpsimd
    def _(pool):
        def plain():
            nc.gpsimd.sem_inc(carrier, 1)

        pool.dma_start(vs[:, 0:WINDOW - DEC_SEQ, :], vcache[:, DEC_SEQ:WINDOW, :]).then_inc(vs_out, 16)
        with pool.Fori(0, DEPTH) as l:
            for i in range(4):
                pool.wait_ge(x_in[i], 16)
            pool.wait_ge(d_out, l * ND + 2)
            plain()
            pool.dma_start(spill, X[:, :, :]).then_inc(x_spilled, 16)
            pool.dma_start(G[:, :, TP + CF_H:TP + 2 * CF_H], cfhist[bass.ds(l, 1), :, :, :]
                           .rearrange("l p t n -> (l p) t n")).then_inc(hist_in, 16)
            pool.wait_ge(nx_lo, l * 16 + 8)
            plain()
            pool.dma_start(KD[:, :, TP:TP + WINDOW], kcache[bass.ds(l, 1), :, :, :]
                           .rearrange("l p v n -> (l p) v n")).then_inc(cache_in, 16)
            pool.dma_start(VV[:, 7, 0, :], vcache[bass.ds(l, 1), :, :].rearrange("l p n -> (l p) n")).then_inc(cache_in, 16)
            nc.gpsimd.memset(view(O_QS, 1024), 0.0).then_inc(zero_qs, 1)
            pool.wait_ge(zero_qs, l + 1)
            plain()

            def stage(c, n):
                q0 = chunk_span(c)[0]
                for v in range(N_KV):
                    pool.wait_ge(s_done, l * 20 + n * 2 + v + 1)
                    plain()
                    dst = view(O_QS + 512 * v, 512).rearrange("p (i n) -> p i n", i=4)
                    if isinstance(q0, int):
                        src = X[:, 4 * v:4 * v + 4, q0:q0 + 64]
                    else:
                        src = X[:, 4 * v:4 * v + 4, bass.ds(q0, 64)]
                    nc.gpsimd.tensor_copy(dst[0:64, :, 0:64], src[0:64, :, :])
                    nc.gpsimd.tensor_copy(dst[64:128, :, 64:128], src[64:128, :, :]).then_inc(qs_done, 1)

            pool.wait_ge(qrot, l * KT + KT)
            plain()
            for c in range(3):
                stage(c, c)
            with pool.Fori(3, N_CHUNK) as c:
                stage(c, c)
            stage(CHUNKS - 1, CHUNKS - 1)
            pool.wait_ge(krot, l * 2 + 2)
            pool.wait_ge(cache_in, l * 32 + 32)
            plain()
            for v in range(N_KV):
                r = slice(64 * v, 64 * v + 64)
                pool.dma_start(kp[bass.ds(l, 1), r, :].rearrange("l p n -> (l p) n"),
                               KD[r, v, TP - WINDOW:TP]).then_inc(kv_out, 16)
                pool.dma_start(ks[bass.ds(l, 1), r, :].rearrange("l p n -> (l p) n"),
                               KD[r, v, TP + DEC_SEQ:TP + DEC_SEQ + WINDOW]).then_inc(kv_out, 16)
            pool.wait_ge(d_out, d_ready(l, D_V + 1))
            plain()
            pool.dma_start(vp[bass.ds(l, 1), 0:64, :].rearrange("l p n -> (l p) n"), VV[64:128, 6, 0, :]).then_inc(kv_out, 16)
            pool.dma_start(vp[bass.ds(l, 1), 64:128, :].rearrange("l p n -> (l p) n"), VV[0:64, 6, 1, :]).then_inc(kv_out, 16)
            pool.dma_start(vs[bass.ds(l, 1), WINDOW - DEC_SEQ:WINDOW, :].rearrange("l p n -> (l p) n"),
                           VV[0:64, 7, 1, :]).then_inc(kv_out, 16)
            pool.wait_ge(d_out, d_ready(l, D_CF + 7))
            plain()
            pool.dma_start(cfp[bass.ds(l, 1), :, :, 0, :].rearrange("l p t n -> (l p) t n"),
                           G[:, :, TP:TP + CF_H]).then_inc(tails_out, 16)
            pool.dma_start(cfp[bass.ds(l, 1), :, :, 1, :].rearrange("l p t n -> (l p) t n"),
                           G[:, :, CF_IN - CF_H:CF_IN]).then_inc(tails_out, 16)
            pool.wait_ge(sc_tail_done, l * KT + KT)
            plain()
            pool.dma_start(scp[bass.ds(l, 1), :, :].rearrange("l p n -> (l p) n"),
                           sct[:, :, :].rearrange("p t n -> p (t n)")).then_inc(small_out, 16)
            with pool.Fori(0, KT) as m:
                pool.wait_ge(mg_lo, l * KT + m + 1)
                pool.wait_ge(x_spilled, l * 16 + 16)
                plain()
                pool.dma_start(tile(X, m), spill[:, bass.ds(m, 1), :].rearrange("p t n -> p (t n)")).then_inc(x_back, 16)
                pool.wait_ge(x_back, l * (KT * 16) + m * 16 + 16)
            pool.wait_ge(ff_tail_done, l * (2 * FT) + (2 * FT + 2))
            plain()
            pool.dma_start(ffp[bass.ds(l, 1), :, :].rearrange("l p n -> (l p) n"),
                           fft[:, :, :].rearrange("p t n -> p (t n)")).then_inc(small_out, 16)
            pool.wait_ge(small_out, l * 32 + 32)
            plain()
        for m in range(KT):
            pool.wait_ge(yn_done, m + 1)
            pool.dma_start(y[:, m, :], X[:, m, :]).then_inc(y_out, 16)
        pool.wait_ge(y_out, 16 * KT)
        pool.wait_ge(vs_out, 16)
        pool.wait_ge(kv_out, DEPTH * 7 * 16)
        pool.wait_ge(tails_out, DEPTH * 32)

    @block.tensor
    def _(pe):
        def panel(w, s, out, nk, rh, rl, kwait=None):
            pe.wait_ge(lo_done, w + 1)
            for k in range(nk):
                if kwait:
                    pe.wait_ge(kwait[0], kwait[1] + k + 1)
                wk = slice(k * 128, k * 128 + 128)
                for j, (a, b) in enumerate(((wh, rh), (wh, rl), (wl, rh))):
                    for h in range(2):
                        last = nc.tensor.matmul(out[:, h, :], a[:, s, wk], b[:, k, h * HALF:(h + 1) * HALF],
                                                start=(k == 0 and j == 0), stop=(k == nk - 1 and j == 2))
            last.then_inc(panel_done, 1)

        def two_panels(w, outs, nk, r0, r1, free, kwait, last_late, middle=None):
            if last_late:
                order = [(p, k) for p in range(2) for k in range(nk - 3)]
            else:
                order = [(p, k) for k in range(nk - 3) for p in range(2)]
            order += [(p, k) for p in range(2) for k in range(nk - 3, nk)]
            for u, (p, k) in enumerate(order):
                if k == 0:
                    pe.wait_ge(*free[p])
                    pe.wait_ge(lo_done, w + p + 1)
                if p == 0:
                    pe.wait_ge(kwait[0], kwait[1] + k + 1)
                if u == 5 and middle:
                    middle()
                wk = slice(k * 128, k * 128 + 128)
                rh, rl = (r0, r1)[p]
                for j, (a, b) in enumerate(((wh, rh), (wh, rl), (wl, rh))):
                    for h in range(2):
                        last = nc.tensor.matmul(outs[p][:, h, :], a[:, p, wk], b[:, k, h * HALF:(h + 1) * HALF],
                                                start=(k == 0 and j == 0), stop=(k == nk - 1 and j == 2))
                if k == nk - 1:
                    last.then_inc(panel_done, 1)

        def channel_sum(l, a, n, ready):
            pe.wait_ge(a_out, a_free(l, a))
            pe.wait_ge(*ready)
            for h in range(2):
                last = nc.tensor.matmul(a_tile(a, n)[:, h, :], ones, view(O_SS, 622)[:, h * n:(h + 1) * n],
                                        start=True, stop=True)
            last.then_inc(sum_ps, 1)

        def squares_ready(l, q):
            return sq_sum, l * (NQ * 9) + (q * 9 + 10)

        def residual(l, w, d, nk, rh, rl, kwait):
            two_panels(l * PANELS + w, (d_tile(d), d_tile(d + 1)), nk, (rh, rl), (rh, rl),
                       [(d_out, d_free(l, d + j)) for j in range(2)], kwait, True)
            with pe.Fori(1, 4) as i:
                for j in range(2):
                    pe.wait_ge(d_out, l * ND + i * 2 + (d + j + 1))
                    panel(l * PANELS + i * 2 + (w + j), j, d_tile(d + j), nk, rh, rl)

        def first_pair(l, w, a, d, kwait, middle=None):
            two_panels(w, (a_tile(a), d_tile(d)), KT, (xh, xl), (xh, xl), ((a_out, a_free(l, a)), (d_out, d_free(l, d))),
                       kwait, False, middle)

        def pair(l, w, a, d, rg, ro, kwait=None, middle=None):
            pe.wait_ge(a_out, a_free(l, a[0]))
            panel(w, 0, a_tile(a[1]), KT, *rg)
            if middle:
                middle()
            pe.wait_ge(d_out, d_free(l, d[0]))
            panel(w + 1, 1, d_tile(d[1]), KT, *ro, kwait=kwait)

        def scores(l, c, n, v):
            k0, nk = chunk_span(c)[1:]
            it = l * 20 + n * 2 + v
            pe.wait_ge(qs_done, it + 1)
            pe.wait_ge(p_done, it + 1)
            for i in range(4):
                keys = KD[:, v, k0:k0 + nk] if isinstance(k0, int) else \
                    view(O_KD, 1440)[:, bass.ds(k0 + 720 * v, nk)]
                last = nc.tensor.matmul(PS[:, 2 * v + i // 2, 256 * (i % 2):256 * (i % 2) + nk],
                                        view(O_QS + 512 * v + 128 * i, 128), keys, start=True, stop=True)
            last.then_inc(s_done, 1)

        def turn(l, c, n, v):
            nk = chunk_span(c)[2]
            n1, n2 = min(nk, 128), max(nk - 128, 0)
            it = l * 20 + n * 2 + v
            pe.wait_ge(p_done, it + 3)
            pe.wait_ge(pt1_done, it + 1)
            if n2:
                pe.wait_ge(pt2_done, it2(l, n, v) + 1)
            for i in range(4):
                P = view(O_P + 768 * v + 192 * i, 192)
                last = nc.tensor.transpose(PS[0:n1, 4, 128 * i:128 * i + 128], P[:, 0:n1], ident)
                if n2:
                    last = nc.tensor.transpose(PS[0:n2, 5, 128 * i:128 * i + 128], P[:, 128:nk], ident)
            last.then_inc(t_done, 1)

        def values(l, c, n, v):
            nk = chunk_span(c)[2]
            n1, n2 = min(nk, 128), max(nk - 128, 0)
            vt = v_tile(c)
            it = l * 20 + n * 2 + v
            pe.wait_ge(pt1_done, it + 2)
            if n2:
                pe.wait_ge(pt2_done, it2(l, n, v) + 2)
            pe.wait_ge(on_done, it + 1)
            for i in range(4):
                for j, (nn, o) in enumerate(((n1, O_PT1), (n2, O_PT2))):
                    if nn:
                        if isinstance(vt, int):
                            vals = VV[0:nn, vt, j, 64 * v:64 * v + 64]
                        else:
                            vals = scr[0:nn, bass.ds(vt * 256 + (O_VV + 128 * j + 64 * v), 64)]
                        last = nc.tensor.matmul(PS[:, 6, 64 * i:64 * i + 64],
                                                scr[0:nn, o + 512 * v + 128 * i:o + 512 * v + 128 * i + 128], vals,
                                                start=(i == 0 and j == 0), stop=(j == (1 if n2 else 0)),
                                                skip_group_check=True)
            last.then_inc(o_done, 1)

        def turn_back(l, n, v):
            it = l * 20 + n * 2 + v
            pe.wait_ge(on_done, it + 2)
            pe.wait_ge(ol_done, it + 1)
            for j in range(2):
                last = nc.tensor.transpose(PS[:, 7, 128 * j:128 * j + 128], view(O_ON + 256 * v + 128 * j, 128), ident)
            last.then_inc(ot_done, 1)

        def attention(l, n):
            if has(n):
                scores(l, n, n, 0)
            if has(n - 2):
                values(l, n - 2, n - 2, 1)
            if has(n - 1):
                turn(l, n - 1, n - 1, 0)
            if has(n - 2):
                turn_back(l, n - 2, 0)
            if has(n):
                scores(l, n, n, 1)
            if has(n - 1):
                values(l, n - 1, n - 1, 0)
                turn(l, n - 1, n - 1, 1)
            if has(n - 2):
                turn_back(l, n - 2, 1)

        nc.tensor.sem_inc(s_done, 2)
        nc.tensor.sem_inc(t_done, 2)
        nc.tensor.sem_inc(o_done, 2)
        pe.wait_ge(inputs_in, 32)
        with pe.Fori(0, DEPTH) as l:
            W = l * PANELS
            channel_sum(l, A_N1, HALF, squares_ready(l, Q_N1))

            def glu(i, j):
                pair(l, W + i * 4 + (P_CF + 2 * j), (i * 2 + (A_CF + j), A_CF + j), (i * 2 + (D_CF + j), D_CF + j),
                     (xh, xl), (xh, xl))
            first_pair(l, W + P_CF, A_CF, D_CF, (nx_lo, l * 16))
            glu(0, 1)
            with pe.Fori(1, 4) as i:
                glu(i, 0)
                glu(i, 1)
            def rotate(i, j):
                pe.wait_ge(a_out, l * NA + i * 2 + (A_Q + j + 3))
                pe.wait_ge(d_out, l * ND + i * 2 + (D_Q + j + 1))
                for h in range(2):
                    last = nc.tensor.matmul(d_tile(D_Q + j)[:, h, :], con[:, CON["rot"]:CON["rot"] + 128],
                                            slot(O_QR, TOK, j)[:, h * HALF:(h + 1) * HALF], start=True, stop=True)
                last.then_inc(qrot_ps, 1)

            def queries(i):
                for j in range(2):
                    pe.wait_ge(a_out, l * NA + i * 2 + (A_Q + j + 1))
                    panel(W + i * 2 + (P_Q + j), j, a_tile(A_Q + j), KT, xh, xl)
                    if j:
                        rotate(i, 0)
                    elif not isinstance(i, int):
                        rotate(i - 1, 1)
            queries(0)
            with pe.Fori(1, 4) as i:
                queries(i)
            pe.wait_ge(a_out, a_free(l, A_K))
            panel(W + P_K, 0, a_tile(A_K), KT, xh, xl)
            rotate(3, 1)
            pe.wait_ge(a_out, a_free(l, A_V))
            panel(W + P_V, 1, a_tile(A_V), KT, xh, xl)
            pe.wait_ge(a_out, a_ready(l, A_K))
            for j, name in enumerate(("ka", "kar", "kb", "kbr")):
                pe.wait_ge(d_out, d_free(l, D_K + j))
                for h in range(2):
                    last = nc.tensor.matmul(d_tile(D_K + j)[:, h, :], con[:, CON[name]:CON[name] + 128],
                                            slot(O_QR, TOK, 0)[:, h * HALF:(h + 1) * HALF], start=True, stop=True)
                last.then_inc(krot_ps, 1)
            pe.wait_ge(a_out, a_ready(l, A_V))
            for j in range(2):
                pe.wait_ge(d_out, d_free(l, D_V + j))
                nc.tensor.sem_inc(carrier, 1)
                for b, (t0, n) in enumerate(v_blocks(j)):
                    last = nc.tensor.transpose(PS[0:n, 4 + 2 * ((D_V + j) % 2) + b // 4, 128 * (b % 4):128 * (b % 4) + 128],
                                               slot(O_QR, TOK, 1)[:, t0:t0 + n], ident)
                last.then_inc(vt_ps, 1)
            pe.wait_ge(a_out, a_ready(l, A_V))
            pe.wait_ge(d_out, d_ready(l, D_V + 1))
            pe.wait_ge(cache_in, l * 32 + 32)
            pe.wait_ge(krot, l * 2 + 2)
            for n in range(5):
                attention(l, n)
            with pe.Fori(5, N_CHUNK) as n:
                attention(l, n)
            for n in range(N_CHUNK, CHUNKS + 2):
                attention(l, n)
            pe.wait_ge(ol_done, l * 20 + 21)
            nc.tensor.sem_inc(carrier, 1)
            with pe.Fori(0, 4) as i:
                for j in range(2):
                    pair(l, W + i * 4 + (P_OA + 2 * j), (i * 2 + (A_OA + j), A_OA + j), (i * 2 + (D_OA + j), D_OA + j),
                         (xh, xl), (bh, bl))
            with pe.Fori(0, 4) as i:
                for j in range(2):
                    w = W + i * 6 + (P_SC + 3 * j)
                    pe.wait_ge(a_out, l * NA + i * 2 + (A_SC + j + 1))
                    panel(w, j % 2, a_tile(A_SC + j), KT, xh, xl)
                    for e in range(2):
                        pe.wait_ge(d_out, l * ND + i * 4 + (D_SC + 2 * j + e + 1))
                        panel(w + (1 + e), (j + 1 + e) % 2, d_tile(D_SC + 2 * j + e), KT, xh, xl)

            def mean():
                channel_sum(l, A_MEAN, 311, (mean_sum, l * 7 + 7))

            def variance():
                channel_sum(l, A_VAR, 311, squares_ready(l, Q_VAR))
            for m in range(KT):
                pair(l, W + (P_OS + 2 * m), (a_gate_sc(m), a_gate_sc(m)), (D_OS + m, D_OS + m), (xh, xl), (bh, bl),
                     kwait=(sc_lo, l * KT) if m == 0 else None, middle={1: mean, 4: variance}.get(m))
            with pe.Fori(0, 4) as i:
                for j in range(2):
                    pe.wait_ge(a_out, l * NA + i * 2 + (A_OC + j + 1))
                    panel(W + i * 4 + (P_OC + 2 * j), 0, a_tile(A_OC + j), KT, xh, xl)
                    pe.wait_ge(d_out, l * ND + i * 2 + (D_OC + j + 1))
                    panel(W + i * 4 + (P_OC + 2 * j + 1), 1, d_tile(D_OC + j), KT, bh, bl,
                          kwait=(cf_lo, l * KT) if j == 0 else None)
            residual(l, P_WO, D_WO, KT, mh, ml, (mg_lo, l * KT))
            for t0, n, p0, a0, d0 in thirds:
                def up(i, j):
                    pair(l, W + i * 4 + (p0 + 2 * j), (i * 2 + (a0 + j), a0 + j), (i * 2 + (d0 + j), d0 + j),
                         (xh, xl), (xh, xl))

                def mean_square():
                    channel_sum(l, A_N2, HALF, squares_ready(l, Q_N2))
                if t0 == 0:
                    first_pair(l, W + p0, a0, d0, (nx_lo, l * 16 + 8), mean_square)
                    up(0, 1)
                with pe.Fori(1 if t0 == 0 else 0, n // 2) as i:
                    up(i, 0)
                    up(i, 1)
                residual(l, p0 + 2 * n, d0 + n, n, bh, bl, (ff_lo, l * FT + t0))
        channel_sum(DEPTH, A_N1, HALF, squares_ready(DEPTH, Q_N1))

    @block.scalar
    def _(act):
        def step(wbase, off, s):
            act.wait_ge(panel_done, wbase + (off + 1))
            act.wait_ge(raw_in[s], wbase * 8 + ((off - s) // 2 + 2) * 16)
            nc.scalar.activation(wh[:, s, :], raw[:, s, :], ACT.Copy).then_inc(hi_done, 1)

        def square(l, q, m, s, src, n):
            act.wait_ge(sq_sum, l * (NQ * 9) + (q * 9 + 1) + m)
            nc.scalar.activation(slot(O_SQ, 622, s)[:, 0:n], src, ACT.Square).then_inc(sq_done, 1)

        def residual(l, w, d, squares=None, g=None):
            with act.Fori(0, 4) as i:
                for j in range(2):
                    step(l * PANELS + i * 2, w + j, j)
                    if squares is not None:
                        act.wait_ge(d_out, l * ND + i * 2 + (d + j + 3))
                        square(*squares, i * 2 + j, j, tile(X, i * 2 + j), TOK)
                    if g:
                        nc.scalar.activation(tile(xh, i * 2 + j), tile(X, i * 2 + j), ACT.Identity, bias=0.0,
                                             scale=col(l, g, i * 2 + j)).then_inc(nx_hi, 1)

        def root(l, s, a, n, at):
            act.wait_ge(sum_ps, l * NS + (s + 1))
            nc.scalar.activation(halves(view(at, 2 * n)), a_tile(a, n), ACT.Sqrt, bias=eps, scale=1.0 / D_MODEL) \
                .then_inc(a_out, 1)

        def gate(a, j, b, used):
            act.wait_ge(d_out, used)
            nc.scalar.activation(halves(slot(O_SG, TOK, j)), a_tile(a), ACT.Sigmoid, bias=b).then_inc(a_out, 1)

        nc.scalar.sem_inc(a_out, 2)
        nc.scalar.sem_inc(p_done, 2)
        nc.scalar.sem_inc(pt1_done, 1)
        for m in range(KT):
            act.wait_ge(x_in[m // 2], 16)
            square(0, Q_N1, m, m % 2, X[:, m, :], TOK)
        act.wait_ge(raw_in[0], 16)
        nc.scalar.activation(wh[:, 0, :], raw[:, 0, :], ACT.Copy).then_inc(hi_done, 1)
        act.wait_ge(raw_in[1], 16)
        nc.scalar.activation(wh[:, 1, :], raw[:, 1, :], ACT.Copy).then_inc(hi_done, 1)
        act.wait_ge(inputs_in, 32)
        with act.Fori(0, DEPTH) as l:
            W = l * PANELS
            root(l, S_N1, A_N1, HALF, O_RT)
            for m in range(KT):
                act.wait_ge(nx_mul, l * KT + (m + 1))
                nc.scalar.activation(xh[:, m, :], slot(O_NT, TOK, m % 3), ACT.Identity, bias=0.0, scale=col(l, "g1", m)) \
                    .then_inc(nx_hi, 1)
            with act.Fori(0, 4) as i:
                for j in range(2):
                    step(W + i * 4, P_CF + 2 * j, 0)
                    gate(A_CF + j, j, 0.0, l * ND + i * 2 + (D_CF + j + 1))
                    step(W + i * 4, P_CF + 2 * j + 1, 1)
            with act.Fori(0, 4) as i:
                for j in range(2):
                    step(W + i * 2, P_Q + j, j)
                    act.wait_ge(d_out, l * ND + i * 2 + (D_Q + j + 1))
                    nc.scalar.activation(halves(slot(O_QR, TOK, j)), a_tile(A_Q + j), ACT.Copy).then_inc(a_out, 1)
            step(W, P_K, 0)
            act.wait_ge(qrot, l * KT + KT)
            nc.scalar.activation(halves(slot(O_QR, TOK, 0)), a_tile(A_K), ACT.Copy).then_inc(a_out, 1)
            step(W, P_V, 1)
            nc.scalar.activation(halves(slot(O_QR, TOK, 1)), a_tile(A_V), ACT.Copy).then_inc(a_out, 1)

            def exps(n, v):
                nk = chunk_span(n)[2]
                it = l * 20 + n * 2 + v
                act.wait_ge(nm_done, 2 * it + 2)
                act.wait_ge(rinv_done, it + 1)
                nc.scalar.activation(es[:, v, :], ds_[:, v, :], ACT.Exp).then_inc(es_done, 1)
                act.wait_ge(t_done, it + 1)
                for i in range(4):
                    last = nc.scalar.activation(view(O_P + 768 * v + 192 * i, nk),
                                                PS[:, 2 * v + i // 2, 256 * (i % 2):256 * (i % 2) + nk], ACT.Exp,
                                                bias=nm[:, v, i:i + 1], scale=SCALE, accum_out=sums[:, v, i:i + 1])
                last.then_inc(p_done, 1)

            def copy_first(n, v):
                n1 = min(chunk_span(n)[2], 128)
                it = l * 20 + n * 2 + v
                act.wait_ge(t_done, it + 3)
                act.wait_ge(o_done, it + 1)
                nc.scalar.activation(scr[0:n1, O_PT1 + 512 * v:O_PT1 + 512 * v + 512], PS[0:n1, 4, :], ACT.Copy) \
                    .then_inc(pt1_done, 1)

            def outputs_hi(n, v):
                q0 = chunk_span(n)[0]
                act.wait_ge(ot_done, l * 20 + n * 2 + v + 1)
                src = PS[:, 7, 0:256].rearrange("p (t n) -> p t n", n=64)
                dst = bh[:, 4 * v:4 * v + 4, q0:q0 + 64] if isinstance(q0, int) else bh[:, 4 * v:4 * v + 4, bass.ds(q0, 64)]
                nc.scalar.activation(dst, src, ACT.Copy).then_inc(oh_done, 1)

            def attention(n):
                for v in range(N_KV):
                    if has(n - 1):
                        copy_first(n - 1, v)
                    if has(n - 2) and v == 0:
                        outputs_hi(n - 2, v)
                    if has(n):
                        exps(n, v)
                    if has(n - 2) and v == 1:
                        outputs_hi(n - 2, v)

            for n in range(5):
                attention(n)
            with act.Fori(5, N_CHUNK) as n:
                attention(n)
            for n in range(N_CHUNK, CHUNKS + 2):
                attention(n)
            with act.Fori(0, 4) as i:
                for j in range(2):
                    step(W + i * 4, P_OA + 2 * j, 0)
                    gate(A_OA + j, j, col(l, "bg", i * 2 + j), l * ND + i * 2 + (D_OA + j + 1))
                    step(W + i * 4, P_OA + 2 * j + 1, 1)
            act.wait_ge(kv_out, l * 112 + 112)
            with act.Fori(0, 4) as i:
                for j in range(2):
                    step(W + i * 6, P_SC + 3 * j, j)
                    act.wait_ge(d_out, l * ND + i * 4 + (D_SC + 2 * j))
                    nc.scalar.activation(halves(slot(O_CT, TOK, j)), a_tile(A_SC + j), ACT.Copy).then_inc(a_out, 1)
                    step(W + i * 6, P_SC + 3 * j + 1, 1 - j)
                    step(W + i * 6, P_SC + 3 * j + 2, j)
                    act.wait_ge(d_out, l * ND + i * 4 + (D_SC + 2 * j + 1 + 3))
                    nc.scalar.activation(tile(bh, i * 2 + j), slot(O_BT, TOK, j), ACT.Copy).then_inc(sc_hi, 1)

            def mean(m):
                act.wait_ge(sum_ps, l * NS + (S_MEAN + 1))
                nc.scalar.activation(halves(view(O_MU, 622)), a_tile(A_MEAN, 311), ACT.Copy, scale=1.0 / D_MODEL) \
                    .then_inc(a_out, 1)

            def ln_square(m):
                act.wait_ge(ln_sub, l * KT + m + 1)
                square(l, Q_VAR, m, m % 2, acc[:, m, :], CF_OUT)

            def ln_root(m):
                root(l, S_VAR, A_VAR, 311, O_RT)

            def silu(m):
                act.wait_ge(ln_mul, l * KT + m + 1)
                nc.scalar.activation(acc[:, m, :], acc[:, m, :], ACT.Silu, bias=col(l, "lnb", m), scale=col(l, "lng", m)) \
                    .then_inc(ln_silu, 1)

            def branch_hi(m):
                act.wait_ge(ln_silu, l * KT + m + 1)
                nc.scalar.activation(bh[:, m, 0:TP], acc[:, m, 0:TP], ACT.Copy)
                nc.scalar.activation(bh[:, m, TP:TOK], acc[:, m, TP + CF_H:CF_OUT], ACT.Copy).then_inc(cf_hi, 1)

            plan = {2: (mean, (0,)), 4: (ln_square, (0, 1)), 5: (ln_square, (2, 3, 4)), 6: (ln_square, (5, 6, 7)),
                    8: (ln_root, (0,)), 11: (silu, (0, 1)), 12: (silu, (2, 3)), 13: (silu, (4, 5, 6, 7)),
                    15: (branch_hi, (0, 1, 2, 3, 4, 5, 6, 7))}
            for p in range(2 * KT):
                m = p // 2
                if p % 2 == 0:
                    step(W, P_OS + p, 0)
                    gate(a_gate_sc(m), m % 2, col(l, "bg", KT + m), d_free(l, D_OS + m))
                else:
                    step(W, P_OS + p, 1)
                work, tiles = plan.get(p, (None, ()))
                for t in tiles:
                    work(t)
            with act.Fori(0, 4) as i:
                for j in range(2):
                    step(W + i * 4, P_OC + 2 * j, 0)
                    gate(A_OC + j, j, col(l, "bg", i * 2 + (2 * KT + j)), l * ND + i * 2 + (D_OC + j + 1))
                    step(W + i * 4, P_OC + 2 * j + 1, 1)
                    act.wait_ge(mg_done, l * 16 + i * 2 + (8 + j + 1))
                    act.wait_ge(tails_out, l * 32 + 32)
                    nc.scalar.activation(tile(mh, i * 2 + j), tile(X, i * 2 + j), ACT.Copy).then_inc(mg_hi, 1)
            residual(l, P_WO, D_WO, (l, Q_N2), "g2")
            root(l, S_N2, A_N2, HALF, O_RF)
            act.wait_ge(ff_zero, l * 4 + 4)
            for t0, n, p0, a0, d0 in thirds:
                def product_hi(m, j):
                    act.wait_ge(ff_prod, l * FT + m + (t0 + 1))
                    src = slot(O_PB, S_OUT, j)
                    nc.scalar.activation(tile(bh, m, 0, TP), src[:, 0:TP], ACT.Copy)
                    nc.scalar.activation(tile(bh, m, TP, DEC_SEQ), src[:, TP + S_H:S_OUT], ACT.Copy).then_inc(ff_hi, 1)

                def tap_and_tail(m, src, dst):
                    nc.scalar.activation(dst, src[:, 0:S_OUT], ACT.Identity, bias=0.0, scale=col(l, "ffw", m * 3)) \
                        .then_inc(ff_first, 1)
                    nc.scalar.activation(tile(fft, m, 0, S_H), src[:, TP:TP + S_H], ACT.Copy)
                    nc.scalar.activation(tile(fft, m, S_H, S_H), src[:, S_IN - S_H:S_IN], ACT.Copy).then_inc(ff_tail_done, 1)

                def conv_product(i):
                    for j in range(2):
                        m = i * 2 + (t0 + j)
                        hg, hu = slot(O_HG, S_IN, j), slot(O_HU, S_IN, j)
                        gc, uc = slot(O_GC, S_OUT, j), slot(O_UC, S_OUT, j)
                        step(W + i * 4, p0 + 2 * j, 0)
                        if j or not isinstance(i, int):
                            product_hi(i * 2 + (j - 1), 1 - j)
                        act.wait_ge(ff_tap, l * (FT * 4) + i * 8 + (t0 * 4 + 4 * j + 4))
                        nc.scalar.activation(hg[:, TP + S_H:TP + 2 * S_H], col(l, "ffh", m * 2, 2), ACT.Copy).then_inc(ff_hist, 1)
                        nc.scalar.activation(hu[:, TP + S_H:TP + 2 * S_H], col(l, "ffh", m * 2 + 2 * FT, 2), ACT.Copy) \
                            .then_inc(ff_hist, 1)
                        act.wait_ge(ff_hist, l * (2 * FT) + i * 4 + (2 * t0 + 2 * j + 2))
                        act.wait_ge(a_out, l * NA + i * 2 + (a0 + j + 3))
                        tap_and_tail(m, hg, gc)
                        step(W + i * 4, p0 + 2 * j + 1, 1)
                        act.wait_ge(d_out, l * ND + i * 2 + (d0 + j + 3))
                        tap_and_tail(m + FT, hu, uc)
                        act.wait_ge(ff_tap, l * (FT * 4) + i * 8 + (t0 * 4 + 4 * j + 2 + 8))
                        nc.scalar.activation(gc, gc, ACT.Silu).then_inc(ff_silu, 1)
                conv_product(0)
                with act.Fori(1, n // 2) as i:
                    conv_product(i)
                product_hi(n - 1, 1)
                residual(l, p0 + 2 * n, d0 + n, (l + 1, Q_N1) if t0 + n == FT else None)
        root(DEPTH, S_N1, A_N1, HALF, O_RT)

    @block.vector
    def _(dve):
        V = nc.vector

        def low(s):
            return V.tensor_tensor(wl[:, s, :], raw[:, s, :], f(wh[:, s, :]), ALU.subtract).then_inc(lo_done, 1)

        def step(wbase, off, s):
            dve.wait_ge(panel_done, wbase + (off + 1))
            dve.wait_ge(hi_done, wbase + (off + 3))
            low(s)

        def zero_sum(n):
            V.memset(view(O_SS, n), 0.0).then_inc(sq_sum, 1)

        def add_square(l, q, m, s, n):
            dve.wait_ge(sq_done, l * (NQ * 8) + (q * 8 + 1) + m)
            dve.wait_ge(sq_sum, l * (NQ * 9) + (q * 9 + 2) + m)
            V.tensor_tensor(view(O_SS, n), view(O_SS, n), slot(O_SQ, 622, s)[:, 0:n], ALU.add).then_inc(sq_sum, 1)

        def rsqrt(a_at, n, at, count):
            dve.wait_ge(a_out, a_at)
            V.reciprocal(view(at, 2 * n), view(at, 2 * n)).then_inc(rs_done, 1)
            dve.wait_ge(rs_done, count)

        def norm(l, a, nxb, g, count):
            rsqrt(a_ready(l, a), HALF, O_RT, count)

            def lo(m):
                dve.wait_ge(nx_hi, nxb + m + 1)
                V.scalar_tensor_tensor(xl[:, m, :], slot(O_NT, TOK, m % 3), col(l, g, m), f(xh[:, m, :]), ALU.mult,
                                       ALU.subtract).then_inc(nx_lo, 1)
            for m in range(KT):
                if m >= 3:
                    dve.wait_ge(nx_lo, nxb + m - 2)
                V.tensor_tensor(slot(O_NT, TOK, m % 3), X[:, m, :], view(O_RT, TOK), ALU.mult).then_inc(nx_mul, 1)
                if m:
                    lo(m - 1)
            lo(KT - 1)

        def first_taps(l, m, k0, k1):
            for k in range(k0, k1):
                src = tile(G, m, k, CF_OUT)
                if k == 0:
                    V.tensor_scalar(tile(acc, m), src, col(l, "cfw", m * CF_K), None, ALU.mult).then_inc(tap_glu, 1)
                else:
                    dve.wait_ge(tap_glu, l * (KT * TAPS_GLU) + m * TAPS_GLU + k)
                    V.scalar_tensor_tensor(tile(acc, m), src, col(l, "cfw", m * CF_K + k), tile(acc, m), ALU.mult,
                                           ALU.add).then_inc(tap_glu, 1)

        def taps(l, k, *groups):
            for g in groups:
                if isinstance(k, int) and k == TAPS_GLU:
                    dve.wait_ge(tap_glu, l * (KT * TAPS_GLU) + KT * TAPS_GLU)
                for t in range(2):
                    if not (isinstance(k, int) and k == TAPS_GLU):
                        dve.wait_ge(tap_rest[g], l * (2 * (CF_K - TAPS_GLU)) + k * 2 + (t - 2 * TAPS_GLU - 1))
                    a = acc[:, 2 * g + t, :]
                    V.scalar_tensor_tensor(a, tile(G, 2 * g + t, k, CF_OUT), col(l, "cfw", k + (2 * g + t) * CF_K), a,
                                           ALU.mult, ALU.add).then_inc(tap_rest[g], 1)

        def conv3(l, src, dst, name, t, sem_, base):
            V.tensor_scalar(dst, src[:, 0:S_OUT], col(l, name, t * 3), None, ALU.mult).then_inc(sem_, 1)
            for k in (1, 2):
                dve.wait_ge(sem_, base + k)
                V.scalar_tensor_tensor(dst, src[:, k:k + S_OUT], col(l, name, t * 3 + k), dst, ALU.mult, ALU.add) \
                    .then_inc(sem_, 1)

        def keep_tail(t, m, src, sem_):
            V.tensor_copy(tile(t, m, 0, S_H), src[:, TP:TP + S_H])
            V.tensor_copy(tile(t, m, S_H, S_H), src[:, S_IN - S_H:S_IN]).then_inc(sem_, 1)

        V.sem_inc(d_out, 2)
        V.sem_inc(pt2_done, 1)
        V.sem_inc(on_done, 1)
        V.sem_inc(ol_done, 1)
        V.sem_inc(rinv_done, 2)
        V.sem_inc(ff_tap, 8)
        V.sem_inc(ff_tail_done, 2)
        V.sem_inc(sq_sum, 1)
        zero_sum(TOK)
        for m in range(KT):
            add_square(0, Q_N1, m, m % 2, TOK)
        for s in range(2):
            dve.wait_ge(hi_done, s + 1)
            low(s)
        dve.wait_ge(inputs_in, 32)
        for l_ in range(DEPTH):
            V.tensor_scalar(nsink[:, 8 * l_:8 * l_ + 8], col(l_, "sink", 0, 8), -1.0, None, ALU.mult).then_inc(nsink_done, 1)
        dve.wait_ge(nsink_done, DEPTH)
        with dve.Fori(0, DEPTH) as l:
            W = l * PANELS
            V.memset(G[:, :, 0:CF_H], 0.0).then_inc(g_zero, 1)
            norm(l, A_N1, l * 16, "g1", l * 3 + 1)
            dve.wait_ge(g_zero, l + 1)
            dve.wait_ge(hist_in, l * 16 + 16)

            def glu(i):
                for j in range(2):
                    m = i * 2 + j
                    step(W + i * 4, P_CF + 2 * j, 0)
                    if j or not isinstance(i, int):
                        first_taps(l, i * 2 + (j - 1), TAPS_GLU // 2, TAPS_GLU)
                    step(W + i * 4, P_CF + 2 * j + 1, 1)
                    dve.wait_ge(a_out, l * NA + i * 2 + (A_CF + j + 3))
                    for piece in PIECES:
                        last = V.tensor_tensor(tile(G, m, after(piece[3], CF_H), piece[2]),
                                               slot(O_SG, TOK, j)[:, piece[3]:piece[3] + piece[2]],
                                               d_piece(D_CF + j, piece), ALU.mult)
                    last.then_inc(d_out, 1)
                    dve.wait_ge(d_out, l * ND + i * 2 + (D_CF + j + 3))
                    first_taps(l, m, 0, TAPS_GLU // 2)
            glu(0)
            with dve.Fori(1, 4) as i:
                glu(i)
            dve.wait_ge(x_spilled, l * 16 + 16)
            dve.wait_ge(late_in, 32)

            def queries(i):
                for j in range(2):
                    step(W + i * 2, P_Q + j, j)
                    if j == 0 and isinstance(i, int):
                        first_taps(l, KT - 1, TAPS_GLU // 2, TAPS_GLU)
                    if j:
                        taps(l, i + TAPS_GLU, 0, 1, 2)
                for j in range(2):
                    dve.wait_ge(a_out, l * NA + i * 2 + (A_Q + j + 3))
                    V.tensor_tensor(tile(X, i * 2 + j), slot(O_QR, TOK, j), cos, ALU.mult).then_inc(qtmp, 1)
                    dve.wait_ge(qrot_ps, l * KT + i * 2 + (j + 1))
                    V.tensor_tensor(halves(slot(O_TQ, TOK, j)), halves(sin), d_tile(D_Q + j), ALU.mult).then_inc(d_out, 1)
                    dve.wait_ge(d_out, l * ND + i * 2 + (D_Q + j + 3))
                    V.tensor_tensor(tile(X, i * 2 + j), tile(X, i * 2 + j), slot(O_TQ, TOK, j), ALU.add).then_inc(qrot, 1)
            queries(0)
            with dve.Fori(1, 4) as i:
                queries(i)
            step(W, P_K, 0)
            taps(l, TAPS_GLU + 4, 0, 1)
            step(W, P_V, 1)
            for v in range(N_KV):
                for j in range(2):
                    dve.wait_ge(krot_ps, l * 4 + 2 * v + j + 1)
                    V.tensor_tensor(halves(slot(O_TQ, TOK, j)), halves((cos, sin)[j]), d_tile(D_K + 2 * v + j), ALU.mult) \
                        .then_inc(d_out, 1)
                dve.wait_ge(d_out, d_ready(l, D_K + 2 * v + 1))
                V.tensor_tensor(KD[:, v, 0:TP], slot(O_TQ, TOK, 0)[:, 0:TP], slot(O_TQ, TOK, 1)[:, 0:TP], ALU.add)
                V.tensor_tensor(KD[:, v, TP + WINDOW:720], slot(O_TQ, TOK, 0)[:, TP:TOK], slot(O_TQ, TOK, 1)[:, TP:TOK],
                                ALU.add).then_inc(krot, 1)
                dve.wait_ge(krot, l * 2 + v + 1)
            for j in range(2):
                dve.wait_ge(vt_ps, l * 2 + j + 1)
                b0 = 4 + 2 * ((D_V + j) % 2)
                groups = (((0, 0, 4, 128, 0), (1, 0, 3, 128, 4)), ((0, 0, 4, 64, 1), (1, 0, 3, 64, 5), (1, 3, 1, 16, 0)))[j]
                for b, c0, n, rows, v0 in groups:
                    last = V.tensor_copy(VV[0:rows, v0:v0 + n, j, :],
                                         PS[0:rows, b0 + b, 128 * c0:128 * (c0 + n)].rearrange("p (t n) -> p t n", n=128))
                last.then_inc(d_out, 1)
            dve.wait_ge(d_out, d_ready(l, D_V + 1))

            def maxima(n, v):
                nk = chunk_span(n)[2]
                it = l * 20 + n * 2 + v
                dve.wait_ge(s_done, it + 3)
                sc = PS[:, 2 * v:2 * v + 2, :].rearrange("p b (i n) -> p (b i) n", i=2)[:, :, 0:nk]
                V.tensor_reduce(mx[:, v, :], sc, AX.X, ALU.max).then_inc(mx_done, 1)
                dve.wait_ge(mx_done, it + 1)
                dve.wait_ge(p_done, it + 1)
                ns = nsink[:, bass.ds(l * 8 + 4 * v, 4)]
                V.scalar_tensor_tensor(nm[:, v, :], mx[:, v, :], -SCALE, ns, ALU.mult, ALU.min).then_inc(nm_done, 1)
                dve.wait_ge(nm_done, 2 * it + 1)
                V.tensor_tensor(ds_[:, v, :], nm[:, v, :], ns, ALU.subtract).then_inc(nm_done, 1)

            def copy_rest(n, v):
                n2 = max(chunk_span(n)[2] - 128, 0)
                it = l * 20 + n * 2 + v
                if n2:
                    dve.wait_ge(t_done, it + 3)
                    dve.wait_ge(o_done, it + 1)
                    V.tensor_copy(scr[0:n2, O_PT2 + 512 * v:O_PT2 + 512 * v + 512], PS[0:n2, 5, :]).then_inc(pt2_done, 1)

            def denominators(n, v):
                it = l * 20 + n * 2 + v
                dve.wait_ge(p_done, it + 3)
                V.tensor_tensor(sums[:, v, :], sums[:, v, :], es[:, v, :], ALU.add).then_inc(den_done, 1)
                dve.wait_ge(den_done, it + 1)
                V.reciprocal(rinv[:, v, :], sums[:, v, :]).then_inc(rinv_done, 1)

            def norm_outputs(n, v):
                it = l * 20 + n * 2 + v
                dve.wait_ge(rinv_done, it + 3)
                dve.wait_ge(o_done, it + 3)
                V.tensor_tensor(view(O_ON + 256 * v, 256).rearrange("p (i n) -> p i n", i=4),
                                PS[:, 6, 0:256].rearrange("p (i n) -> p i n", i=4),
                                rinv[:, v, :].rearrange("p (i o) -> p i o", o=1).to_broadcast([128, 4, 64]),
                                ALU.mult).then_inc(on_done, 1)

            def outputs_lo(n, v):
                q0 = chunk_span(n)[0]
                dve.wait_ge(oh_done, l * 20 + n * 2 + v + 1)
                src = PS[:, 7, 0:256].rearrange("p (t n) -> p t n", n=64)
                at = slice(q0, q0 + 64) if isinstance(q0, int) else bass.ds(q0, 64)
                V.tensor_tensor(bl[:, 4 * v:4 * v + 4, at], src, f(bh[:, 4 * v:4 * v + 4, at]), ALU.subtract) \
                    .then_inc(ol_done, 1)

            def attention_taps(n, late):
                k = TAPS_GLU
                static = (((k + 4, 2), (k, 3)), ((k + 5, 0), (k + 5, 1)), ((k + 6, 0), (k + 6, 1)), ((k + 5, 2), (k + 6, 2)),
                          ((k + 1, 3), None))
                if isinstance(n, int) and n < len(static):
                    if static[n][late]:
                        taps(l, *static[n][late])
                elif has(n) and not late:
                    taps(l, n + (k - 3), 3)

            def attention(n):
                if has(n - 1):
                    denominators(n - 1, 0)
                if has(n):
                    maxima(n, 0)
                if has(n - 2):
                    norm_outputs(n - 2, 1)
                if has(n - 1):
                    copy_rest(n - 1, 0)
                attention_taps(n, False)
                if has(n - 2):
                    outputs_lo(n - 2, 0)
                if has(n - 1):
                    denominators(n - 1, 1)
                if has(n):
                    maxima(n, 1)
                if has(n - 1):
                    norm_outputs(n - 1, 0)
                    copy_rest(n - 1, 1)
                attention_taps(n, True)
                if has(n - 2):
                    outputs_lo(n - 2, 1)

            for n in range(5):
                attention(n)
            with dve.Fori(5, N_CHUNK) as n:
                attention(n)
            for n in range(N_CHUNK, CHUNKS + 2):
                attention(n)
            with dve.Fori(0, 4) as i:
                for j in range(2):
                    step(W + i * 4, P_OA + 2 * j, 0)
                    taps(l, i * 2 + (15 + j), 0, 1)
                    step(W + i * 4, P_OA + 2 * j + 1, 1)
                    dve.wait_ge(a_out, l * NA + i * 2 + (A_OA + j + 3))
                    V.tensor_tensor(halves(tile(X, i * 2 + j)), halves(slot(O_SG, TOK, j)), d_tile(D_OA + j),
                                    ALU.mult).then_inc(d_out, 1)
                    taps(l, i * 2 + (15 + j), 2, 3)
            dve.wait_ge(kv_out, l * 112 + 112)
            for j in range(2):
                V.memset(slot(O_CH, S_IN, j)[:, 0:S_H], 0.0).then_inc(sc_hist, 1)
            with dve.Fori(0, 4) as i:
                for j in range(2):
                    m = i * 2 + j
                    step(W + i * 6, P_SC + 3 * j, j)
                    ch, cv = slot(O_CH, S_IN, j), slot(O_CV, S_OUT, j)
                    V.tensor_copy(ch[:, TP + S_H:TP + 2 * S_H], col(l, "sch", m * 2, 2)).then_inc(sc_hist, 1)
                    taps(l, i * 2 + (23 + j), 0, 1)
                    step(W + i * 6, P_SC + 3 * j + 1, 1 - j)
                    dve.wait_ge(a_out, l * NA + i * 2 + (A_SC + j + 3))
                    for piece in PIECES:
                        o = after(piece[3], S_H)
                        last = V.tensor_tensor(ch[:, o:o + piece[2]], slot(O_CT, TOK, j)[:, piece[3]:piece[3] + piece[2]],
                                               d_piece(D_SC + 2 * j, piece), ALU.mult)
                    last.then_inc(d_out, 1)
                    dve.wait_ge(d_out, l * ND + i * 4 + (D_SC + 2 * j + 3))
                    keep_tail(sct, m, ch, sc_tail_done)
                    conv3(l, ch, cv, "scw", m, sc_tap, l * 24 + i * 6 + 3 * j)
                    step(W + i * 6, P_SC + 3 * j + 2, j)
                    dve.wait_ge(sc_tap, l * 24 + i * 6 + (3 * j + 3))
                    bt = slot(O_BT, TOK, j)
                    for piece in PIECES:
                        o = piece[3] + (S_H if piece[3] >= TP else 0)
                        last = V.tensor_tensor(bt[:, piece[3]:piece[3] + piece[2]], cv[:, o:o + piece[2]],
                                               d_piece(D_SC + 2 * j + 1, piece), ALU.mult)
                    last.then_inc(d_out, 1)
                    taps(l, i * 2 + (23 + j), 2, 3)
                    dve.wait_ge(sc_hi, l * KT + i * 2 + (j + 1))
                    V.tensor_tensor(tile(bl, m), bt, f(tile(bh, m)), ALU.subtract).then_inc(sc_lo, 1)

            def merge(m, j, d, ready):
                V.tensor_tensor(halves(slot(O_TQ, TOK, j)), halves(slot(O_SG, TOK, j)), d_tile(d), ALU.mult) \
                    .then_inc(d_out, 1)
                dve.wait_ge(d_out, ready)
                V.tensor_tensor(tile(X, m), tile(X, m), slot(O_TQ, TOK, j), ALU.add).then_inc(mg_done, 1)

            def tile_sum(m):
                ss = view(O_SS, CF_OUT)
                if m == 1:
                    for g in range(4):
                        dve.wait_ge(tap_rest[g], (l + 1) * (2 * (CF_K - TAPS_GLU)))
                    V.tensor_tensor(ss, acc[:, 0, :], acc[:, 1, :], ALU.add).then_inc(mean_sum, 1)
                else:
                    dve.wait_ge(mean_sum, l * 7 + (m - 1))
                    V.tensor_tensor(ss, ss, acc[:, m, :], ALU.add).then_inc(mean_sum, 1)

            def ln_center(m):
                if m == 0:
                    dve.wait_ge(a_out, a_ready(l, A_MEAN))
                    zero_sum(622)
                V.tensor_tensor(acc[:, m, :], acc[:, m, :], view(O_MU, 622), ALU.subtract).then_inc(ln_sub, 1)

            def ln_add(m):
                add_square(l, Q_VAR, m, m % 2, 622)

            def ln_rsqrt(m):
                rsqrt(a_ready(l, A_VAR), 311, O_RT, l * 3 + 2)

            def ln_scale(m):
                V.tensor_tensor(acc[:, m, :], acc[:, m, :], view(O_RT, 622), ALU.mult).then_inc(ln_mul, 1)

            plan = {0: (tile_sum, (1, 2, 3, 4)), 1: (tile_sum, (5, 6, 7)), 3: (ln_center, (0, 1, 2, 3)),
                    4: (ln_center, (4, 5, 6, 7)), 5: (ln_add, (0, 1, 2)), 6: (ln_add, (3, 4, 5)), 7: (ln_add, (6, 7)),
                    9: (ln_rsqrt, (0,)), 10: (ln_scale, (0, 1, 2, 3)), 11: (ln_scale, (4, 5, 6, 7))}
            for p in range(2 * KT):
                m = p // 2
                step(W, P_OS + p, p % 2)
                if p % 2:
                    dve.wait_ge(a_out, a_ready(l, a_gate_sc(m)))
                    merge(m, m % 2, D_OS + m, d_ready(l, D_OS + m))
                work, tiles = plan.get(p, (None, ()))
                for t in tiles:
                    work(t)

            def branch_lo(m):
                dve.wait_ge(cf_hi, l * KT + m + 1)
                V.tensor_tensor(bl[:, m, 0:TP], acc[:, m, 0:TP], f(bh[:, m, 0:TP]), ALU.subtract)
                V.tensor_tensor(bl[:, m, TP:TOK], acc[:, m, TP + CF_H:CF_OUT], f(bh[:, m, TP:TOK]), ALU.subtract) \
                    .then_inc(cf_lo, 1)
            for m in range(KT):
                branch_lo(m)
            with dve.Fori(0, 4) as i:
                for j in range(2):
                    m = i * 2 + j
                    step(W + i * 4, P_OC + 2 * j, 0)
                    step(W + i * 4, P_OC + 2 * j + 1, 1)
                    dve.wait_ge(a_out, l * NA + i * 2 + (A_OC + j + 3))
                    merge(m, j, D_OC + j, l * ND + i * 2 + (D_OC + j + 3))
                    dve.wait_ge(mg_hi, l * KT + i * 2 + (j + 1))
                    V.tensor_tensor(tile(ml, m), tile(X, m), f(tile(mh, m)), ALU.subtract).then_inc(mg_lo, 1)
            zero_sum(TOK)
            with dve.Fori(0, 4) as i:
                for j in range(2):
                    m = i * 2 + j
                    dve.wait_ge(panel_done, W + i * 2 + (P_WO + j + 1))
                    dve.wait_ge(x_back, l * (KT * 16) + i * 32 + (16 * j + 16))
                    V.tensor_tensor(halves(tile(X, m)), halves(tile(X, m)), d_tile(D_WO + j), ALU.add).then_inc(d_out, 1)
                    step(W + i * 2, P_WO + j, j)
                    add_square(l, Q_N2, m, j, TOK)
                    dve.wait_ge(nx_hi, l * 16 + i * 2 + (8 + j + 1))
                    V.scalar_tensor_tensor(tile(xl, m), tile(X, m), col(l, "g2", m), f(tile(xh, m)), ALU.mult,
                                           ALU.subtract).then_inc(nx_lo, 1)
            rsqrt(a_ready(l, A_N2), HALF, O_RF, l * 3 + 3)
            for j in range(2):
                V.memset(slot(O_HG, S_IN, j)[:, 0:S_H], 0.0).then_inc(ff_zero, 1)
                V.memset(slot(O_HU, S_IN, j)[:, 0:S_H], 0.0).then_inc(ff_zero, 1)
            for t0, n, p0, a0, d0 in thirds:
                def product_lo(m, j):
                    dve.wait_ge(ff_hi, l * FT + m + (t0 + 1))
                    pb_ = slot(O_PB, S_OUT, j)
                    V.tensor_tensor(tile(bl, m, 0, TP), pb_[:, 0:TP], f(tile(bh, m, 0, TP)), ALU.subtract)
                    V.tensor_tensor(tile(bl, m, TP, DEC_SEQ), pb_[:, TP + S_H:S_OUT],
                                    f(tile(bh, m, TP, DEC_SEQ)), ALU.subtract).then_inc(ff_lo, 1)

                def tap(l, k, src, dst, m):
                    V.scalar_tensor_tensor(dst, src[:, k:k + S_OUT], col(l, "ffw", m * 3 + k), dst, ALU.mult, ALU.add) \
                        .then_inc(ff_tap, 1)

                def conv_product(i):
                    for j in range(2):
                        m = i * 2 + (t0 + j)
                        hg, hu = slot(O_HG, S_IN, j), slot(O_HU, S_IN, j)
                        gc, uc = slot(O_GC, S_OUT, j), slot(O_UC, S_OUT, j)
                        first = l * (2 * FT) + i * 4 + (2 * t0 + 2 * j)
                        taps_ = l * (FT * 4) + i * 8 + (t0 * 4 + 4 * j + 8)
                        step(W + i * 4, p0 + 2 * j, 0)
                        for piece in PIECES:
                            o = after(piece[3], S_H)
                            last = V.tensor_tensor(hg[:, o:o + piece[2]], view(O_RF + piece[3], piece[2]),
                                                   a_piece(a0 + j, piece), ALU.mult)
                        last.then_inc(a_out, 1)
                        if j or not isinstance(i, int):
                            product_lo(i * 2 + (j - 1), 1 - j)
                        dve.wait_ge(ff_first, first + 1)
                        tap(l, 1, hg, gc, m)
                        step(W + i * 4, p0 + 2 * j + 1, 1)
                        for piece in PIECES:
                            o = after(piece[3], S_H)
                            last = V.tensor_tensor(hu[:, o:o + piece[2]], view(O_RF + piece[3], piece[2]),
                                                   d_piece(d0 + j, piece), ALU.mult)
                        last.then_inc(d_out, 1)
                        dve.wait_ge(ff_tap, taps_ + 1)
                        tap(l, 2, hg, gc, m)
                        dve.wait_ge(ff_first, first + 2)
                        tap(l, 1, hu, uc, m + FT)
                        dve.wait_ge(ff_tap, taps_ + 3)
                        tap(l, 2, hu, uc, m + FT)
                        dve.wait_ge(ff_silu, l * FT + i * 2 + (t0 + j + 1))
                        dve.wait_ge(ff_tap, taps_ + 4)
                        V.tensor_tensor(slot(O_PB, S_OUT, j), gc, uc, ALU.mult).then_inc(ff_prod, 1)
                conv_product(0)
                with dve.Fori(1, n // 2) as i:
                    conv_product(i)
                product_lo(n - 1, 1)
                final = t0 + n == FT
                if final:
                    zero_sum(TOK)
                with dve.Fori(0, 4) as i:
                    for j in range(2):
                        m = i * 2 + j
                        dve.wait_ge(panel_done, W + i * 2 + (p0 + 2 * n + j + 1))
                        V.tensor_tensor(halves(tile(X, m)), halves(tile(X, m)), d_tile(d0 + n + j), ALU.add) \
                            .then_inc(d_out, 1)
                        step(W + i * 2, p0 + 2 * n + j, j)
                        if final:
                            add_square(l + 1, Q_N1, m, j, TOK)
        rsqrt(a_ready(DEPTH, A_N1), HALF, O_RT, DEPTH * 3 + 1)
        for m in range(KT):
            V.scalar_tensor_tensor(X[:, m, :], X[:, m, :], fg[:, m:m + 1], view(O_RT, TOK), ALU.mult, ALU.mult) \
                .then_inc(yn_done, 1)


def weight_panels(w_in, w_attn_out, w_sc_out, w_cf_out, w_o, w_up, w_down):
    q, kv = N_HEADS * HEAD_DIM, N_KV * HEAD_DIM
    at = np.cumsum([0, q, kv, kv] + [D_MODEL] * 8)
    panels = []
    wa = w_attn_out.reshape(DEPTH, N_KV, 2, 2, 2, HEAD_DIM, D_MODEL).transpose(0, 1, 2, 4, 3, 5, 6)
    wa = wa.reshape(DEPTH, q, D_MODEL)

    def cols(w, l, c, rows=slice(None)):
        p = w[l, rows, c * 128:(c + 1) * 128]
        p = p.reshape(-1, 128, 128).transpose(1, 0, 2)
        if p.shape[1] < KT:
            p = np.concatenate([p, np.zeros((128, KT - p.shape[1], 128), p.dtype)], axis=1)
        return p.reshape(128, KT * 128)

    for l in range(DEPTH):
        part = [w_in[:, :, at[i]:at[i + 1]] for i in range(10)] + [w_in[:, :, at[10]:]]
        wq, wk, wv, sb_, sc_, sh_, ca, cg, ga, gs, gc = part
        for m in range(KT):
            panels += [cols(cg, l, m), cols(ca, l, m)]
        panels += [cols(wq, l, m) for m in range(KT)]
        panels += [cols(wk, l, 0), cols(wv, l, 0)]
        for m in range(KT):
            panels += [cols(ga, l, m), cols(wa, l, m)]
        for m in range(KT):
            panels += [cols(sc_, l, m), cols(sh_, l, m), cols(sb_, l, m)]
        for m in range(KT):
            panels += [cols(gs, l, m), cols(w_sc_out, l, m)]
        for m in range(KT):
            panels += [cols(gc, l, m), cols(w_cf_out, l, m)]
        panels += [cols(w_o, l, m) for m in range(KT)]
        t0 = 0
        for n in THIRDS:
            for m in range(t0, t0 + n):
                panels += [cols(w_up, l, m), cols(w_up, l, m + FT)]
            panels += [cols(w_down, l, m, slice(t0 * 128, (t0 + n) * 128)) for m in range(KT)]
            t0 += n
    return np.ascontiguousarray(np.stack(panels + panels[:2]))


def channel_major(a):
    lead = a.shape[:-1]
    a = a.reshape(*lead, a.shape[-1] // 128, 128)
    n = a.ndim
    return a.transpose(n - 1, n - 2, *range(n - 2))


def constants():
    half = ROT // 2
    pos = np.concatenate([np.arange(TP), PAST + np.arange(DEC_SEQ)]).astype(np.float32)
    inv = np.power(np.float32(THETA), -np.arange(0, ROT, 2, dtype=np.float32) / np.float32(ROT)).astype(np.float32)
    ang = inv[:, None] * pos[None, :]
    c = np.ones((HEAD_DIM, TOK), np.float32)
    s = np.zeros((HEAD_DIM, TOK), np.float32)
    for d in range(ROT):
        c[d], s[d] = np.cos(ang[d % half]), np.sin(ang[d % half])
    rot = np.zeros((128, 128), np.float32)
    for h in (0, HEAD_DIM):
        for d in range(half):
            rot[h + d + half, h + d] = -1.0
            rot[h + d, h + d + half] = 1.0
    eye = np.eye(128, dtype=np.float32)
    dup = [np.concatenate([m[:, v:v + 64]] * 2, axis=1) for v in (0, 64) for m in (eye, rot)]
    parts = [eye, np.ones((128, 128), np.float32), rot, dup[0], dup[1], dup[2], dup[3],
             np.full((128, 1), EPS, np.float32), np.concatenate([c, c]), np.concatenate([s, s])]
    return np.ascontiguousarray(np.concatenate(parts, axis=1))


def kernel(x_prompt, x_sample, cache_k, cache_v, state_sc, state_cf, state_ffn, meta_tokens, norm1_g, w_in,
           b_gate, attn_sinks, w_attn_out, sc_conv_w, w_sc_out, cf_conv_w, cf_ln_g, cf_ln_b, w_cf_out, w_o,
           norm2_g, w_up, ffn_conv_w, w_down, final_g):
    import concourse.bacc as bacc
    from concourse.bass_utils import run_bass_kernel_spmd

    (x_prompt, x_sample, cache_k, cache_v, state_sc, state_cf, state_ffn, meta_tokens, norm1_g, w_in, b_gate, attn_sinks,
     w_attn_out, sc_conv_w, w_sc_out, cf_conv_w, cf_ln_g, cf_ln_b, w_cf_out, w_o, norm2_g, w_up, ffn_conv_w, w_down,
     final_g) = (np.asarray(a) for a in (
         x_prompt, x_sample, cache_k, cache_v, state_sc, state_cf, state_ffn, meta_tokens, norm1_g, w_in, b_gate,
         attn_sinks, w_attn_out, sc_conv_w, w_sc_out, cf_conv_w, cf_ln_g, cf_ln_b, w_cf_out, w_o, norm2_g, w_up,
         ffn_conv_w, w_down, final_g))
    vecs = []
    for l in range(DEPTH):
        sinks = np.repeat(attn_sinks[l].reshape(8, 2).transpose(1, 0), 64, axis=0)
        vecs += [channel_major(norm1_g[l]), channel_major(norm2_g[l]), channel_major(b_gate[l]), channel_major(cf_ln_g[l]),
                 channel_major(cf_ln_b[l]), channel_major(sc_conv_w[l]), channel_major(cf_conv_w[l]),
                 channel_major(ffn_conv_w[l]), channel_major(state_sc[l, 0]), channel_major(state_ffn[l, 0]), sinks]
    kc = cache_k[:, 0].transpose(0, 3, 2, 1)
    arrays = {
        "weights": weight_panels(w_in, w_attn_out, w_sc_out, w_cf_out, w_o, w_up, w_down),
        "xt": channel_major(np.concatenate([meta_tokens, x_prompt[0], x_sample[0]])),
        "vecs": np.concatenate([v.reshape(128, -1) for v in vecs], axis=1),
        "consts": constants(),
        "final_g": channel_major(final_g),
        "kcache": np.concatenate([kc, kc], axis=1),
        "vcache": cache_v.reshape(DEPTH, WINDOW, N_KV * HEAD_DIM),
        "cfhist": np.stack([channel_major(state_cf[l, 0]) for l in range(DEPTH)]),
    }
    arrays = {k: np.ascontiguousarray(v) for k, v in arrays.items()}
    outs = {
        "y": (128, KT, TOK), "kp": (DEPTH, 128, WINDOW), "vp": (DEPTH, WINDOW, 128), "scp": (DEPTH, 128, KT * 2 * S_H),
        "cfp": (DEPTH, 128, KT, 2, CF_H), "ffp": (DEPTH, 128, 2 * FT * 2 * S_H), "ks": (DEPTH, 128, WINDOW),
        "vs": (DEPTH, WINDOW, 128),
    }
    nc = bacc.Bacc("TRN2", target_bir_lowering=False, num_devices=1)
    aps = {k: nc.dram_tensor(f"in_{k}", v.shape, F32, kind="ExternalInput").ap() for k, v in arrays.items()}
    aps["spill"] = nc.dram_tensor("spill", (128, KT, TOK), F32, kind="Internal").ap()
    for k, shape in outs.items():
        aps[k] = nc.dram_tensor(f"out_{k}", shape, F32, kind="ExternalOutput").ap()
    encoder(nc, **aps)
    r = run_bass_kernel_spmd(nc, [{f"in_{k}": v for k, v in arrays.items()}], core_ids=[0]).results[0]
    got = {k: np.asarray(r[f"out_{k}"]) for k in outs}

    def rows(a):
        return np.ascontiguousarray(a.transpose(2, 1, 0).reshape(a.shape[2], -1))

    y = rows(got["y"])

    def heads(a, frames_last):
        a = a.transpose(0, 2, 1) if frames_last else a
        return np.ascontiguousarray(a).reshape(DEPTH, 1, WINDOW, N_KV, HEAD_DIM)

    def tails(a, tiles, n, g):
        a = a.reshape(DEPTH, 128, tiles, 2, n)[:, :, :, g]
        return np.ascontiguousarray(np.stack([rows(a[l]) for l in range(DEPTH)])[:, None])

    return (y[N_META:TP][None], y[TP:][None],
            heads(got["kp"], True), heads(got["vp"], False), tails(got["scp"], KT, S_H, 0), tails(got["cfp"], KT, CF_H, 0),
            tails(got["ffp"], 2 * FT, S_H, 0),
            heads(got["ks"], True), heads(got["vs"], False), tails(got["scp"], KT, S_H, 1), tails(got["cfp"], KT, CF_H, 1),
            tails(got["ffp"], 2 * FT, S_H, 1))
```

```python
import numpy as np
import concourse.bass as bass
from concourse import mybir
from contextlib import ExitStack

F32 = mybir.dt.float32
F32R = mybir.dt.float32r
ALU = mybir.AluOpType
ACT = mybir.ActivationFunctionType
AX = mybir.AxisListType

DEPTH, D_MODEL, SEQ, N_META, DEC_SEQ, CHUNK, WINDOW, PAST = 2, 1024, 512, 16, 64, 64, 128, 128
HEAD_DIM, N_HEADS, N_KV, ROT, THETA = 64, 16, 2, 16, 500000.0
D_FF, SC_K, CF_K, FFN_K, EPS = 2816, 3, 31, 3, 1e-5
TP = N_META + SEQ
TOK = TP + DEC_SEQ
HALF = TOK // 2
KT = D_MODEL // 128
FT = D_FF // 128
THIRDS = (8, 8, 6)
SCALE = HEAD_DIM ** -0.5
N_CHUNK = 1 + SEQ // CHUNK
CF_H, S_H = CF_K - 1, SC_K - 1
CF_IN, CF_OUT = 2 * CF_H + TOK, CF_H + TOK
S_IN, S_OUT = 2 * S_H + TOK, S_H + TOK
VEC = {}
VEC_N = 0
for _name, _n in (("g1", KT), ("g2", KT), ("bg", 3 * KT), ("lng", KT), ("lnb", KT), ("scw", SC_K * KT),
                  ("cfw", CF_K * KT), ("ffw", FFN_K * 2 * FT), ("sch", S_H * KT), ("ffh", S_H * 2 * FT), ("sink", 8)):
    VEC[_name] = VEC_N
    VEC_N += _n
CON = {}
CON_N = 0
for _name, _n in (("ident", 128), ("ones", 128), ("rot", 128), ("ka", 128), ("kar", 128), ("kb", 128), ("kbr", 128),
                  ("eps", 1), ("cos", TOK), ("sin", TOK)):
    CON[_name] = CON_N
    CON_N += _n

P_CF, P_K, P_Q, P_V, P_OA, P_SC, P_OS, P_OC, P_WO, P_FF = 0, 16, 17, 25, 26, 42, 66, 82, 98, 106
PANELS = 174
A_N1, A_CF, A_K, A_Q, A_V, A_OA, A_SC, A_OS, A_MEAN, A_VAR, A_OC, A_N2, A_FF, NA = \
    0, 1, 9, 10, 18, 19, 27, 35, 37, 41, 45, 53, 54, 76
D_CF, D_K, D_Q, D_V, D_OA, D_SC, D_OS, D_OC, D_WO, D_FF, ND = 0, 8, 12, 20, 22, 30, 46, 54, 62, 70, 116
S_N1, S_MEAN, S_VAR, S_N2, NS = 0, 1, 2, 3, 4
Q_N1, Q_VAR, Q_N2, NQ = 0, 1, 2, 3
TAPS_GLU = 8
CHUNKS = N_CHUNK + 1

O_KD, O_VV, O_QS, O_P, O_PT1, O_PT2, O_ON = 0, 1440, 3488, 4512, 6048, 7072, 8096
O_QR, O_TQ, O_SG = 4512, 6048, 7232
O_SQ, O_SS, O_RT, O_MU, O_NT = 0, 1244, 1866, 2488, 2488
O_CT, O_CH, O_CV, O_BT = 0, 1184, 2376, 3564
O_HG, O_HU, O_GC, O_UC, O_PB, O_RF = 0, 1192, 2384, 3572, 4760, 5960
N_SCRATCH = 8608

PIECES = ((0, 0, HALF, 0), (1, 0, TP - HALF, HALF), (1, TP - HALF, DEC_SEQ, TP))


def halves(ap):
    return ap.rearrange("p (h n) -> p h n", h=2)


def after(t0, hist):
    return t0 + hist + (hist if t0 >= TP else 0)


def a_free(l, a):
    return l * NA + a + 1


def a_ready(l, a):
    return l * NA + a + 3


def d_free(l, d):
    return l * ND + d + 1


def d_ready(l, d):
    return l * ND + d + 3


def a_gate_sc(m):
    return A_OS + m + (m >= 2) + (m >= 5)


def chunk_span(c):
    if isinstance(c, int):
        if c == CHUNKS - 1:
            return TP, TP, WINDOW + DEC_SEQ
        if c == 0:
            return 0, 0, N_META
        if c < 3:
            return N_META + CHUNK * (c - 1), 0, N_META + CHUNK * c
    return c * CHUNK + (N_META - CHUNK), c * CHUNK + (N_META - 3 * CHUNK), 3 * CHUNK


def it2(l, n, v):
    return l * 16 + n * 2 + (v - 4)


def v_blocks(j):
    if j == 0:
        return [(0, 128)] + [(chunk_span(c)[1], 128) for c in range(3, N_CHUNK)]
    return [(chunk_span(c)[1] + 128, CHUNK) for c in range(3, N_CHUNK)] + [(TP, DEC_SEQ), (128, N_META)]


def has(c):
    return not isinstance(c, int) or 0 <= c < CHUNKS


def v_tile(c):
    if isinstance(c, int):
        return 7 if c == CHUNKS - 1 else max(c - 2, 0)
    return c - 2


def encoder(nc, weights, xt, vecs, consts, kcache, vcache, cfhist, spill, y, kp, vp, scp, cfp, ffp, ks, vs):
    ctx = ExitStack()

    def sb(name, shape, dt=F32):
        return ctx.enter_context(nc.sbuf_tensor(name, shape, dt))

    def sem(name):
        return ctx.enter_context(nc.semaphore(name))

    xh, xl = sb("xn_hi", [128, KT, TOK], F32R), sb("xn_lo", [128, KT, TOK], F32R)
    bh, bl = sb("branch_hi", [128, KT, TOK], F32R), sb("branch_lo", [128, KT, TOK], F32R)
    X = sb("x_q_merged", [128, KT, TOK])
    raw = sb("raw", [128, 2, KT * 128])
    wh, wl = sb("w_hi", [128, 2, KT * 128], F32R), sb("w_lo", [128, 2, KT * 128], F32R)
    scr = sb("scratch", [128, N_SCRATCH])
    vec = sb("vec", [128, DEPTH * VEC_N + KT])
    con = sb("con", [128, CON_N])
    sct = sb("sc_tail", [128, KT, 2 * S_H])
    fft = sb("ffn_tail", [128, 2 * FT, 2 * S_H])
    mx, nm, ds_, es = (sb(n, [128, N_KV, 4]) for n in ("score_max", "neg_max", "sink_diff", "sink_exp"))
    sums, rinv = sb("exp_sums", [128, N_KV, 4]), sb("inv_den", [128, N_KV, 4])
    warm = sb("warm", [128, 1])
    nsink = sb("neg_sink", [128, DEPTH * 8])
    with nc.sbuf_tensor("glu", [128, KT, CF_IN], F32) as G, nc.sbuf_tensor("cf_acc", [128, KT, CF_OUT], F32) as acc:
        pass
    with nc.sbuf_tensor("merged_hi", [128, KT, TOK], F32R) as mh, nc.sbuf_tensor("merged_lo", [128, KT, TOK], F32R) as ml:
        pass
    PS = ctx.enter_context(nc.psum_tensor("ps", [128, 8, 512], F32))

    def view(off, n):
        return scr[:, off:off + n]

    def slot(off, n, s):
        return scr[:, off + n * s:off + n * (s + 1)]

    KD = view(O_KD, 2 * 720).rearrange("p (v n) -> p v n", v=2)
    VV = view(O_VV, 2048).rearrange("p (c j n) -> p c j n", c=8, j=2)
    ident, ones = con[:, CON["ident"]:CON["ident"] + 128], con[:, CON["ones"]:CON["ones"] + 128]
    cos, sin = con[:, CON["cos"]:CON["cos"] + TOK], con[:, CON["sin"]:CON["sin"] + TOK]
    eps = con[:, CON["eps"]:CON["eps"] + 1]

    def f(ap):
        return ap.bitcast(F32)

    def col(l, name, i, n=1):
        if isinstance(l, int) and isinstance(i, int):
            at = l * VEC_N + VEC[name] + i
            return vec[:, at:at + n]
        return vec[:, bass.ds(l * VEC_N + VEC[name] + i, n)]

    def tile(t, m, a=0, n=None):
        n = t.shape[2] if n is None else n
        if isinstance(m, int) and isinstance(a, int):
            return t[:, m, a:a + n]
        return t[:, :, :].rearrange("p t n -> p (t n)")[:, bass.ds(m * t.shape[2] + a, n)]

    def a_tile(a, n=HALF):
        b = 2 * (a % 2)
        return PS[:, b:b + 2, 0:n]

    def d_tile(d, n=HALF):
        b = 4 + 2 * (d % 2)
        return PS[:, b:b + 2, 0:n]

    def d_piece(d, piece):
        return PS[:, 4 + 2 * (d % 2) + piece[0], piece[1]:piece[1] + piece[2]]

    def a_piece(a, piece):
        return PS[:, 2 * (a % 2) + piece[0], piece[1]:piece[1] + piece[2]]

    raw_in = [sem("raw_in0"), sem("raw_in1")]
    hi_done, lo_done = sem("hi_done"), sem("lo_done")
    panel_done = sem("panel_done")
    a_out, d_out = sem("a_out"), sem("d_out")
    x_in = [sem(f"x_in{i}") for i in range(4)]
    vec_in, con_in = sem("vec_in"), sem("con_in")
    late_in = sem("late_in")
    x_spilled = sem("x_spilled")
    x_back = sem("x_back")
    cache_in = sem("cache_in")
    hist_in = sem("hist_in")
    kv_out = sem("kv_out")
    tails_out = sem("tails_out")
    small_out = sem("small_out")
    vs_out = sem("vs_out")
    y_out = sem("y_out")
    sq_done, sq_sum = sem("sq_done"), sem("sq_sum")
    mean_sum = sem("mean_sum")
    sum_ps = sem("sum_ps")
    rs_done = sem("rs_done")
    nx_mul = sem("nx_mul")
    nx_hi, nx_lo = sem("nx_hi"), sem("nx_lo")
    glu_gate, glu_first = sem("glu_gate"), sem("glu_first")
    qrot = sem("qrot")
    qtmp = sem("qtmp")
    krot = sem("krot")
    qrot_ps, krot_ps = sem("qrot_ps"), sem("krot_ps")
    vt_ps = sem("vt_ps")
    zero_qs = sem("zero_qs")
    qs_done = sem("qs_done")
    s_done = sem("s_done")
    nm_done = sem("nm_done")
    mx_done = sem("mx_done")
    es_done, p_done = sem("es_done"), sem("p_done")
    t_done = sem("t_done")
    pt1_done, pt2_done = sem("pt1_done"), sem("pt2_done")
    den_done, rinv_done = sem("den_done"), sem("rinv_done")
    o_done, on_done, ot_done = sem("o_done"), sem("on_done"), sem("ot_done")
    oh_done, ol_done = sem("oh_done"), sem("ol_done")
    tap_glu, tap_rest = sem("tap_glu"), [sem(f"tap_rest{g}") for g in range(4)]
    mg_done = sem("mg_done")
    mg_hi, mg_lo = sem("mg_hi"), sem("mg_lo")
    sc_hist = sem("sc_hist")
    sc_tap = sem("sc_tap")
    sc_hi, sc_lo = sem("sc_hi"), sem("sc_lo")
    sc_tail_done = sem("sc_tail_done")
    ln_sub, ln_mul, ln_silu = sem("ln_sub"), sem("ln_mul"), sem("ln_silu")
    cf_hi, cf_lo = sem("cf_hi"), sem("cf_lo")
    g_zero = sem("g_zero")
    ff_zero, ff_hist = sem("ff_zero"), sem("ff_hist")
    ff_first, ff_tap = sem("ff_first"), sem("ff_tap")
    ff_silu, ff_prod = sem("ff_silu"), sem("ff_prod")
    ff_hi, ff_lo = sem("ff_hi"), sem("ff_lo")
    ff_tail_done = sem("ff_tail_done")
    yn_done = sem("yn_done")
    nsink_done = sem("nsink_done")
    carrier = sem("carrier")

    thirds, at = [], (0, P_FF, A_FF, D_FF)
    for n in THIRDS:
        thirds.append((at[0], n, at[1], at[2], at[3]))
        at = (at[0] + n, at[1] + 2 * n + KT, at[2] + n, at[3] + n + KT)

    block = ctx.enter_context(nc.Block())

    @block.sync
    def _(sp):
        sp.dma_start(X[:, 0:2, :], xt[:, 0:2, :]).then_inc(x_in[0], 16)
        sp.dma_start(vec[:, :], vecs).then_inc(vec_in, 16)
        for i in range(1, 4):
            if i < 3:
                sp.dma_start(raw[:, i - 1, :], weights[i - 1, :, :]).then_inc(raw_in[i - 1], 16)
            sp.dma_start(X[:, 2 * i:2 * i + 2, :], xt[:, 2 * i:2 * i + 2, :]).then_inc(x_in[i], 16)
        sp.dma_start(con[:, 0:CON["cos"]], consts[:, 0:CON["cos"]]).then_inc(con_in, 16)
        sp.dma_start(con[:, CON["cos"]:], consts[:, CON["cos"]:]).then_inc(late_in, 16)
        with sp.Fori(0, DEPTH * PANELS // 2) as i:
            for s in range(2):
                sp.wait_ge(lo_done, 2 * i + s + 1)
                sp.dma_start(raw[:, s, :], weights.rearrange("w p n -> p w n")[:, bass.ds(2 * i + (s + 2), 1), :]) \
                    .then_inc(raw_in[s], 16)
        for m in range(KT):
            sp.wait_ge(yn_done, m + 1)
            sp.dma_start(y[:, m, :], X[:, m, :]).then_inc(y_out, 16)
        sp.wait_ge(y_out, 16 * KT)

    @block.gpsimd
    def _(pool):
        def plain():
            nc.gpsimd.sem_inc(carrier, 1)

        pool.dma_start(vs[:, 0:WINDOW - DEC_SEQ, :], vcache[:, DEC_SEQ:WINDOW, :]).then_inc(vs_out, 16)
        with pool.Fori(0, DEPTH) as l:
            for i in range(4):
                pool.wait_ge(x_in[i], 16)
            pool.wait_ge(d_out, l * ND + 2)
            plain()
            pool.dma_start(spill, X[:, :, :]).then_inc(x_spilled, 16)
            pool.dma_start(G[:, :, TP + CF_H:TP + 2 * CF_H], cfhist[bass.ds(l, 1), :, :, :]
                           .rearrange("l p t n -> (l p) t n")).then_inc(hist_in, 16)
            pool.wait_ge(nx_lo, l * 24 + 16)
            plain()
            pool.dma_start(KD[:, :, TP:TP + WINDOW], kcache[bass.ds(l, 1), :, :, :]
                           .rearrange("l p v n -> (l p) v n")).then_inc(cache_in, 16)
            pool.dma_start(VV[:, 7, 0, :], vcache[bass.ds(l, 1), :, :].rearrange("l p n -> (l p) n")).then_inc(cache_in, 16)
            nc.gpsimd.memset(view(O_QS, 1024), 0.0).then_inc(zero_qs, 1)
            pool.wait_ge(zero_qs, l + 1)
            plain()

            def stage(c, n):
                q0 = chunk_span(c)[0]
                for v in range(N_KV):
                    if isinstance(c, int) and c == 0:
                        pool.wait_ge(qrot, l * KT + 4 * (v + 1))
                    pool.wait_ge(s_done, l * 20 + n * 2 + v + 1)
                    plain()
                    dst = view(O_QS + 512 * v, 512).rearrange("p (i n) -> p i n", i=4)
                    if isinstance(q0, int):
                        src = X[:, 4 * v:4 * v + 4, q0:q0 + 64]
                    else:
                        src = X[:, 4 * v:4 * v + 4, bass.ds(q0, 64)]
                    nc.gpsimd.tensor_copy(dst[0:64, :, 0:64], src[0:64, :, :])
                    nc.gpsimd.tensor_copy(dst[64:128, :, 64:128], src[64:128, :, :]).then_inc(qs_done, 1)

            for c in range(3):
                stage(c, c)
            with pool.Fori(3, N_CHUNK) as c:
                stage(c, c)
            stage(CHUNKS - 1, CHUNKS - 1)
            pool.wait_ge(krot, l * 2 + 2)
            pool.wait_ge(cache_in, l * 32 + 32)
            plain()
            for v in range(N_KV):
                r = slice(64 * v, 64 * v + 64)
                pool.dma_start(kp[bass.ds(l, 1), r, :].rearrange("l p n -> (l p) n"),
                               KD[r, v, TP - WINDOW:TP]).then_inc(kv_out, 16)
                pool.dma_start(ks[bass.ds(l, 1), r, :].rearrange("l p n -> (l p) n"),
                               KD[r, v, TP + DEC_SEQ:TP + DEC_SEQ + WINDOW]).then_inc(kv_out, 16)
            pool.wait_ge(d_out, d_ready(l, D_V + 1))
            plain()
            pool.dma_start(vp[bass.ds(l, 1), 0:64, :].rearrange("l p n -> (l p) n"), VV[64:128, 6, 0, :]).then_inc(kv_out, 16)
            pool.dma_start(vp[bass.ds(l, 1), 64:128, :].rearrange("l p n -> (l p) n"), VV[0:64, 6, 1, :]).then_inc(kv_out, 16)
            pool.dma_start(vs[bass.ds(l, 1), WINDOW - DEC_SEQ:WINDOW, :].rearrange("l p n -> (l p) n"),
                           VV[0:64, 7, 1, :]).then_inc(kv_out, 16)
            pool.wait_ge(d_out, d_ready(l, D_CF + 7))
            plain()
            pool.dma_start(cfp[bass.ds(l, 1), :, :, 0, :].rearrange("l p t n -> (l p) t n"),
                           G[:, :, TP:TP + CF_H]).then_inc(tails_out, 16)
            pool.dma_start(cfp[bass.ds(l, 1), :, :, 1, :].rearrange("l p t n -> (l p) t n"),
                           G[:, :, CF_IN - CF_H:CF_IN]).then_inc(tails_out, 16)
            pool.wait_ge(sc_tail_done, l * KT + KT)
            plain()
            pool.dma_start(scp[bass.ds(l, 1), :, :].rearrange("l p n -> (l p) n"),
                           sct[:, :, :].rearrange("p t n -> p (t n)")).then_inc(small_out, 16)
            with pool.Fori(0, KT) as m:
                pool.wait_ge(mg_lo, l * KT + m + 1)
                pool.wait_ge(x_spilled, l * 16 + 16)
                plain()
                pool.dma_start(tile(X, m), spill[:, bass.ds(m, 1), :].rearrange("p t n -> p (t n)")).then_inc(x_back, 16)
                pool.wait_ge(x_back, l * (KT * 16) + m * 16 + 16)
            pool.wait_ge(ff_tail_done, l * (2 * FT) + (2 * FT + 2))
            plain()
            pool.dma_start(ffp[bass.ds(l, 1), :, :].rearrange("l p n -> (l p) n"),
                           fft[:, :, :].rearrange("p t n -> p (t n)")).then_inc(small_out, 16)
            pool.wait_ge(small_out, l * 32 + 32)
            plain()
        pool.wait_ge(vs_out, 16)
        pool.wait_ge(kv_out, DEPTH * 7 * 16)
        pool.wait_ge(tails_out, DEPTH * 32)

    @block.tensor
    def _(pe):
        def panel(w, s, out, nk, rh, rl, kwait=None, k0=0, k1=KT, between=None):
            pe.wait_ge(lo_done, w + 1)
            for k in range(k0, min(nk, k1)):
                if between and k == 2:
                    between()
                if kwait:
                    pe.wait_ge(kwait[0], kwait[1] + k + 1)
                wk = slice(k * 128, k * 128 + 128)
                for j, (a, b) in enumerate(((wh, rh), (wh, rl), (wl, rh))):
                    for h in range(2):
                        last = nc.tensor.matmul(out[:, h, :], a[:, s, wk], b[:, k, h * HALF:(h + 1) * HALF],
                                                start=(k == 0 and j == 0), stop=(k == nk - 1 and j == 2))
                if k == nk - 1:
                    last.then_inc(panel_done, 1)

        def two_panels(w, outs, nk, r0, r1, free, kwait, last_late, middle=None):
            if last_late:
                order = [(p, k) for p in range(2) for k in range(nk - 3)]
            else:
                order = [(p, k - 2 * p) for k in range(nk - 1) for p in range(2) if 0 <= k - 2 * p < nk - 3]
            order += [(p, k) for p in range(2) for k in range(nk - 3, nk)]
            for u, (p, k) in enumerate(order):
                if k == 0:
                    pe.wait_ge(*free[p])
                    pe.wait_ge(lo_done, w + p + 1)
                if p == 0:
                    pe.wait_ge(kwait[0], kwait[1] + k + 1)
                if u == 5 and middle:
                    middle()
                wk = slice(k * 128, k * 128 + 128)
                rh, rl = (r0, r1)[p]
                for j, (a, b) in enumerate(((wh, rh), (wh, rl), (wl, rh))):
                    for h in range(2):
                        last = nc.tensor.matmul(outs[p][:, h, :], a[:, p, wk], b[:, k, h * HALF:(h + 1) * HALF],
                                                start=(k == 0 and j == 0), stop=(k == nk - 1 and j == 2))
                if k == nk - 1:
                    last.then_inc(panel_done, 1)

        def channel_sum(l, a, n, ready):
            pe.wait_ge(a_out, a_free(l, a))
            pe.wait_ge(*ready)
            for h in range(2):
                last = nc.tensor.matmul(a_tile(a, n)[:, h, :], ones, view(O_SS, 622)[:, h * n:(h + 1) * n],
                                        start=True, stop=True)
            last.then_inc(sum_ps, 1)

        def squares_ready(l, q):
            return sq_sum, l * (NQ * 9) + (q * 9 + 10)

        def residual(l, w, d, nk, rh, rl, kwait):
            two_panels(l * PANELS + w, (d_tile(d), d_tile(d + 1)), nk, (rh, rl), (rh, rl),
                       [(d_out, d_free(l, d + j)) for j in range(2)], kwait, True)
            with pe.Fori(1, 4) as i:
                for j in range(2):
                    pe.wait_ge(d_out, l * ND + i * 2 + (d + j + 1))
                    panel(l * PANELS + i * 2 + (w + j), j, d_tile(d + j), nk, rh, rl)

        def first_pair(l, w, a, d, kwait, last_late, middle=None):
            two_panels(w, (a_tile(a), d_tile(d)), KT, (xh, xl), (xh, xl), ((a_out, a_free(l, a)), (d_out, d_free(l, d))),
                       kwait, last_late, middle)

        def pair(l, w, a, d, rg, ro, kwait=None, middle=None):
            pe.wait_ge(a_out, a_free(l, a[0]))
            panel(w, 0, a_tile(a[1]), KT, *rg)
            if middle:
                middle()
            pe.wait_ge(d_out, d_free(l, d[0]))
            panel(w + 1, 1, d_tile(d[1]), KT, *ro, kwait=kwait)

        def scores(l, c, n, v):
            k0, nk = chunk_span(c)[1:]
            it = l * 20 + n * 2 + v
            pe.wait_ge(qs_done, it + 1)
            pe.wait_ge(p_done, it + 1)
            for i in range(4):
                keys = KD[:, v, k0:k0 + nk] if isinstance(k0, int) else \
                    view(O_KD, 1440)[:, bass.ds(k0 + 720 * v, nk)]
                last = nc.tensor.matmul(PS[:, 2 * v + i // 2, 256 * (i % 2):256 * (i % 2) + nk],
                                        view(O_QS + 512 * v + 128 * i, 128), keys, start=True, stop=True)
            last.then_inc(s_done, 1)

        def turn(l, c, n, v):
            nk = chunk_span(c)[2]
            n1, n2 = min(nk, 128), max(nk - 128, 0)
            it = l * 20 + n * 2 + v
            pe.wait_ge(p_done, it + 3)
            pe.wait_ge(pt1_done, it + 1)
            if n2:
                pe.wait_ge(pt2_done, it2(l, n, v) + 1)
            for i in range(4):
                P = view(O_P + 768 * v + 192 * i, 192)
                last = nc.tensor.transpose(PS[0:n1, 4, 128 * i:128 * i + 128], P[:, 0:n1], ident)
                if n2:
                    last = nc.tensor.transpose(PS[0:n2, 5, 128 * i:128 * i + 128], P[:, 128:nk], ident)
            last.then_inc(t_done, 1)

        def values(l, c, n, v):
            nk = chunk_span(c)[2]
            n1, n2 = min(nk, 128), max(nk - 128, 0)
            vt = v_tile(c)
            it = l * 20 + n * 2 + v
            pe.wait_ge(pt1_done, it + 2)
            if n2:
                pe.wait_ge(pt2_done, it2(l, n, v) + 2)
            pe.wait_ge(on_done, it + 1)
            for i in range(4):
                for j, (nn, o) in enumerate(((n1, O_PT1), (n2, O_PT2))):
                    if nn:
                        if isinstance(vt, int):
                            vals = VV[0:nn, vt, j, 64 * v:64 * v + 64]
                        else:
                            vals = scr[0:nn, bass.ds(vt * 256 + (O_VV + 128 * j + 64 * v), 64)]
                        last = nc.tensor.matmul(PS[:, 6, 64 * i:64 * i + 64],
                                                scr[0:nn, o + 512 * v + 128 * i:o + 512 * v + 128 * i + 128], vals,
                                                start=(i == 0 and j == 0), stop=(j == (1 if n2 else 0)),
                                                skip_group_check=True)
            last.then_inc(o_done, 1)

        def turn_back(l, n, v):
            it = l * 20 + n * 2 + v
            pe.wait_ge(on_done, it + 2)
            pe.wait_ge(ol_done, it + 1)
            for j in range(2):
                last = nc.tensor.transpose(PS[:, 7, 128 * j:128 * j + 128], view(O_ON + 256 * v + 128 * j, 128), ident)
            last.then_inc(ot_done, 1)

        def attention(l, n):
            if has(n):
                scores(l, n, n, 0)
            if has(n - 2):
                values(l, n - 2, n - 2, 1)
            if isinstance(n, int) and n == 1:
                pe.wait_ge(d_out, d_ready(l, D_V + 1))
            if has(n - 1):
                turn(l, n - 1, n - 1, 0)
            if has(n - 2):
                turn_back(l, n - 2, 0)
            if has(n):
                scores(l, n, n, 1)
            if has(n - 1):
                values(l, n - 1, n - 1, 0)
                turn(l, n - 1, n - 1, 1)
            if has(n - 2):
                turn_back(l, n - 2, 1)

        def attention_end(l):
            n = CHUNKS - 1

            def gate_part(k0, k1):
                panel(l * PANELS + P_OA, 0, a_tile(A_OA), KT, xh, xl, k0=k0, k1=k1)
            values(l, n - 1, n - 1, 1)
            turn(l, n, n, 0)
            turn_back(l, n - 1, 0)
            pe.wait_ge(p_done, l * 20 + 22)
            gate_part(0, 2)
            values(l, n, n, 0)
            turn(l, n, n, 1)
            turn_back(l, n - 1, 1)
            gate_part(2, 5)
            values(l, n, n, 1)
            gate_part(5, 6)
            turn_back(l, n, 0)
            turn_back(l, n, 1)
            gate_part(6, KT)

        nc.tensor.sem_inc(s_done, 2)
        nc.tensor.sem_inc(t_done, 2)
        nc.tensor.sem_inc(o_done, 2)
        with pe.Fori(0, DEPTH) as l:
            W = l * PANELS

            def mean_square1():
                pe.wait_ge(con_in, 16)
                channel_sum(l, A_N1, HALF, squares_ready(l, Q_N1))

            def glu(i, j):
                pair(l, W + i * 4 + (P_CF + 2 * j), (i * 2 + (A_CF + j), A_CF + j), (i * 2 + (D_CF + j), D_CF + j),
                     (xh, xl), (xh, xl))
            first_pair(l, W + P_CF, A_CF, D_CF, (nx_lo, l * 24), False, mean_square1)
            first_pair(l, W + P_CF + 2, A_CF + 1, D_CF + 1, (nx_lo, l * 24 + 8), False)
            with pe.Fori(1, 4) as i:
                glu(i, 0)
                glu(i, 1)
            def rotate(i, j):
                pe.wait_ge(a_out, l * NA + i * 2 + (A_Q + j + 3))
                pe.wait_ge(d_out, l * ND + i * 2 + (D_Q + j + 1))
                for h in range(2):
                    last = nc.tensor.matmul(d_tile(D_Q + j)[:, h, :], con[:, CON["rot"]:CON["rot"] + 128],
                                            slot(O_QR, TOK, j)[:, h * HALF:(h + 1) * HALF], start=True, stop=True)
                last.then_inc(qrot_ps, 1)

            def keys():
                pe.wait_ge(a_out, a_ready(l, A_K))
                for j, name in enumerate(("ka", "kar", "kb", "kbr")):
                    pe.wait_ge(d_out, d_free(l, D_K + j))
                    for h in range(2):
                        last = nc.tensor.matmul(d_tile(D_K + j)[:, h, :], con[:, CON[name]:CON[name] + 128],
                                                slot(O_QR, TOK, 0)[:, h * HALF:(h + 1) * HALF], start=True, stop=True)
                    last.then_inc(krot_ps, 1)

            def queries(i):
                for j in range(2):
                    pe.wait_ge(a_out, l * NA + i * 2 + (A_Q + j + 1))
                    panel(W + i * 2 + (P_Q + j), 1 - j, a_tile(A_Q + j), KT, xh, xl)
                    if j:
                        rotate(i, 0)
                    elif isinstance(i, int):
                        keys()
                    else:
                        rotate(i - 1, 1)
            pe.wait_ge(a_out, a_free(l, A_K))
            panel(W + P_K, 0, a_tile(A_K), KT, xh, xl)
            queries(0)
            with pe.Fori(1, 4) as i:
                queries(i)
            pe.wait_ge(a_out, a_free(l, A_V))
            panel(W + P_V, 1, a_tile(A_V), KT, xh, xl, between=lambda: rotate(3, 1))
            pe.wait_ge(a_out, a_ready(l, A_V))
            pe.wait_ge(cache_in, l * 32 + 32)
            pe.wait_ge(krot, l * 2 + 2)
            attention(l, 0)
            for j in range(2):
                pe.wait_ge(d_out, d_free(l, D_V + j))
                nc.tensor.sem_inc(carrier, 1)
                for b, (t0, n) in enumerate(v_blocks(j)):
                    last = nc.tensor.transpose(PS[0:n, 4 + 2 * ((D_V + j) % 2) + b // 4, 128 * (b % 4):128 * (b % 4) + 128],
                                               slot(O_QR, TOK, 0)[:, t0:t0 + n], ident)
                last.then_inc(vt_ps, 1)
            for n in range(1, 5):
                attention(l, n)
            with pe.Fori(5, N_CHUNK) as n:
                attention(l, n)
            attention(l, CHUNKS - 1)
            attention_end(l)

            def branch(i, j):
                pair(l, W + i * 4 + (P_OA + 2 * j), (i * 2 + (A_OA + j), A_OA + j), (i * 2 + (D_OA + j), D_OA + j),
                     (xh, xl), (bh, bl))
            pe.wait_ge(ol_done, l * 20 + 21)
            panel(W + P_OA + 1, 1, d_tile(D_OA), KT, bh, bl)
            branch(0, 1)
            with pe.Fori(1, 4) as i:
                branch(i, 0)
                branch(i, 1)
            with pe.Fori(0, 4) as i:
                for j in range(2):
                    w = W + i * 6 + (P_SC + 3 * j)
                    pe.wait_ge(a_out, l * NA + i * 2 + (A_SC + j + 1))
                    panel(w, j % 2, a_tile(A_SC + j), KT, xh, xl)
                    for e in range(2):
                        pe.wait_ge(d_out, l * ND + i * 4 + (D_SC + 2 * j + e + 1))
                        panel(w + (1 + e), (j + 1 + e) % 2, d_tile(D_SC + 2 * j + e), KT, xh, xl)

            def mean():
                channel_sum(l, A_MEAN, 311, (mean_sum, l * 7 + 7))

            def variance():
                channel_sum(l, A_VAR, 311, squares_ready(l, Q_VAR))
            for m in range(KT):
                pair(l, W + (P_OS + 2 * m), (a_gate_sc(m), a_gate_sc(m)), (D_OS + m, D_OS + m), (xh, xl), (bh, bl),
                     kwait=(sc_lo, l * KT) if m == 0 else None, middle={1: mean, 4: variance}.get(m))
            with pe.Fori(0, 4) as i:
                for j in range(2):
                    pe.wait_ge(a_out, l * NA + i * 2 + (A_OC + j + 1))
                    panel(W + i * 4 + (P_OC + 2 * j), 0, a_tile(A_OC + j), KT, xh, xl)
                    pe.wait_ge(d_out, l * ND + i * 2 + (D_OC + j + 1))
                    panel(W + i * 4 + (P_OC + 2 * j + 1), 1, d_tile(D_OC + j), KT, bh, bl,
                          kwait=(cf_lo, l * KT) if j == 0 else None)
            residual(l, P_WO, D_WO, KT, mh, ml, (mg_lo, l * KT))
            for t0, n, p0, a0, d0 in thirds:
                def up(i, j):
                    pair(l, W + i * 4 + (p0 + 2 * j), (i * 2 + (a0 + j), a0 + j), (i * 2 + (d0 + j), d0 + j),
                         (xh, xl), (xh, xl))

                def mean_square():
                    channel_sum(l, A_N2, HALF, squares_ready(l, Q_N2))
                if t0 == 0:
                    first_pair(l, W + p0, a0, d0, (nx_lo, l * 24 + 16), True, mean_square)
                    up(0, 1)
                with pe.Fori(1 if t0 == 0 else 0, n // 2) as i:
                    up(i, 0)
                    up(i, 1)
                residual(l, p0 + 2 * n, d0 + n, n, bh, bl, (ff_lo, l * FT + t0))
        channel_sum(DEPTH, A_N1, HALF, squares_ready(DEPTH, Q_N1))

    @block.scalar
    def _(act):
        def step(wbase, off, s):
            act.wait_ge(panel_done, wbase + (off + 1))
            act.wait_ge(raw_in[s], wbase * 8 + ((off - s) // 2 + 2) * 16)
            nc.scalar.activation(wh[:, s, :], raw[:, s, :], ACT.Copy).then_inc(hi_done, 1)

        def square(l, q, m, s, src, n):
            act.wait_ge(sq_sum, l * (NQ * 9) + (q * 9 + 1) + m)
            nc.scalar.activation(slot(O_SQ, 622, s)[:, 0:n], src, ACT.Square).then_inc(sq_done, 1)

        def residual(l, w, d, squares=None, g=None):
            with act.Fori(0, 4) as i:
                for j in range(2):
                    step(l * PANELS + i * 2, w + j, j)
                    if squares is not None:
                        act.wait_ge(d_out, l * ND + i * 2 + (d + j + 3))
                        square(*squares, i * 2 + j, j, tile(X, i * 2 + j), TOK)
                        nc.scalar.activation(tile(xh, i * 2 + j), tile(X, i * 2 + j), ACT.Identity, bias=0.0,
                                             scale=col(squares[0], g, i * 2 + j)).then_inc(nx_hi, 1)

        def root(l, s, a, n, at):
            nc.scalar.activation(warm[:, :], eps, ACT.Sqrt)
            act.wait_ge(sum_ps, l * NS + (s + 1))
            nc.scalar.activation(halves(view(at, 2 * n)), a_tile(a, n), ACT.Sqrt, bias=eps, scale=1.0 / D_MODEL) \
                .then_inc(a_out, 1)

        def gate(a, j, b, used):
            act.wait_ge(d_out, used)
            nc.scalar.activation(halves(slot(O_SG, TOK, j)), a_tile(a), ACT.Sigmoid, bias=b).then_inc(a_out, 1)

        nc.scalar.sem_inc(a_out, 2)
        nc.scalar.sem_inc(p_done, 2)
        nc.scalar.sem_inc(pt1_done, 1)
        for m in range(KT):
            act.wait_ge(x_in[m // 2], 16)
            square(0, Q_N1, m, m % 2, X[:, m, :], TOK)
            if m == 0:
                act.wait_ge(vec_in, 16)
            nc.scalar.activation(xh[:, m, :], X[:, m, :], ACT.Identity, bias=0.0, scale=col(0, "g1", m)).then_inc(nx_hi, 1)
            if m in (1, 3):
                s = m // 2
                act.wait_ge(raw_in[s], 16)
                nc.scalar.activation(wh[:, s, :], raw[:, s, :], ACT.Copy).then_inc(hi_done, 1)
        act.wait_ge(con_in, 16)
        with act.Fori(0, DEPTH) as l:
            W = l * PANELS

            def normed_hi(m):
                act.wait_ge(nx_mul, l * KT + (m + 1))
                nc.scalar.activation(xh[:, m, :], slot(O_NT, TOK, m % 3), ACT.Identity, bias=0.0, scale=col(l, "g1", m)) \
                    .then_inc(nx_hi, 1)
            root(l, S_N1, A_N1, HALF, O_RT)
            step(W, P_CF, 0)
            act.wait_ge(panel_done, W + (P_CF + 2))
            normed_hi(0)
            normed_hi(1)
            step(W, P_CF + 1, 1)
            normed_hi(2)
            act.wait_ge(a_out, a_ready(l, A_CF))
            nc.scalar.activation(slot(O_SG, TOK, 0), slot(O_QR, TOK, 0), ACT.Sigmoid).then_inc(glu_gate, 1)
            for m in range(3, KT):
                normed_hi(m)
            step(W, P_CF + 2, 0)
            gate(A_CF + 1, 1, 0.0, d_free(l, D_CF + 1))
            act.wait_ge(glu_first, l + 1)
            step(W, P_CF + 3, 1)

            def glu(i):
                for j in range(2):
                    step(W + i * 4, P_CF + 2 * j, 0)
                    gate(A_CF + j, j, 0.0, l * ND + i * 2 + (D_CF + j + 1))
                    step(W + i * 4, P_CF + 2 * j + 1, 1)
            with act.Fori(1, 4) as i:
                glu(i)
            step(W, P_K, 0)
            nc.scalar.activation(halves(slot(O_QR, TOK, 0)), a_tile(A_K), ACT.Copy).then_inc(a_out, 1)
            with act.Fori(0, 4) as i:
                for j in range(2):
                    step(W + i * 2, P_Q + j, 1 - j)
                    act.wait_ge(d_out, l * ND + i * 2 + (D_Q + j + 1))
                    act.wait_ge(krot_ps, l * 4 + 4)
                    nc.scalar.activation(halves(slot(O_QR, TOK, j)), a_tile(A_Q + j), ACT.Copy).then_inc(a_out, 1)
            act.wait_ge(panel_done, W + (P_V + 1))
            act.wait_ge(qrot, l * KT + (KT - 1))
            nc.scalar.activation(halves(slot(O_QR, TOK, 0)), a_tile(A_V), ACT.Copy).then_inc(a_out, 1)
            step(W, P_V, 1)

            def exps(n, v):
                nk = chunk_span(n)[2]
                it = l * 20 + n * 2 + v
                act.wait_ge(nm_done, 2 * it + 2)
                act.wait_ge(rinv_done, it + 1)
                nc.scalar.activation(es[:, v, :], ds_[:, v, :], ACT.Exp).then_inc(es_done, 1)
                act.wait_ge(t_done, it + 1)
                for i in range(4):
                    last = nc.scalar.activation(view(O_P + 768 * v + 192 * i, nk),
                                                PS[:, 2 * v + i // 2, 256 * (i % 2):256 * (i % 2) + nk], ACT.Exp,
                                                bias=nm[:, v, i:i + 1], scale=SCALE, accum_out=sums[:, v, i:i + 1])
                last.then_inc(p_done, 1)

            def copy_first(n, v):
                n1 = min(chunk_span(n)[2], 128)
                it = l * 20 + n * 2 + v
                act.wait_ge(t_done, it + 3)
                act.wait_ge(o_done, it + 1)
                nc.scalar.activation(scr[0:n1, O_PT1 + 512 * v:O_PT1 + 512 * v + 512], PS[0:n1, 4, :], ACT.Copy) \
                    .then_inc(pt1_done, 1)

            def outputs_hi(n, v):
                q0 = chunk_span(n)[0]
                act.wait_ge(ot_done, l * 20 + n * 2 + v + 1)
                src = PS[:, 7, 0:256].rearrange("p (t n) -> p t n", n=64)
                dst = bh[:, 4 * v:4 * v + 4, q0:q0 + 64] if isinstance(q0, int) else bh[:, 4 * v:4 * v + 4, bass.ds(q0, 64)]
                nc.scalar.activation(dst, src, ACT.Copy).then_inc(oh_done, 1)

            def attention(n):
                for v in range(N_KV):
                    if has(n - 1):
                        copy_first(n - 1, v)
                    if has(n - 2) and v == 0:
                        outputs_hi(n - 2, v)
                    if has(n):
                        exps(n, v)
                    if has(n - 2) and v == 1:
                        outputs_hi(n - 2, v)

            nc.scalar.activation(warm[:, :], eps, ACT.Exp)
            act.wait_ge(vt_ps, l * 2 + 2)
            for n in range(5):
                attention(n)
            with act.Fori(5, N_CHUNK) as n:
                attention(n)
            for n in range(N_CHUNK, CHUNKS + 2):
                attention(n)
            with act.Fori(0, 4) as i:
                for j in range(2):
                    step(W + i * 4, P_OA + 2 * j, 0)
                    gate(A_OA + j, j, col(l, "bg", i * 2 + j), l * ND + i * 2 + (D_OA + j + 1))
                    step(W + i * 4, P_OA + 2 * j + 1, 1)
            act.wait_ge(kv_out, l * 112 + 112)
            with act.Fori(0, 4) as i:
                for j in range(2):
                    step(W + i * 6, P_SC + 3 * j, j)
                    act.wait_ge(d_out, l * ND + i * 4 + (D_SC + 2 * j))
                    nc.scalar.activation(halves(slot(O_CT, TOK, j)), a_tile(A_SC + j), ACT.Copy).then_inc(a_out, 1)
                    step(W + i * 6, P_SC + 3 * j + 1, 1 - j)
                    step(W + i * 6, P_SC + 3 * j + 2, j)
                    act.wait_ge(d_out, l * ND + i * 4 + (D_SC + 2 * j + 1 + 3))
                    nc.scalar.activation(tile(bh, i * 2 + j), slot(O_BT, TOK, j), ACT.Copy).then_inc(sc_hi, 1)

            def mean(m):
                act.wait_ge(sum_ps, l * NS + (S_MEAN + 1))
                nc.scalar.activation(halves(view(O_MU, 622)), a_tile(A_MEAN, 311), ACT.Copy, scale=1.0 / D_MODEL) \
                    .then_inc(a_out, 1)

            def ln_square(m):
                act.wait_ge(ln_sub, l * KT + m + 1)
                square(l, Q_VAR, m, m % 2, acc[:, m, :], CF_OUT)

            def ln_root(m):
                root(l, S_VAR, A_VAR, 311, O_RT)

            def silu(m):
                act.wait_ge(ln_mul, l * KT + m + 1)
                nc.scalar.activation(acc[:, m, :], acc[:, m, :], ACT.Silu, bias=col(l, "lnb", m), scale=col(l, "lng", m)) \
                    .then_inc(ln_silu, 1)

            def branch_hi(m):
                act.wait_ge(ln_silu, l * KT + m + 1)
                nc.scalar.activation(bh[:, m, 0:TP], acc[:, m, 0:TP], ACT.Copy)
                nc.scalar.activation(bh[:, m, TP:TOK], acc[:, m, TP + CF_H:CF_OUT], ACT.Copy).then_inc(cf_hi, 1)

            plan = {2: (mean, (0,)), 4: (ln_square, (0, 1)), 5: (ln_square, (2, 3, 4)), 6: (ln_square, (5, 6, 7)),
                    8: (ln_root, (0,)), 11: (silu, (0, 1)), 12: (silu, (2, 3)), 13: (silu, (4, 5, 6, 7)),
                    15: (branch_hi, (0, 1, 2, 3, 4, 5, 6, 7))}
            for p in range(2 * KT):
                m = p // 2
                if p % 2 == 0:
                    step(W, P_OS + p, 0)
                    gate(a_gate_sc(m), m % 2, col(l, "bg", KT + m), d_free(l, D_OS + m))
                else:
                    step(W, P_OS + p, 1)
                work, tiles = plan.get(p, (None, ()))
                for t in tiles:
                    work(t)
            with act.Fori(0, 4) as i:
                for j in range(2):
                    step(W + i * 4, P_OC + 2 * j, 0)
                    gate(A_OC + j, j, col(l, "bg", i * 2 + (2 * KT + j)), l * ND + i * 2 + (D_OC + j + 1))
                    step(W + i * 4, P_OC + 2 * j + 1, 1)
                    act.wait_ge(mg_done, l * 16 + i * 2 + (8 + j + 1))
                    act.wait_ge(tails_out, l * 32 + 32)
                    nc.scalar.activation(tile(mh, i * 2 + j), tile(X, i * 2 + j), ACT.Copy).then_inc(mg_hi, 1)
            residual(l, P_WO, D_WO, (l, Q_N2), "g2")
            root(l, S_N2, A_N2, HALF, O_RF)
            act.wait_ge(ff_zero, l * 4 + 4)
            for t0, n, p0, a0, d0 in thirds:
                def product_hi(m, j):
                    act.wait_ge(ff_prod, l * FT + m + (t0 + 1))
                    src = slot(O_PB, S_OUT, j)
                    nc.scalar.activation(tile(bh, m, 0, TP), src[:, 0:TP], ACT.Copy)
                    nc.scalar.activation(tile(bh, m, TP, DEC_SEQ), src[:, TP + S_H:S_OUT], ACT.Copy).then_inc(ff_hi, 1)

                def tap_and_tail(m, src, dst):
                    nc.scalar.activation(dst, src[:, 0:S_OUT], ACT.Identity, bias=0.0, scale=col(l, "ffw", m * 3)) \
                        .then_inc(ff_first, 1)
                    nc.scalar.activation(tile(fft, m, 0, S_H), src[:, TP:TP + S_H], ACT.Copy)
                    nc.scalar.activation(tile(fft, m, S_H, S_H), src[:, S_IN - S_H:S_IN], ACT.Copy).then_inc(ff_tail_done, 1)

                def conv_product(i):
                    for j in range(2):
                        m = i * 2 + (t0 + j)
                        hg, hu = slot(O_HG, S_IN, j), slot(O_HU, S_IN, j)
                        gc, uc = slot(O_GC, S_OUT, j), slot(O_UC, S_OUT, j)
                        step(W + i * 4, p0 + 2 * j, 0)
                        if j or not isinstance(i, int):
                            product_hi(i * 2 + (j - 1), 1 - j)
                        act.wait_ge(ff_tap, l * (FT * 4) + i * 8 + (t0 * 4 + 4 * j + 4))
                        nc.scalar.activation(hg[:, TP + S_H:TP + 2 * S_H], col(l, "ffh", m * 2, 2), ACT.Copy).then_inc(ff_hist, 1)
                        nc.scalar.activation(hu[:, TP + S_H:TP + 2 * S_H], col(l, "ffh", m * 2 + 2 * FT, 2), ACT.Copy) \
                            .then_inc(ff_hist, 1)
                        act.wait_ge(ff_hist, l * (2 * FT) + i * 4 + (2 * t0 + 2 * j + 2))
                        act.wait_ge(a_out, l * NA + i * 2 + (a0 + j + 3))
                        tap_and_tail(m, hg, gc)
                        step(W + i * 4, p0 + 2 * j + 1, 1)
                        act.wait_ge(d_out, l * ND + i * 2 + (d0 + j + 3))
                        tap_and_tail(m + FT, hu, uc)
                        act.wait_ge(ff_tap, l * (FT * 4) + i * 8 + (t0 * 4 + 4 * j + 2 + 8))
                        nc.scalar.activation(gc, gc, ACT.Silu).then_inc(ff_silu, 1)
                conv_product(0)
                with act.Fori(1, n // 2) as i:
                    conv_product(i)
                product_hi(n - 1, 1)
                residual(l, p0 + 2 * n, d0 + n, (l + 1, Q_N1) if t0 + n == FT else None, "g1")
        root(DEPTH, S_N1, A_N1, HALF, O_RT)

    @block.vector
    def _(dve):
        V = nc.vector

        def low(s):
            return V.tensor_tensor(wl[:, s, :], raw[:, s, :], f(wh[:, s, :]), ALU.subtract).then_inc(lo_done, 1)

        def step(wbase, off, s):
            dve.wait_ge(panel_done, wbase + (off + 1))
            dve.wait_ge(hi_done, wbase + (off + 3))
            low(s)

        def zero_sum(n):
            V.memset(view(O_SS, n), 0.0).then_inc(sq_sum, 1)

        def add_square(l, q, m, s, n):
            dve.wait_ge(sq_done, l * (NQ * 8) + (q * 8 + 1) + m)
            dve.wait_ge(sq_sum, l * (NQ * 9) + (q * 9 + 2) + m)
            V.tensor_tensor(view(O_SS, n), view(O_SS, n), slot(O_SQ, 622, s)[:, 0:n], ALU.add).then_inc(sq_sum, 1)

        def rsqrt(a_at, n, at, count):
            dve.wait_ge(a_out, a_at)
            V.reciprocal(view(at, 2 * n), view(at, 2 * n)).then_inc(rs_done, 1)
            dve.wait_ge(rs_done, count)

        def scaled_lo(l, g, m, hi_count):
            dve.wait_ge(nx_hi, hi_count)
            V.scalar_tensor_tensor(tile(xl, m), tile(X, m), col(l, g, m), f(tile(xh, m)), ALU.mult, ALU.subtract) \
                .then_inc(nx_lo, 1)

        def first_taps(l, m, k0, k1):
            for k in range(k0, k1):
                src = tile(G, m, k, CF_OUT)
                if k == 0:
                    V.tensor_scalar(tile(acc, m), src, col(l, "cfw", m * CF_K), None, ALU.mult).then_inc(tap_glu, 1)
                else:
                    dve.wait_ge(tap_glu, l * (KT * TAPS_GLU) + m * TAPS_GLU + k)
                    V.scalar_tensor_tensor(tile(acc, m), src, col(l, "cfw", m * CF_K + k), tile(acc, m), ALU.mult,
                                           ALU.add).then_inc(tap_glu, 1)

        def taps(l, k, *groups):
            for g in groups:
                if isinstance(k, int) and k == TAPS_GLU:
                    dve.wait_ge(tap_glu, l * (KT * TAPS_GLU) + KT * TAPS_GLU)
                for t in range(2):
                    if not (isinstance(k, int) and k == TAPS_GLU):
                        dve.wait_ge(tap_rest[g], l * (2 * (CF_K - TAPS_GLU)) + k * 2 + (t - 2 * TAPS_GLU + 1))
                    a = acc[:, 2 * g + t, :]
                    V.scalar_tensor_tensor(a, tile(G, 2 * g + t, k, CF_OUT), col(l, "cfw", k + (2 * g + t) * CF_K), a,
                                           ALU.mult, ALU.add).then_inc(tap_rest[g], 1)

        def conv3(l, src, dst, name, t, sem_, base):
            V.tensor_scalar(dst, src[:, 0:S_OUT], col(l, name, t * 3), None, ALU.mult).then_inc(sem_, 1)
            for k in (1, 2):
                dve.wait_ge(sem_, base + k)
                V.scalar_tensor_tensor(dst, src[:, k:k + S_OUT], col(l, name, t * 3 + k), dst, ALU.mult, ALU.add) \
                    .then_inc(sem_, 1)

        def keep_tail(t, m, src, sem_):
            V.tensor_copy(tile(t, m, 0, S_H), src[:, TP:TP + S_H])
            V.tensor_copy(tile(t, m, S_H, S_H), src[:, S_IN - S_H:S_IN]).then_inc(sem_, 1)

        V.sem_inc(d_out, 2)
        V.sem_inc(pt2_done, 1)
        V.sem_inc(on_done, 1)
        V.sem_inc(ol_done, 1)
        V.sem_inc(rinv_done, 2)
        V.sem_inc(ff_tap, 8)
        V.sem_inc(ff_tail_done, 2)
        V.sem_inc(sq_sum, 1)
        for g in range(4):
            V.sem_inc(tap_rest[g], 2)
        zero_sum(TOK)
        for m in range(KT):
            add_square(0, Q_N1, m, m % 2, TOK)
            scaled_lo(0, "g1", m, m + 1)
            if m in (1, 3):
                dve.wait_ge(hi_done, m // 2 + 1)
                low(m // 2)
        for l_ in range(DEPTH):
            V.tensor_scalar(nsink[:, 8 * l_:8 * l_ + 8], col(l_, "sink", 0, 8), -1.0, None, ALU.mult).then_inc(nsink_done, 1)
        dve.wait_ge(nsink_done, DEPTH)
        with dve.Fori(0, DEPTH) as l:
            W = l * PANELS
            V.memset(G[:, :, 0:CF_H], 0.0).then_inc(g_zero, 1)

            def normed(m):
                if m >= 3:
                    dve.wait_ge(nx_lo, l * 24 + (8 + m - 2))
                V.tensor_tensor(slot(O_NT, TOK, m % 3), X[:, m, :], view(O_RT, TOK), ALU.mult).then_inc(nx_mul, 1)

            def normed_lo(m):
                dve.wait_ge(nx_hi, l * 24 + (8 + m + 1))
                V.scalar_tensor_tensor(xl[:, m, :], slot(O_NT, TOK, m % 3), col(l, "g1", m), f(xh[:, m, :]), ALU.mult,
                                       ALU.subtract).then_inc(nx_lo, 1)
            rsqrt(a_ready(l, A_N1), HALF, O_RT, l * 3 + 1)
            for m in range(3):
                normed(m)
            step(W, P_CF, 0)
            V.tensor_tensor(halves(slot(O_QR, TOK, 0)), halves(view(O_RT, TOK)), a_tile(A_CF), ALU.mult).then_inc(a_out, 1)
            normed_lo(0)
            normed_lo(1)
            for m in range(3, KT):
                normed(m)
                if m == 3:
                    step(W, P_CF + 1, 1)
                normed_lo(m - 1)
            normed_lo(KT - 1)
            V.tensor_tensor(halves(slot(O_TQ, TOK, 0)), halves(view(O_RT, TOK)), d_tile(D_CF), ALU.mult).then_inc(d_out, 1)
            dve.wait_ge(glu_gate, l + 1)
            dve.wait_ge(d_out, d_ready(l, D_CF))
            for piece in PIECES:
                last = V.tensor_tensor(tile(G, 0, after(piece[3], CF_H), piece[2]),
                                       slot(O_SG, TOK, 0)[:, piece[3]:piece[3] + piece[2]],
                                       slot(O_TQ, TOK, 0)[:, piece[3]:piece[3] + piece[2]], ALU.mult)
            last.then_inc(glu_first, 1)
            dve.wait_ge(g_zero, l + 1)
            dve.wait_ge(hist_in, l * 16 + 16)
            dve.wait_ge(glu_first, l + 1)
            first_taps(l, 0, 0, TAPS_GLU // 2)

            def glu(i, j):
                m = i * 2 + j
                step(W + i * 4, P_CF + 2 * j, 0)
                first_taps(l, i * 2 + (j - 1), TAPS_GLU // 2, TAPS_GLU)
                step(W + i * 4, P_CF + 2 * j + 1, 1)
                dve.wait_ge(a_out, l * NA + i * 2 + (A_CF + j + 3))
                for piece in PIECES:
                    last = V.tensor_tensor(tile(G, m, after(piece[3], CF_H), piece[2]),
                                           slot(O_SG, TOK, j)[:, piece[3]:piece[3] + piece[2]],
                                           d_piece(D_CF + j, piece), ALU.mult)
                last.then_inc(d_out, 1)
                dve.wait_ge(d_out, l * ND + i * 2 + (D_CF + j + 3))
                first_taps(l, m, 0, TAPS_GLU // 2)
            glu(0, 1)
            with dve.Fori(1, 4) as i:
                glu(i, 0)
                glu(i, 1)
            dve.wait_ge(x_spilled, l * 16 + 16)
            dve.wait_ge(late_in, 16)

            def keys():
                for v in range(N_KV):
                    for j in range(2):
                        dve.wait_ge(krot_ps, l * 4 + 2 * v + j + 1)
                        V.tensor_tensor(halves(slot(O_TQ, TOK, j)), halves((cos, sin)[j]), d_tile(D_K + 2 * v + j), ALU.mult) \
                            .then_inc(d_out, 1)
                    dve.wait_ge(d_out, d_ready(l, D_K + 2 * v + 1))
                    V.tensor_tensor(KD[:, v, 0:TP], slot(O_TQ, TOK, 0)[:, 0:TP], slot(O_TQ, TOK, 1)[:, 0:TP], ALU.add)
                    V.tensor_tensor(KD[:, v, TP + WINDOW:720], slot(O_TQ, TOK, 0)[:, TP:TOK],
                                    slot(O_TQ, TOK, 1)[:, TP:TOK], ALU.add).then_inc(krot, 1)
                    dve.wait_ge(krot, l * 2 + v + 1)

            def rotation(i, j):
                dve.wait_ge(a_out, l * NA + i * 2 + (A_Q + j + 3))
                V.tensor_tensor(tile(X, i * 2 + j), slot(O_QR, TOK, j), cos, ALU.mult).then_inc(qtmp, 1)
                dve.wait_ge(qrot_ps, l * KT + i * 2 + (j + 1))
                V.tensor_tensor(halves(slot(O_TQ, TOK, j)), halves(sin), d_tile(D_Q + j), ALU.mult).then_inc(d_out, 1)
                dve.wait_ge(d_out, l * ND + i * 2 + (D_Q + j + 3))
                V.tensor_tensor(tile(X, i * 2 + j), tile(X, i * 2 + j), slot(O_TQ, TOK, j), ALU.add).then_inc(qrot, 1)

            def queries(i):
                step(W + i * 2, P_Q, 1)
                if isinstance(i, int):
                    keys()
                else:
                    rotation(i - 1, 1)
                    taps(l, i + (TAPS_GLU - 1), 0, 1, 2)
                step(W + i * 2, P_Q + 1, 0)
                rotation(i, 0)
            step(W, P_K, 0)
            first_taps(l, KT - 1, TAPS_GLU // 2, TAPS_GLU)
            queries(0)
            dve.wait_ge(tap_glu, (l + 1) * (KT * TAPS_GLU))
            V.sem_inc(carrier, 1)
            with dve.Fori(1, 4) as i:
                queries(i)
            rotation(3, 1)
            taps(l, TAPS_GLU + 3, 0, 1, 2)
            step(W, P_V, 1)

            def value_tiles():
                for j in range(2):
                    dve.wait_ge(vt_ps, l * 2 + j + 1)
                    b0 = 4 + 2 * ((D_V + j) % 2)
                    groups = (((0, 0, 4, 128, 0), (1, 0, 3, 128, 4)), ((0, 0, 4, 64, 1), (1, 0, 3, 64, 5), (1, 3, 1, 16, 0)))[j]
                    for b, c0, n, rows, v0 in groups:
                        last = V.tensor_copy(VV[0:rows, v0:v0 + n, j, :],
                                             PS[0:rows, b0 + b, 128 * c0:128 * (c0 + n)].rearrange("p (t n) -> p t n", n=128))
                    last.then_inc(d_out, 1)

            def maxima(n, v):
                nk = chunk_span(n)[2]
                it = l * 20 + n * 2 + v
                dve.wait_ge(s_done, it + 3)
                sc = PS[:, 2 * v:2 * v + 2, :].rearrange("p b (i n) -> p (b i) n", i=2)[:, :, 0:nk]
                V.tensor_reduce(mx[:, v, :], sc, AX.X, ALU.max).then_inc(mx_done, 1)
                dve.wait_ge(mx_done, it + 1)
                dve.wait_ge(p_done, it + 1)
                ns = nsink[:, bass.ds(l * 8 + 4 * v, 4)]
                V.scalar_tensor_tensor(nm[:, v, :], mx[:, v, :], -SCALE, ns, ALU.mult, ALU.min).then_inc(nm_done, 1)
                dve.wait_ge(nm_done, 2 * it + 1)
                V.tensor_tensor(ds_[:, v, :], nm[:, v, :], ns, ALU.subtract).then_inc(nm_done, 1)

            def copy_rest(n, v):
                n2 = max(chunk_span(n)[2] - 128, 0)
                it = l * 20 + n * 2 + v
                if n2:
                    dve.wait_ge(t_done, it + 3)
                    dve.wait_ge(o_done, it + 1)
                    V.tensor_copy(scr[0:n2, O_PT2 + 512 * v:O_PT2 + 512 * v + 512], PS[0:n2, 5, :]).then_inc(pt2_done, 1)

            def denominators(n, v):
                it = l * 20 + n * 2 + v
                dve.wait_ge(p_done, it + 3)
                V.tensor_tensor(sums[:, v, :], sums[:, v, :], es[:, v, :], ALU.add).then_inc(den_done, 1)
                dve.wait_ge(den_done, it + 1)
                V.reciprocal(rinv[:, v, :], sums[:, v, :]).then_inc(rinv_done, 1)

            def norm_outputs(n, v):
                it = l * 20 + n * 2 + v
                dve.wait_ge(rinv_done, it + 3)
                dve.wait_ge(o_done, it + 3)
                V.tensor_tensor(view(O_ON + 256 * v, 256).rearrange("p (i n) -> p i n", i=4),
                                PS[:, 6, 0:256].rearrange("p (i n) -> p i n", i=4),
                                rinv[:, v, :].rearrange("p (i o) -> p i o", o=1).to_broadcast([128, 4, 64]),
                                ALU.mult).then_inc(on_done, 1)

            def outputs_lo(n, v):
                q0 = chunk_span(n)[0]
                dve.wait_ge(oh_done, l * 20 + n * 2 + v + 1)
                src = PS[:, 7, 0:256].rearrange("p (t n) -> p t n", n=64)
                at = slice(q0, q0 + 64) if isinstance(q0, int) else bass.ds(q0, 64)
                V.tensor_tensor(bl[:, 4 * v:4 * v + 4, at], src, f(bh[:, 4 * v:4 * v + 4, at]), ALU.subtract) \
                    .then_inc(ol_done, 1)

            def attention_taps(n, late):
                k = TAPS_GLU + 4
                static = {1: ((k, 0), (k, 1)), 2: ((k + 1, 0), (k + 1, 1)), 3: ((k + 2, 0), (k + 2, 1)),
                          4: ((k, 2), (k - 4, 3)), 9: ((k + 1, 2), (k + 1, 3)), 10: ((k + 2, 2), (k + 2, 3))}
                if not isinstance(n, int) or 5 <= n < 9:
                    if not late:
                        taps(l, n + (k - 8), 3)
                elif n in static:
                    taps(l, *static[n][late])

            def attention(n):
                if has(n - 1):
                    denominators(n - 1, 0)
                if has(n):
                    maxima(n, 0)
                if has(n - 2):
                    norm_outputs(n - 2, 1)
                if has(n - 1):
                    copy_rest(n - 1, 0)
                attention_taps(n, False)
                if has(n - 2):
                    outputs_lo(n - 2, 0)
                if has(n - 1):
                    denominators(n - 1, 1)
                if has(n):
                    maxima(n, 1)
                if has(n - 1):
                    norm_outputs(n - 1, 0)
                    copy_rest(n - 1, 1)
                attention_taps(n, True)
                if has(n - 2):
                    outputs_lo(n - 2, 1)

            attention(0)
            value_tiles()
            for n in range(1, 5):
                attention(n)
            with dve.Fori(5, N_CHUNK) as n:
                attention(n)
            for n in range(N_CHUNK, CHUNKS + 2):
                attention(n)
            with dve.Fori(0, 4) as i:
                for j in range(2):
                    step(W + i * 4, P_OA + 2 * j, 0)
                    taps(l, i * 2 + (15 + j), 0, 1)
                    step(W + i * 4, P_OA + 2 * j + 1, 1)
                    dve.wait_ge(a_out, l * NA + i * 2 + (A_OA + j + 3))
                    V.tensor_tensor(halves(tile(X, i * 2 + j)), halves(slot(O_SG, TOK, j)), d_tile(D_OA + j),
                                    ALU.mult).then_inc(d_out, 1)
                    taps(l, i * 2 + (15 + j), 2, 3)
            dve.wait_ge(kv_out, l * 112 + 112)
            for j in range(2):
                V.memset(slot(O_CH, S_IN, j)[:, 0:S_H], 0.0).then_inc(sc_hist, 1)
            with dve.Fori(0, 4) as i:
                for j in range(2):
                    m = i * 2 + j
                    step(W + i * 6, P_SC + 3 * j, j)
                    ch, cv = slot(O_CH, S_IN, j), slot(O_CV, S_OUT, j)
                    V.tensor_copy(ch[:, TP + S_H:TP + 2 * S_H], col(l, "sch", m * 2, 2)).then_inc(sc_hist, 1)
                    taps(l, i * 2 + (23 + j), 0, 1)
                    step(W + i * 6, P_SC + 3 * j + 1, 1 - j)
                    dve.wait_ge(a_out, l * NA + i * 2 + (A_SC + j + 3))
                    for piece in PIECES:
                        o = after(piece[3], S_H)
                        last = V.tensor_tensor(ch[:, o:o + piece[2]], slot(O_CT, TOK, j)[:, piece[3]:piece[3] + piece[2]],
                                               d_piece(D_SC + 2 * j, piece), ALU.mult)
                    last.then_inc(d_out, 1)
                    dve.wait_ge(d_out, l * ND + i * 4 + (D_SC + 2 * j + 3))
                    keep_tail(sct, m, ch, sc_tail_done)
                    conv3(l, ch, cv, "scw", m, sc_tap, l * 24 + i * 6 + 3 * j)
                    step(W + i * 6, P_SC + 3 * j + 2, j)
                    dve.wait_ge(sc_tap, l * 24 + i * 6 + (3 * j + 3))
                    bt = slot(O_BT, TOK, j)
                    for piece in PIECES:
                        o = piece[3] + (S_H if piece[3] >= TP else 0)
                        last = V.tensor_tensor(bt[:, piece[3]:piece[3] + piece[2]], cv[:, o:o + piece[2]],
                                               d_piece(D_SC + 2 * j + 1, piece), ALU.mult)
                    last.then_inc(d_out, 1)
                    taps(l, i * 2 + (23 + j), 2, 3)
                    dve.wait_ge(sc_hi, l * KT + i * 2 + (j + 1))
                    V.tensor_tensor(tile(bl, m), bt, f(tile(bh, m)), ALU.subtract).then_inc(sc_lo, 1)

            def merge(m, j, d, ready):
                V.tensor_tensor(halves(slot(O_TQ, TOK, j)), halves(slot(O_SG, TOK, j)), d_tile(d), ALU.mult) \
                    .then_inc(d_out, 1)
                dve.wait_ge(d_out, ready)
                V.tensor_tensor(tile(X, m), tile(X, m), slot(O_TQ, TOK, j), ALU.add).then_inc(mg_done, 1)

            def tile_sum(m):
                ss = view(O_SS, CF_OUT)
                if m == 1:
                    for g in range(4):
                        dve.wait_ge(tap_rest[g], (l + 1) * (2 * (CF_K - TAPS_GLU)) + 2)
                    V.tensor_tensor(ss, acc[:, 0, :], acc[:, 1, :], ALU.add).then_inc(mean_sum, 1)
                else:
                    dve.wait_ge(mean_sum, l * 7 + (m - 1))
                    V.tensor_tensor(ss, ss, acc[:, m, :], ALU.add).then_inc(mean_sum, 1)

            def ln_center(m):
                if m == 0:
                    dve.wait_ge(a_out, a_ready(l, A_MEAN))
                    zero_sum(622)
                V.tensor_tensor(acc[:, m, :], acc[:, m, :], view(O_MU, 622), ALU.subtract).then_inc(ln_sub, 1)

            def ln_add(m):
                add_square(l, Q_VAR, m, m % 2, 622)

            def ln_rsqrt(m):
                rsqrt(a_ready(l, A_VAR), 311, O_RT, l * 3 + 2)

            def ln_scale(m):
                V.tensor_tensor(acc[:, m, :], acc[:, m, :], view(O_RT, 622), ALU.mult).then_inc(ln_mul, 1)

            plan = {0: (tile_sum, (1, 2, 3, 4)), 1: (tile_sum, (5, 6, 7)), 3: (ln_center, (0, 1, 2, 3)),
                    4: (ln_center, (4, 5, 6, 7)), 5: (ln_add, (0, 1, 2)), 6: (ln_add, (3, 4, 5)), 7: (ln_add, (6, 7)),
                    9: (ln_rsqrt, (0,)), 10: (ln_scale, (0, 1, 2, 3)), 11: (ln_scale, (4, 5, 6, 7))}
            for p in range(2 * KT):
                m = p // 2
                step(W, P_OS + p, p % 2)
                if p % 2:
                    dve.wait_ge(a_out, a_ready(l, a_gate_sc(m)))
                    merge(m, m % 2, D_OS + m, d_ready(l, D_OS + m))
                work, tiles = plan.get(p, (None, ()))
                for t in tiles:
                    work(t)

            def branch_lo(m):
                dve.wait_ge(cf_hi, l * KT + m + 1)
                V.tensor_tensor(bl[:, m, 0:TP], acc[:, m, 0:TP], f(bh[:, m, 0:TP]), ALU.subtract)
                V.tensor_tensor(bl[:, m, TP:TOK], acc[:, m, TP + CF_H:CF_OUT], f(bh[:, m, TP:TOK]), ALU.subtract) \
                    .then_inc(cf_lo, 1)
            for m in range(KT):
                branch_lo(m)
            with dve.Fori(0, 4) as i:
                for j in range(2):
                    m = i * 2 + j
                    step(W + i * 4, P_OC + 2 * j, 0)
                    step(W + i * 4, P_OC + 2 * j + 1, 1)
                    dve.wait_ge(a_out, l * NA + i * 2 + (A_OC + j + 3))
                    merge(m, j, D_OC + j, l * ND + i * 2 + (D_OC + j + 3))
                    dve.wait_ge(mg_hi, l * KT + i * 2 + (j + 1))
                    V.tensor_tensor(tile(ml, m), tile(X, m), f(tile(mh, m)), ALU.subtract).then_inc(mg_lo, 1)
            zero_sum(TOK)
            with dve.Fori(0, 4) as i:
                for j in range(2):
                    m = i * 2 + j
                    dve.wait_ge(panel_done, W + i * 2 + (P_WO + j + 1))
                    dve.wait_ge(x_back, l * (KT * 16) + i * 32 + (16 * j + 16))
                    V.tensor_tensor(halves(tile(X, m)), halves(tile(X, m)), d_tile(D_WO + j), ALU.add).then_inc(d_out, 1)
                    step(W + i * 2, P_WO + j, j)
                    add_square(l, Q_N2, m, j, TOK)
                    scaled_lo(l, "g2", m, l * 24 + i * 2 + (16 + j + 1))
            rsqrt(a_ready(l, A_N2), HALF, O_RF, l * 3 + 3)
            for j in range(2):
                V.memset(slot(O_HG, S_IN, j)[:, 0:S_H], 0.0).then_inc(ff_zero, 1)
                V.memset(slot(O_HU, S_IN, j)[:, 0:S_H], 0.0).then_inc(ff_zero, 1)
            for t0, n, p0, a0, d0 in thirds:
                def product_lo(m, j):
                    dve.wait_ge(ff_hi, l * FT + m + (t0 + 1))
                    pb_ = slot(O_PB, S_OUT, j)
                    V.tensor_tensor(tile(bl, m, 0, TP), pb_[:, 0:TP], f(tile(bh, m, 0, TP)), ALU.subtract)
                    V.tensor_tensor(tile(bl, m, TP, DEC_SEQ), pb_[:, TP + S_H:S_OUT],
                                    f(tile(bh, m, TP, DEC_SEQ)), ALU.subtract).then_inc(ff_lo, 1)

                def tap(l, k, src, dst, m):
                    V.scalar_tensor_tensor(dst, src[:, k:k + S_OUT], col(l, "ffw", m * 3 + k), dst, ALU.mult, ALU.add) \
                        .then_inc(ff_tap, 1)

                def conv_product(i):
                    for j in range(2):
                        m = i * 2 + (t0 + j)
                        hg, hu = slot(O_HG, S_IN, j), slot(O_HU, S_IN, j)
                        gc, uc = slot(O_GC, S_OUT, j), slot(O_UC, S_OUT, j)
                        first = l * (2 * FT) + i * 4 + (2 * t0 + 2 * j)
                        taps_ = l * (FT * 4) + i * 8 + (t0 * 4 + 4 * j + 8)
                        step(W + i * 4, p0 + 2 * j, 0)
                        for piece in PIECES:
                            o = after(piece[3], S_H)
                            last = V.tensor_tensor(hg[:, o:o + piece[2]], view(O_RF + piece[3], piece[2]),
                                                   a_piece(a0 + j, piece), ALU.mult)
                        last.then_inc(a_out, 1)
                        if j or not isinstance(i, int):
                            product_lo(i * 2 + (j - 1), 1 - j)
                        dve.wait_ge(ff_first, first + 1)
                        tap(l, 1, hg, gc, m)
                        step(W + i * 4, p0 + 2 * j + 1, 1)
                        for piece in PIECES:
                            o = after(piece[3], S_H)
                            last = V.tensor_tensor(hu[:, o:o + piece[2]], view(O_RF + piece[3], piece[2]),
                                                   d_piece(d0 + j, piece), ALU.mult)
                        last.then_inc(d_out, 1)
                        dve.wait_ge(ff_tap, taps_ + 1)
                        tap(l, 2, hg, gc, m)
                        dve.wait_ge(ff_first, first + 2)
                        tap(l, 1, hu, uc, m + FT)
                        dve.wait_ge(ff_tap, taps_ + 3)
                        tap(l, 2, hu, uc, m + FT)
                        dve.wait_ge(ff_silu, l * FT + i * 2 + (t0 + j + 1))
                        dve.wait_ge(ff_tap, taps_ + 4)
                        V.tensor_tensor(slot(O_PB, S_OUT, j), gc, uc, ALU.mult).then_inc(ff_prod, 1)
                conv_product(0)
                with dve.Fori(1, n // 2) as i:
                    conv_product(i)
                product_lo(n - 1, 1)
                final = t0 + n == FT
                if final:
                    zero_sum(TOK)
                with dve.Fori(0, 4) as i:
                    for j in range(2):
                        m = i * 2 + j
                        dve.wait_ge(panel_done, W + i * 2 + (p0 + 2 * n + j + 1))
                        V.tensor_tensor(halves(tile(X, m)), halves(tile(X, m)), d_tile(d0 + n + j), ALU.add) \
                            .then_inc(d_out, 1)
                        step(W + i * 2, p0 + 2 * n + j, j)
                        if final:
                            add_square(l + 1, Q_N1, m, j, TOK)
                            scaled_lo(l + 1, "g1", m, (l + 1) * 24 + i * 2 + (j + 1))
        rsqrt(a_ready(DEPTH, A_N1), HALF, O_RT, DEPTH * 3 + 1)
        for m in range(KT):
            V.scalar_tensor_tensor(X[:, m, :], X[:, m, :], col(DEPTH, "g1", m), view(O_RT, TOK), ALU.mult, ALU.mult) \
                .then_inc(yn_done, 1)


def weight_panels(w_in, w_attn_out, w_sc_out, w_cf_out, w_o, w_up, w_down):
    q, kv = N_HEADS * HEAD_DIM, N_KV * HEAD_DIM
    at = np.cumsum([0, q, kv, kv] + [D_MODEL] * 8)
    panels = []
    wa = w_attn_out.reshape(DEPTH, N_KV, 2, 2, 2, HEAD_DIM, D_MODEL).transpose(0, 1, 2, 4, 3, 5, 6)
    wa = wa.reshape(DEPTH, q, D_MODEL)

    def cols(w, l, c, rows=slice(None)):
        p = w[l, rows, c * 128:(c + 1) * 128]
        p = p.reshape(-1, 128, 128).transpose(1, 0, 2)
        if p.shape[1] < KT:
            p = np.concatenate([p, np.zeros((128, KT - p.shape[1], 128), p.dtype)], axis=1)
        return p.reshape(128, KT * 128)

    for l in range(DEPTH):
        part = [w_in[:, :, at[i]:at[i + 1]] for i in range(10)] + [w_in[:, :, at[10]:]]
        wq, wk, wv, sb_, sc_, sh_, ca, cg, ga, gs, gc = part
        for m in range(KT):
            panels += [cols(cg, l, m), cols(ca, l, m)]
        panels += [cols(wk, l, 0)] + [cols(wq, l, m) for m in range(KT)] + [cols(wv, l, 0)]
        for m in range(KT):
            panels += [cols(ga, l, m), cols(wa, l, m)]
        for m in range(KT):
            panels += [cols(sc_, l, m), cols(sh_, l, m), cols(sb_, l, m)]
        for m in range(KT):
            panels += [cols(gs, l, m), cols(w_sc_out, l, m)]
        for m in range(KT):
            panels += [cols(gc, l, m), cols(w_cf_out, l, m)]
        panels += [cols(w_o, l, m) for m in range(KT)]
        t0 = 0
        for n in THIRDS:
            for m in range(t0, t0 + n):
                panels += [cols(w_up, l, m), cols(w_up, l, m + FT)]
            panels += [cols(w_down, l, m, slice(t0 * 128, (t0 + n) * 128)) for m in range(KT)]
            t0 += n
    return np.ascontiguousarray(np.stack(panels + panels[:2]))


def channel_major(a):
    lead = a.shape[:-1]
    a = a.reshape(*lead, a.shape[-1] // 128, 128)
    n = a.ndim
    return a.transpose(n - 1, n - 2, *range(n - 2))


def constants():
    half = ROT // 2
    pos = np.concatenate([np.arange(TP), PAST + np.arange(DEC_SEQ)]).astype(np.float32)
    inv = np.power(np.float32(THETA), -np.arange(0, ROT, 2, dtype=np.float32) / np.float32(ROT)).astype(np.float32)
    ang = inv[:, None] * pos[None, :]
    c = np.ones((HEAD_DIM, TOK), np.float32)
    s = np.zeros((HEAD_DIM, TOK), np.float32)
    for d in range(ROT):
        c[d], s[d] = np.cos(ang[d % half]), np.sin(ang[d % half])
    rot = np.zeros((128, 128), np.float32)
    for h in (0, HEAD_DIM):
        for d in range(half):
            rot[h + d + half, h + d] = -1.0
            rot[h + d, h + d + half] = 1.0
    eye = np.eye(128, dtype=np.float32)
    dup = [np.concatenate([m[:, v:v + 64]] * 2, axis=1) for v in (0, 64) for m in (eye, rot)]
    parts = [eye, np.ones((128, 128), np.float32), rot, dup[0], dup[1], dup[2], dup[3],
             np.full((128, 1), EPS, np.float32), np.concatenate([c, c]), np.concatenate([s, s])]
    return np.ascontiguousarray(np.concatenate(parts, axis=1))


def kernel(x_prompt, x_sample, cache_k, cache_v, state_sc, state_cf, state_ffn, meta_tokens, norm1_g, w_in,
           b_gate, attn_sinks, w_attn_out, sc_conv_w, w_sc_out, cf_conv_w, cf_ln_g, cf_ln_b, w_cf_out, w_o,
           norm2_g, w_up, ffn_conv_w, w_down, final_g):
    import concourse.bacc as bacc
    from concourse.bass_utils import run_bass_kernel_spmd

    (x_prompt, x_sample, cache_k, cache_v, state_sc, state_cf, state_ffn, meta_tokens, norm1_g, w_in, b_gate, attn_sinks,
     w_attn_out, sc_conv_w, w_sc_out, cf_conv_w, cf_ln_g, cf_ln_b, w_cf_out, w_o, norm2_g, w_up, ffn_conv_w, w_down,
     final_g) = (np.asarray(a) for a in (
         x_prompt, x_sample, cache_k, cache_v, state_sc, state_cf, state_ffn, meta_tokens, norm1_g, w_in, b_gate,
         attn_sinks, w_attn_out, sc_conv_w, w_sc_out, cf_conv_w, cf_ln_g, cf_ln_b, w_cf_out, w_o, norm2_g, w_up,
         ffn_conv_w, w_down, final_g))
    vecs = []
    for l in range(DEPTH):
        sinks = np.repeat(attn_sinks[l].reshape(8, 2).transpose(1, 0), 64, axis=0)
        vecs += [channel_major(norm1_g[l]), channel_major(norm2_g[l]), channel_major(b_gate[l]), channel_major(cf_ln_g[l]),
                 channel_major(cf_ln_b[l]), channel_major(sc_conv_w[l]), channel_major(cf_conv_w[l]),
                 channel_major(ffn_conv_w[l]), channel_major(state_sc[l, 0]), channel_major(state_ffn[l, 0]), sinks]
    kc = cache_k[:, 0].transpose(0, 3, 2, 1)
    arrays = {
        "weights": weight_panels(w_in, w_attn_out, w_sc_out, w_cf_out, w_o, w_up, w_down),
        "xt": channel_major(np.concatenate([meta_tokens, x_prompt[0], x_sample[0]])),
        "vecs": np.concatenate([v.reshape(128, -1) for v in vecs + [channel_major(final_g)]], axis=1),
        "consts": constants(),
        "kcache": np.concatenate([kc, kc], axis=1),
        "vcache": cache_v.reshape(DEPTH, WINDOW, N_KV * HEAD_DIM),
        "cfhist": np.stack([channel_major(state_cf[l, 0]) for l in range(DEPTH)]),
    }
    arrays = {k: np.ascontiguousarray(v) for k, v in arrays.items()}
    outs = {
        "y": (128, KT, TOK), "kp": (DEPTH, 128, WINDOW), "vp": (DEPTH, WINDOW, 128), "scp": (DEPTH, 128, KT * 2 * S_H),
        "cfp": (DEPTH, 128, KT, 2, CF_H), "ffp": (DEPTH, 128, 2 * FT * 2 * S_H), "ks": (DEPTH, 128, WINDOW),
        "vs": (DEPTH, WINDOW, 128),
    }
    nc = bacc.Bacc("TRN2", target_bir_lowering=False, num_devices=1)
    aps = {k: nc.dram_tensor(f"in_{k}", v.shape, F32, kind="ExternalInput").ap() for k, v in arrays.items()}
    aps["spill"] = nc.dram_tensor("spill", (128, KT, TOK), F32, kind="Internal").ap()
    for k, shape in outs.items():
        aps[k] = nc.dram_tensor(f"out_{k}", shape, F32, kind="ExternalOutput").ap()
    encoder(nc, **aps)
    r = run_bass_kernel_spmd(nc, [{f"in_{k}": v for k, v in arrays.items()}], core_ids=[0]).results[0]
    got = {k: np.asarray(r[f"out_{k}"]) for k in outs}

    def rows(a):
        return np.ascontiguousarray(a.transpose(2, 1, 0).reshape(a.shape[2], -1))

    y = rows(got["y"])

    def heads(a, frames_last):
        a = a.transpose(0, 2, 1) if frames_last else a
        return np.ascontiguousarray(a).reshape(DEPTH, 1, WINDOW, N_KV, HEAD_DIM)

    def tails(a, tiles, n, g):
        a = a.reshape(DEPTH, 128, tiles, 2, n)[:, :, :, g]
        return np.ascontiguousarray(np.stack([rows(a[l]) for l in range(DEPTH)])[:, None])

    return (y[N_META:TP][None], y[TP:][None],
            heads(got["kp"], True), heads(got["vp"], False), tails(got["scp"], KT, S_H, 0), tails(got["cfp"], KT, CF_H, 0),
            tails(got["ffp"], 2 * FT, S_H, 0),
            heads(got["ks"], True), heads(got["vs"], False), tails(got["scp"], KT, S_H, 1), tails(got["cfp"], KT, CF_H, 1),
            tails(got["ffp"], 2 * FT, S_H, 1))
```
